# Optimizing a Trainium2 kernel written in Bass

```python
import jax, jax.numpy as jnp
from jax import lax
import numpy as np

D_MODEL = 1024
BATCH = 1
SEQ = 256
DEPTH = 2
DEC_BATCH = 8
DEC_SEQ = 4
PAST_LEN = 2048
PAGE_SIZE = 128

D_A = 3 * D_MODEL // 8
A_HEADS = 4
A_HEAD_DIM = D_A // A_HEADS
CHUNK = 128
D_B = 3 * D_MODEL // 8
POOL_WINDOWS = (2, 4, 8, 16)
N_POOL_GROUPS = len(POOL_WINDOWS)
POOL_GD = D_B // N_POOL_GROUPS
MAX_WINDOW = max(POOL_WINDOWS)
POOL_BUF = MAX_WINDOW - 1
D_X = D_MODEL - D_A - D_B
X_HEADS = 4
X_HEAD_DIM = D_X // X_HEADS
N_MEM = 256
D_IN = 2 * D_A + D_B + D_X
D_FF = ((8 * D_MODEL // 3) + 255) // 256 * 256
N_EXPERTS = 8
TOP_K = 2
D_FF_E = 7 * D_MODEL // 2
N_DENSE = (DEPTH + 1) // 2
N_MOE = DEPTH // 2
EPS = 1e-6

kernel_name = "hybrid_gmlp_pool_memxattn_decode_step"

def rmsnorm(x, g):
    xf = x.astype(jnp.float32)
    y = xf * lax.rsqrt(jnp.mean(xf * xf, axis=-1, keepdims=True) + EPS)
    return (y * g.astype(jnp.float32)).astype(x.dtype)

def mixer_a(u, v, g_v, w_s, b_s, chunk_len):
    u = jax.nn.gelu(u)
    v = rmsnorm(jax.nn.gelu(v), g_v)
    bsz, t, _ = u.shape
    n_chunks = t // chunk_len
    causal = jnp.tril(jnp.ones((chunk_len, chunk_len), dtype=bool))
    w = jnp.where(causal[None], w_s[:, :chunk_len, :chunk_len], 0)
    vh = v.reshape(bsz, n_chunks, chunk_len, A_HEADS, A_HEAD_DIM)
    mixed = jnp.einsum('hts,bcshd->bcthd', w, vh) + b_s[:, :chunk_len].T[:, :, None]
    out = u * mixed.reshape(bsz, t, D_A)
    return out, v

def mixer_b(ext, n_prefix, pos0, w_pool, s_pool):
    bsz, length, _ = ext.shape
    t = length - n_prefix
    xf = ext.astype(jnp.float32)
    cs = jnp.concatenate([jnp.zeros((bsz, MAX_WINDOW + 1, D_B), jnp.float32),
                          jnp.cumsum(xf, axis=1)], axis=1)
    top = MAX_WINDOW + 1 + n_prefix
    upper = cs[:, top:top + t]
    pos = pos0 + jnp.arange(t, dtype=jnp.int32)
    parts = []
    for g, w in enumerate(POOL_WINDOWS):
        sl = slice(g * POOL_GD, (g + 1) * POOL_GD)
        lower = cs[:, top - w:top - w + t, sl]
        count = jnp.minimum(pos + 1, w).astype(jnp.float32)[None, :, None]
        parts.append((upper[..., sl] - lower) / count)
    mean = jnp.concatenate(parts, axis=-1)
    d = (mean - xf[:, n_prefix:]).reshape(bsz, t, N_POOL_GROUPS, POOL_GD)
    y = jnp.einsum('btgc,gcd->btgd', d, w_pool.astype(jnp.float32)).reshape(bsz, t, D_B)
    return (y * s_pool.astype(jnp.float32)).astype(ext.dtype)

def mem_kv(mem, g_mem, w_mem_kv):
    m = rmsnorm(mem, g_mem)
    kv = m @ w_mem_kv
    bsz = mem.shape[0]
    k = kv[..., :D_X].reshape(bsz, N_MEM, X_HEADS, X_HEAD_DIM)
    v = kv[..., D_X:].reshape(bsz, N_MEM, X_HEADS, X_HEAD_DIM)
    return k, v

def mixer_x(q, k, v):
    bsz, t, _ = q.shape
    qh = q.reshape(bsz, t, X_HEADS, X_HEAD_DIM).astype(jnp.float32)
    s = jnp.einsum('bthd,bmhd->bhtm', qh, k.astype(jnp.float32)) * (X_HEAD_DIM ** -0.5)
    p = jax.nn.softmax(s, axis=-1)
    o = jnp.einsum('bhtm,bmhd->bthd', p, v.astype(jnp.float32))
    return o.reshape(bsz, t, D_X).astype(q.dtype)

def mixing_sublayer(x, pool_prefix, pos0, chunk_len, mk, mv, g_norm, w_in, g_v, w_s, b_s,
                    w_pool, s_pool, g_group, w_out):
    h = rmsnorm(x, g_norm)
    p = h @ w_in
    u = p[..., :D_A]
    v = p[..., D_A:2 * D_A]
    xb = p[..., 2 * D_A:2 * D_A + D_B]
    q = p[..., 2 * D_A + D_B:]
    a_out, v_rows = mixer_a(u, v, g_v, w_s, b_s, chunk_len)
    if pool_prefix is None:
        ext, n_prefix = xb, 0
    else:
        ext, n_prefix = jnp.concatenate([pool_prefix.astype(xb.dtype), xb], axis=1), POOL_BUF
    b_out = mixer_b(ext, n_prefix, pos0, w_pool, s_pool)
    x_out = mixer_x(q, mk, mv)
    merged = jnp.concatenate([rmsnorm(a_out, g_group[:D_A]),
                              rmsnorm(b_out, g_group[D_A:D_A + D_B]),
                              rmsnorm(x_out, g_group[D_A + D_B:])], axis=-1)
    return x + merged @ w_out, v_rows, ext[:, -POOL_BUF:]

def swiglu(x, wg, wu, wd):
    return (jax.nn.silu(x @ wg) * (x @ wu)) @ wd

def moe_swiglu(x, w_router, wg, wu, wd):
    xf = x.reshape(-1, D_MODEL)
    logits = xf.astype(jnp.float32) @ w_router.astype(jnp.float32)
    vals, idx = lax.top_k(logits, TOP_K)
    wts = jax.nn.softmax(vals, axis=-1)
    gates = jnp.sum(jax.nn.one_hot(idx, N_EXPERTS, dtype=jnp.float32) * wts[..., None], axis=1)
    out = jnp.zeros(xf.shape, jnp.float32)
    for e in range(N_EXPERTS):
        out = out + gates[:, e:e + 1] * swiglu(xf, wg[e], wu[e], wd[e]).astype(jnp.float32)
    return out.astype(x.dtype).reshape(x.shape)

def channel_sublayer(x, l, g_ffn, w_dense_gate, w_dense_up, w_dense_down,
                     w_router, w_moe_gate, w_moe_up, w_moe_down):
    h = rmsnorm(x, g_ffn[l])
    i = l // 2
    if l % 2 == 0:
        f = swiglu(h, w_dense_gate[i], w_dense_up[i], w_dense_down[i])
    else:
        f = moe_swiglu(h, w_router[i], w_moe_gate[i], w_moe_up[i], w_moe_down[i])
    return x + f

def setup_inputs(seed: int = 0) -> dict:
    key = jax.random.key(seed)
    ks = iter(jax.random.split(key, 32))
    f32 = jnp.float32

    def nrm(shape, scale):
        return jax.random.normal(next(ks), shape, f32) * scale

    def gain(shape):
        return 1.0 + 0.05 * jax.random.normal(next(ks), shape, f32)

    return {
        "x_prompt": nrm((BATCH, SEQ, D_MODEL), 1.0),
        "x_sample": nrm((DEC_BATCH, DEC_SEQ, D_MODEL), 1.0),
        "mem_prompt": nrm((BATCH, N_MEM, D_MODEL), 1.0),
        "state_pool": nrm((DEPTH, DEC_BATCH, POOL_BUF, D_B), 1.0),
        "cache_mem_k": nrm((DEPTH, DEC_BATCH, N_MEM, X_HEADS, X_HEAD_DIM), 1.0),
        "cache_mem_v": nrm((DEPTH, DEC_BATCH, N_MEM, X_HEADS, X_HEAD_DIM), 1.0),
        "g_mix_norm": gain((DEPTH, D_MODEL)),
        "w_in": nrm((DEPTH, D_MODEL, D_IN), D_MODEL ** -0.5),
        "g_v": gain((DEPTH, D_A)),
        "w_spatial": nrm((DEPTH, A_HEADS, CHUNK, CHUNK), 0.5 * CHUNK ** -0.5),
        "b_spatial": gain((DEPTH, A_HEADS, CHUNK)),
        "w_pool": nrm((DEPTH, N_POOL_GROUPS, POOL_GD, POOL_GD), POOL_GD ** -0.5),
        "s_pool": gain((DEPTH, D_B)),
        "g_mem": gain((DEPTH, D_MODEL)),
        "w_mem_kv": nrm((DEPTH, D_MODEL, 2 * D_X), D_MODEL ** -0.5),
        "g_group": gain((DEPTH, D_MODEL)),
        "w_out": nrm((DEPTH, D_MODEL, D_MODEL), D_MODEL ** -0.5),
        "g_ffn_norm": gain((DEPTH, D_MODEL)),
        "w_dense_gate": nrm((N_DENSE, D_MODEL, D_FF), D_MODEL ** -0.5),
        "w_dense_up": nrm((N_DENSE, D_MODEL, D_FF), D_MODEL ** -0.5),
        "w_dense_down": nrm((N_DENSE, D_FF, D_MODEL), D_FF ** -0.5),
        "w_router": nrm((N_MOE, D_MODEL, N_EXPERTS), D_MODEL ** -0.5),
        "w_moe_gate": nrm((N_MOE, N_EXPERTS, D_MODEL, D_FF_E), D_MODEL ** -0.5),
        "w_moe_up": nrm((N_MOE, N_EXPERTS, D_MODEL, D_FF_E), D_MODEL ** -0.5),
        "w_moe_down": nrm((N_MOE, N_EXPERTS, D_FF_E, D_MODEL), D_FF_E ** -0.5),
        "g_final": gain((D_MODEL,)),
    }

def reference(x_prompt, x_sample, mem_prompt, state_pool, cache_mem_k, cache_mem_v,
              g_mix_norm, w_in, g_v, w_spatial, b_spatial, w_pool, s_pool, g_mem, w_mem_kv,
              g_group, w_out, g_ffn_norm, w_dense_gate, w_dense_up, w_dense_down,
              w_router, w_moe_gate, w_moe_up, w_moe_down, g_final):
    xp = x_prompt
    xs = x_sample
    dec_seq = x_sample.shape[1]
    pool_p, mk_p, mv_p, pool_s, vrows_s = [], [], [], [], []
    for l in range(DEPTH):
        mix_w = (g_mix_norm[l], w_in[l], g_v[l], w_spatial[l], b_spatial[l],
                 w_pool[l], s_pool[l], g_group[l], w_out[l])
        mk, mv = mem_kv(mem_prompt, g_mem[l], w_mem_kv[l])
        xp, _, buf_p = mixing_sublayer(xp, None, 0, CHUNK, mk, mv, *mix_w)
        mk_p.append(mk)
        mv_p.append(mv)
        pool_p.append(buf_p)
        xs, v_rows, buf_s = mixing_sublayer(xs, state_pool[l], PAST_LEN, dec_seq,
                                            cache_mem_k[l], cache_mem_v[l], *mix_w)
        pool_s.append(buf_s)
        vrows_s.append(v_rows)
        ffn_w = (g_ffn_norm, w_dense_gate, w_dense_up, w_dense_down,
                 w_router, w_moe_gate, w_moe_up, w_moe_down)
        xp = channel_sublayer(xp, l, *ffn_w)
        xs = channel_sublayer(xs, l, *ffn_w)
    y_prompt = rmsnorm(xp, g_final)
    y_sample = rmsnorm(xs, g_final)
    return (y_prompt, y_sample, jnp.stack(pool_p), jnp.stack(mk_p), jnp.stack(mv_p),
            jnp.stack(pool_s), jnp.stack(vrows_s))


_drawn_inputs = setup_inputs


def setup_inputs(seed=0):
    import zlib

    import numpy as np

    out = dict(_drawn_inputs(seed))
    spreads = {}
    factors = {}
    for name, (base, spread) in spreads.items():
        noise = np.random.default_rng([zlib.crc32(name.encode()), seed]).standard_normal(out[name].shape)
        drawn = base * np.exp(spread * noise) if base else spread * noise
        out[name] = __import__('jax').numpy.asarray(drawn.astype(out[name].dtype))
    for name, factor in factors.items():
        out[name] = (out[name] * factor).astype(out[name].dtype)
    return out
```

```python
from contextlib import ExitStack

import concourse.bass as bass
import concourse.mybir as mybir
import numpy as np

D, SEQ, DEPTH, NREQ, REQT = 1024, 256, 2, 8, 4
DA = DB = 384
DX, HEADS, HD, NMEM = 256, 4, 64, 256
AH, AHD = 4, 96
WINDOWS, GD, PBUF = (2, 4, 8, 16), 96, 15
FF, NE, FFE = 2816, 8, 3584
EPS = 1e-6
P = 128
KD = D // P
NS = NREQ * REQT
NT = SEQ + NS
ROWS = (P, P, NS)
CW = 2048

RAWS, SPL = 6, 3
KV_CH, Q_CH, CK_CH, UV_CH, CV_CH, WO_CH = 2, 1, 2, 5, 2, 4
MIX_CH = KV_CH + Q_CH + CK_CH + UV_CH + CV_CH + WO_CH
NF = FF // P
UP_CH = NF
DOWN_BLOCKS = 24
DOWN_CH = KD * DOWN_BLOCKS // 16
C_UP = MIX_CH
C_DOWN = C_UP + UP_CH
C_MIX1 = C_DOWN + DOWN_CH
C_MOE = C_MIX1 + MIX_CH
STEPS = FFE // 256
EXP_CH = 3 * STEPS
ROUND_CH = NE * EXP_CH
N_CH = C_MOE + ROUND_CH
MAX_ROUNDS = -(-NT // P)
FAR = 8192.0
NEVER = -3.0e38
NORMS = 5
N_MEM, N_MIX, N_V, N_GROUP, N_FFN = range(NORMS)
LAYER_STORES = 6

def _columns():
    at, n = {}, 0
    for name, width in (("ident", P), ("gains", DEPTH * 4 * KD),
                        ("pool0", 4 * SEQ), ("pool1", 4 * P), ("pool_s", 4 * NS), ("pool_st", 4 * NS),
                        ("bias", DEPTH * 2 * AH), ("w_pool", DEPTH * 4 * GD),
                        ("w_sp", DEPTH * AH * P), ("w_sps", DEPTH * AH * NS),
                        ("g_v", DEPTH * DA), ("s_pool", DEPTH * DB)):
        at[name] = (n, n + width)
        n += width
    return at, n


COL, N_CONST = _columns()
N_LATE = 3 * P + KD * NE
G_MEM, G_MIX, G_GROUP, G_FFN = range(4)


def build(nc, io):
    F, FR, I32 = mybir.dt.float32, mybir.dt.float32r, mybir.dt.int32
    ACT, ALU, AX = mybir.ActivationFunctionType, mybir.AluOpType, mybir.AxisListType
    ctx = ExitStack()
    with ctx:
        sb = lambda n, s, d=F: ctx.enter_context(nc.sbuf_tensor(n, s, d))
        sem = lambda n: ctx.enter_context(nc.semaphore(n))

        raw = sb("raw", [P, RAWS, CW])
        whi = sb("whi", [P, SPL, CW], FR)
        wlo = sb("wlo", [P, SPL, CW], FR)
        x = sb("x", [P, 3, D])
        hT_hi = sb("hT_hi", [P, KD, NT], FR)
        hT_lo = sb("hT_lo", [P, KD, NT], FR)
        const = sb("const", [P, N_CONST])
        ss = sb("ss", [P, NORMS, 9])
        ms = sb("ms", [P, NORMS, 9])
        rstd = sb("rstd", [P, NORMS, 9])
        half = sb("half", [P, 9])
        junk = sb("junk", [P, D], mybir.dt.bfloat16)

        def phase():
            return ExitStack()

        with phase() as room:
            ph = lambda n, s, d=F: room.enter_context(nc.sbuf_tensor(n, s, d))
            xn = ph("xn", [P, 3, D])
            stage = ph("stage", [P, 6, DA])
            kv = ph("kv", [P, 2, 2 * DX])
            kT = ph("kT", [P, 2, NMEM])
            qT = ph("qT", [P, 2, SEQ])
            state = ph("state", [NREQ * PBUF, DB])
            qs_hi = ph("qs_hi", [P, 2, NREQ, HEADS, REQT], FR)
            qs_lo = ph("qs_lo", [P, 2, NREQ, HEADS, REQT], FR)
            sST = ph("sST", [P, 2, P])
            sP = ph("sP", [P, NMEM])
            sPT_hi = ph("sPT_hi", [P, 2, P], FR)
            sPT_lo = ph("sPT_lo", [P, 2, P], FR)
            PT = ph("PT", [P, 2, 4, P])
            xb = ph("xb", [P, 3, DB])
            dT = ph("dT", [P, 4, NT])
            osT = ph("osT", [P, 2, NS])
            ob = ph("ob", [P, 3, DX])
            mx = ph("mx", [P, 9])
            nmx = ph("nmx", [P, 9])
            den = ph("den", [P, 9])
            rden = ph("rden", [P, 9])
        mem = stage[:, :, :].rearrange("p a b -> p (a b)")[:, 0:2 * D].rearrange("p (t d) -> p t d", t=2)
        b_rows = dT[:, :, :].rearrange("p a b -> p (a b)").rearrange("p (t d) -> p t d", t=3)
        vg, ug = stage[:, 0:3, :], stage[:, 3:6, :]
        prob = xn[:, :, :].rearrange("p a b -> p (a b)")[:, 0:8 * NMEM].rearrange("p (g m) -> p g m", g=8)

        with phase() as room:
            ph = lambda n, s, d=F: room.enter_context(nc.sbuf_tensor(n, s, d))
            HT_hi = ph("HT_hi", [P, NF, NT], FR)
            HT_lo = ph("HT_lo", [P, NF, NT], FR)
            sg = ph("sg", [P, 2, NT])
            hf = ph("hf", [P, 2, NT])
            yT = ph("yT", [P, 2, NT])

        with phase() as room:
            ph = lambda n, s, d=F: room.enter_context(nc.sbuf_tensor(n, s, d))
            xm = ph("xm", [P, 3, D])
            gT_hi = ph("gT_hi", [P, KD, P], FR)
            gT_lo = ph("gT_lo", [P, KD, P], FR)
            sel = ph("sel", [P, 3, P])
            selT = ph("selT", [P, NT], FR)
            esg = ph("esg", [P, 2, 256])
            eh = ph("eh", [P, 2, 256])
            eT_hi = ph("eT_hi", [P, 2, 2, P], FR)
            eT_lo = ph("eT_lo", [P, 2, 2, P], FR)
            y_hi = ph("y_hi", [P, D], FR)
            y_lo = ph("y_lo", [P, D], FR)
            late = ph("late", [P, N_LATE])
            zero = ph("zero", [P, 512], mybir.dt.bfloat16)
            logits = ph("logits", [P, 3, NE])
            top = ph("top", [P, 3, 8])
            nfirst = ph("nfirst", [P, 3])
            left = ph("left", [P, 3, NE])
            mask = ph("mask", [P, 3, NE])
            expo = ph("expo", [P, 3, NE])
            gden = ph("gden", [P, 3])
            gate = ph("gate", [P, 3, NE])
            posm = ph("posm", [P, 3, NE])
            cmax = ph("cmax", [1, 1])
            over = ph("over", [1, 2])
            rounds = ph("rounds", [1, 1], I32)
            rt_hi = ph("rt_hi", [P, KD, NE], FR)
            rt_lo = ph("rt_lo", [P, KD, NE], FR)
            gfin = ph("gfin", [P, D])

        bank = [ctx.enter_context(nc.psum_tensor(f"bank{i}", [P, 512], F)) for i in range(8)]

        def C(name, rows=P):
            a, b = COL[name]
            return const[0:rows, a:b]

        ident = C("ident")
        gains = C("gains").rearrange("p (l g k) -> p l g k", l=DEPTH, g=4)
        pool0 = C("pool0").rearrange("p (g t) -> p g t", g=4)
        pool1 = C("pool1").rearrange("p (g t) -> p g t", g=4)
        pool_s = C("pool_s", NS).rearrange("p (g t) -> p g t", g=4)
        pool_st = C("pool_st", NREQ * PBUF).rearrange("p (g t) -> p g t", g=4)
        bias = C("bias").rearrange("p (l s h) -> p l s h", l=DEPTH, s=2)
        before, ones, slots = late[:, 0:P], late[:, P:2 * P], late[:, 2 * P:3 * P]
        router = late[:, 3 * P:].rearrange("p (k e) -> p k e", k=KD)
        w_pool = C("w_pool", GD).rearrange("p (l g d) -> p l g d", l=DEPTH, g=4)
        w_sp = C("w_sp").rearrange("p (l h t) -> p l h t", l=DEPTH, h=AH)
        w_sps = C("w_sps", NS).rearrange("p (l h t) -> p l h t", l=DEPTH, h=AH)
        g_v = C("g_v").rearrange("p (l d) -> p l d", l=DEPTH)
        s_pool = C("s_pool").rearrange("p (l d) -> p l d", l=DEPTH)

        raw_full = [sem(f"raw_full{i}") for i in range(RAWS)]
        hi_ready, lo_ready, chunk_used = sem("hi_ready"), sem("lo_ready"), sem("chunk_used")
        const_in, mem_in, state_in, x_in, gfin_in, late_in = (sem(n) for n in ("const_in", "mem_in", "state_in", "x_in", "gfin_in", "late_in"))
        preset, masked, q_zeroed, e_zeroed = sem("preset"), sem("masked"), sem("q_zeroed"), sem("e_zeroed")
        squares, rstd_ok, rows_ok = sem("squares"), sem("rstd_ok"), sem("rows_ok")
        turned, turned_hi, turned_lo = sem("turned"), sem("turned_hi"), sem("turned_lo")
        act_chain, dve_chain, pool_chain = sem("act_chain"), sem("dve_chain"), sem("pool_chain")
        S = {n: sem(n) for n in (
            "kv_out", "q_out", "kT_done", "kT_out", "sc_done", "max_out", "exp_done", "ssc_out", "sscT_done", "smax_out",
            "sexp_done", "sprob_out", "v_done", "vg_out", "v_out", "xb_done", "xb_out", "PT_done", "PT_out", "sPT_done",
            "sPT_out", "ug_out", "o_done", "osT_out", "os_done", "o_out", "dT_done", "dT_out", "mix_done", "a_out",
            "y_done", "b_out", "x_mixed", "silu_out", "hf_out", "H_out", "yT_done", "yT_out", "y_turned", "x_dense",
            "rt_out", "xm_out", "logit_done", "logit_out", "exp2_out", "pos_in", "pos_done", "rounds_ok", "pos_moved", "sel_out",
            "selT_done", "selT_out", "gat_done", "gat_hi", "gat_lo", "esilu", "eh_out", "eT_done", "eT_hi_out", "eT_out",
            "y_hi_out", "y_out", "scat_done", "x_added", "fin_out")}
        stored = sem("stored")

        block = ctx.enter_context(nc.Block())

        def load_chunk(sp, c, slot):
            c, row = c
            if not (isinstance(c, int) and c < RAWS):
                sp.wait_ge(lo_ready, c - RAWS + 1)
            sp.dma_start(raw[:, slot, :], io["stream"][bass.ds(row * P, P), :]).then_inc(raw_full[slot], 16)

        def split_hi(act, c, lap, slot):
            act.wait_ge(raw_full[slot], 16 * lap + 16)
            if not (isinstance(c, int) and c < SPL):
                act.wait_ge(chunk_used, c - SPL + 1)
            nc.scalar.activation(whi[:, slot % SPL, :], raw[:, slot, :], ACT.Copy).then_inc(hi_ready, 1)

        def split_lo(dve, c, slot):
            dve.wait_ge(hi_ready, c + 1)
            nc.vector.tensor_tensor(wlo[:, slot % SPL, :], raw[:, slot, :], whi[:, slot % SPL, :].bitcast(F),
                                    ALU.subtract).then_inc(lo_ready, 1)

        def hi_static(act, *cs):
            for c in cs:
                split_hi(act, c, c // RAWS, c % RAWS)

        def lo_static(dve, *cs):
            for c in cs:
                split_lo(dve, c, c % RAWS)

        def mm3(out, a_hi, a_lo, b_hi, b_lo, start, stop, **kw):
            nc.tensor.matmul(out, a_hi, b_hi, start=start, stop=False, **kw)
            nc.tensor.matmul(out, a_hi, b_lo, start=False, stop=False, **kw)
            return nc.tensor.matmul(out, a_lo, b_hi, start=False, stop=stop, **kw)

        def blk(ring, slot, b, n=1):
            return ring[:, slot % SPL, b * P:(b + n) * P]

        def use(l, which):
            return 4 * l + which

        @block.sync
        def _(sp):
            def mix_chunks(base):
                for c in range(base, base + MIX_CH):
                    load_chunk(sp, (c, c), c % RAWS)
            sp.dma_start(const[:, :], io["const"]).then_inc(const_in, 16)
            sp.dma_start(mem, io["mem"].rearrange("(t p) d -> p t d", p=P)).then_inc(mem_in, 16)
            for c in range(2):
                load_chunk(sp, (c, c), c % RAWS)
            sp.dma_start(x[:, 0:2, :], io["x_prompt"].rearrange("(t p) d -> p t d", p=P)).then_inc(x_in, 16)
            sp.dma_start(x[0:NS, 2, :], io["x_sample"]).then_inc(x_in, 16)
            sp.dma_start(state[:, :], io["state"][0]).then_inc(state_in, 16)
            for c in range(2, MIX_CH):
                load_chunk(sp, (c, c), c % RAWS)
            with nc.sync.Fori(0, UP_CH // RAWS) as i:
                for j in range(RAWS):
                    c = C_UP + RAWS * i + j
                    load_chunk(sp, (c, c), (C_UP + j) % RAWS)
            for c in range(C_UP + UP_CH // RAWS * RAWS, C_DOWN):
                load_chunk(sp, (c, c), c % RAWS)
            with nc.sync.Fori(0, DOWN_CH // RAWS) as i:
                for j in range(RAWS):
                    c = C_DOWN + RAWS * i + j
                    load_chunk(sp, (c, c), (C_DOWN + j) % RAWS)
            load_chunk(sp, (C_MIX1, C_MIX1), C_MIX1 % RAWS)
            sp.wait_ge(S["x_dense"], KD + 2)
            sp.dma_start(mem, io["mem"].rearrange("(t p) d -> p t d", p=P)).then_inc(mem_in, 16)
            sp.dma_start(state[:, :], io["state"][1]).then_inc(state_in, 16)
            for c in range(C_MIX1 + 1, C_MOE):
                load_chunk(sp, (c, c), c % RAWS)
            sp.wait_ge(turned_lo, KD * use(DEPTH, 0))
            sp.wait_ge(stored, 16 * LAYER_STORES * DEPTH)
            sp.dma_start(late[:, :], io["late"]).then_inc(late_in, 16)
            sp.wait_ge(S["rounds_ok"], 1)
            n_rounds = nc.sync.value_load(rounds[0:1, 0:1], min_val=1, max_val=MAX_ROUNDS)
            with nc.sync.Fori(0, n_rounds) as r:
                with nc.sync.Fori(0, ROUND_CH // RAWS) as i:
                    for j in range(RAWS):
                        row = C_MOE + RAWS * i + j
                        load_chunk(sp, (row + ROUND_CH * r, row), (C_MOE + j) % RAWS)
            sp.dma_start(gfin[:, :], io["g_final"]).then_inc(gfin_in, 16)

        @block.gpsimd
        def _(pool):
            n_chain = [0]

            def link(ins):
                n_chain[0] += 1
                ins.then_inc(pool_chain, 1)
                pool.wait_ge(pool_chain, n_chain[0])

            nc.gpsimd.memset(ss[:, :, :], 1.0)
            nc.gpsimd.memset(half[:, :], -0.5).then_inc(preset, 1)
            pool.wait_ge(preset, 1)

            def power(n, parts):
                pool.wait_ge(squares, n + 1)
                n %= NORMS
                for a, b, width in parts:
                    last = nc.gpsimd.tensor_scalar(ms[:, n, a:b], ss[:, n, a:b], 1.0 / width, EPS, ALU.mult, ALU.add)
                link(last)
                b = parts[-1][1]
                nc.gpsimd.tensor_tensor(rstd[:, n, 0:b], ms[:, n, 0:b], half[:, 0:b], ALU.pow).then_inc(rstd_ok, 1)

            def store(out, in_):
                pool.dma_start(out, in_).then_inc(stored, 16)

            for l in range(DEPTH):
                n0 = NORMS * l
                if l:
                    pool.wait_ge(S["x_dense"], KD + 2)
                nc.gpsimd.memset(qs_hi[:, :, :, :, :].bitcast(F), 0.0)
                nc.gpsimd.memset(qs_lo[:, :, :, :, :].bitcast(F), 0.0).then_inc(q_zeroed, 1)
                power(n0 + N_MEM, [(0, 3, D)])
                power(n0 + N_MIX, [(0, 3, D)])
                if l == 0:
                    pool.wait_ge(const_in, 16)
                    for k in range(DEPTH):
                        for h in range(AH):
                            nc.gpsimd.affine_select(out=w_sp[:, k, h, :], in_=w_sp[:, k, h, :], compare_op=ALU.is_ge,
                                                    fill=0.0, base=0, pattern=[[1, P]], channel_multiplier=-1)
                            last = nc.gpsimd.affine_select(out=w_sps[:, k, h, :], in_=w_sps[:, k, h, :],
                                                           compare_op=ALU.is_ge, fill=0.0, base=0, pattern=[[1, NS]],
                                                           channel_multiplier=-1)
                    last.then_inc(masked, 1)
                pool.wait_ge(S["kv_out"], l + 1)
                store(io["mem_k"][l].rearrange("(t p) d -> p t d", p=P), kv[:, :, 0:DX])
                store(io["mem_v"][l].rearrange("(t p) d -> p t d", p=P), kv[:, :, DX:2 * DX])
                power(n0 + N_V, [(0, 3, DA)])
                pool.wait_ge(S["xb_out"], l + 1)
                store(io["pool_prompt"][l], xb[P - PBUF:P, 1, :])
                store(io["pool_sample"][l, :, PBUF - REQT:PBUF, :], xb[0:NS, 2, :])
                store(io["pool_sample"][l, :, 0:PBUF - REQT, :],
                      io["state"][l].rearrange("(b r) d -> b r d", r=PBUF)[:, REQT:PBUF, :])
                pool.wait_ge(S["v_out"], l + 1)
                store(io["v_rows"][l], vg[0:NS, 2, :])
                power(n0 + N_GROUP, [(0, 6, DA), (6, 9, DX)])
                power(n0 + N_FFN, [(0, 3, D)])
            power(NORMS * DEPTH, [(0, 3, D)])
            pool.wait_ge(S["fin_out"], 1)
            store(io["y_prompt"].rearrange("(t p) d -> p t d", p=P), xm[:, 0:2, :])
            store(io["y_sample"], xm[0:NS, 2, :])
            pool.wait_ge(stored, 16 * (DEPTH * (LAYER_STORES) + 2))

        @block.scalar
        def _(act):
            n_chain = [0]

            def link(ins):
                n_chain[0] += 1
                ins.then_inc(act_chain, 1)
                act.wait_ge(act_chain, n_chain[0])

            def sum_squares(src, n, col, tiles=(0, 1, 2), signal=True):
                for t in tiles:
                    r = ROWS[t]
                    last = nc.scalar.activation(junk[0:r, 0:src.shape[-1]], src[0:r, t, :], ACT.Square,
                                                accum_out=ss[0:r, n, col + t:col + t + 1])
                    link(last)
                if signal:
                    act.sem_inc(squares, 1)

            def turn_hi(l, which, n_tok):
                for k in range(KD):
                    act.wait_ge(turned, KD * use(l, which) + k + 1)
                    nc.scalar.activation(hT_hi[:, k, 0:n_tok], bank[k % 2][:, 0:n_tok], ACT.Copy,
                                         scale=gains[:, l, which, k:k + 1]).then_inc(turned_hi, 1)

            act.wait_ge(preset, 1)
            for l in range(DEPTH):
                c0 = l * C_MIX1
                if l == 0:
                    hi_static(act, c0)
                hi_static(act, c0 + 1, c0 + 2)
                act.wait_ge(mem_in, 16 * (l + 1))
                sum_squares(mem, N_MEM, 0, (0, 1))
                act.wait_ge(const_in, 16)
                turn_hi(l, G_MEM, NMEM)
                act.wait_ge(x_in, 32)
                sum_squares(x, N_MIX, 0)
                act.wait_ge(chunk_used, c0 + KV_CH)
                turn_hi(l, G_MIX, NT)
                hi_static(act, c0 + 3, c0 + 4)
                for i in range(4):
                    act.wait_ge(S["max_out"], 4 * l + i + 1)
                    for g in (2 * i, 2 * i + 1):
                        last = nc.scalar.activation(prob[:, g, :], bank[4 + i][:, (g % 2) * NMEM:(g % 2 + 1) * NMEM],
                                                    ACT.Exp, bias=nmx[:, g:g + 1], accum_out=den[:, g:g + 1])
                    last.then_inc(S["exp_done"], 1)
                hi_static(act, c0 + 5, c0 + 6)
                act.wait_ge(S["smax_out"], l + 1)
                nc.scalar.activation(sP[:, :], bank[3][:, NMEM:2 * NMEM], ACT.Exp, bias=nmx[:, 8:9],
                                     accum_out=den[:, 8:9]).then_inc(S["sexp_done"], 1)
                hi_static(act, c0 + 7)
                for t in range(3):
                    act.wait_ge(S["v_done"], 3 * l + t + 1)
                    last = nc.scalar.activation(vg[0:ROWS[t], t, :], bank[t][0:ROWS[t], 0:DA], ACT.Gelu_apprx_tanh)
                last.then_inc(S["vg_out"], 1)
                act.wait_ge(S["vg_out"], l + 1)
                sum_squares(vg, N_V, 0)
                hi_static(act, c0 + 8, c0 + 9)
                act.wait_ge(chunk_used, c0 + 10)
                for t in range(3):
                    last = nc.scalar.activation(ug[0:ROWS[t], t, :], bank[t][0:ROWS[t], 0:DA], ACT.Gelu_apprx_tanh)
                last.then_inc(S["ug_out"], 1)
                hi_static(act, c0 + 10, c0 + 11, c0 + 12)
                act.wait_ge(S["o_out"], l + 1)
                sum_squares(ob, N_GROUP, 6, signal=False)
                act.wait_ge(S["a_out"], l + 1)
                sum_squares(ug, N_GROUP, 0, signal=False)
                act.wait_ge(S["b_out"], l + 1)
                sum_squares(b_rows, N_GROUP, 3)
                hi_static(act, c0 + 13, c0 + 14)
                turn_hi(l, G_GROUP, NT)
                hi_static(act, c0 + 15)
                if l == 0:
                    hi_static(act, C_UP)
                act.wait_ge(S["x_mixed"], 6 * l + 6)
                sum_squares(x, N_FFN, 0)
                turn_hi(l, G_FFN, NT)

                if l == 0:
                    with nc.scalar.Fori(0, NF // RAWS) as i:
                        for j in range(RAWS):
                            c = C_UP + 1 + RAWS * i + j
                            at = C_UP + 1 + j
                            split_hi(act, c, i + at // RAWS, at % RAWS)
                            act.wait_ge(chunk_used, C_UP + RAWS * i + j + 1)
                            nc.scalar.activation(sg[:, j % 2, :], bank[2 + 2 * (j % 2)][:, 0:NT], ACT.Silu)\
                                .then_inc(S["silu_out"], 1)
                    for f in range(NF // RAWS * RAWS, NF):
                        hi_static(act, C_UP + 1 + f)
                        act.wait_ge(chunk_used, C_UP + f + 1)
                        nc.scalar.activation(sg[:, f % 2, :], bank[2 + 2 * (f % 2)][:, 0:NT], ACT.Silu)\
                            .then_inc(S["silu_out"], 1)
                    act.sem_inc(S["yT_out"], 2)
                    with nc.scalar.Fori(0, DOWN_CH // RAWS) as i:
                        for what in (1, 2, "y0", 3, "y1", 4, 5, "y2", 6, "y3"):
                            if isinstance(what, int):
                                at = C_DOWN + what
                                split_hi(act, at + RAWS * i, i + at // RAWS, at % RAWS)
                            else:
                                j = int(what[1])
                                if j % 2:
                                    act.wait_ge(chunk_used, C_DOWN + RAWS * i + 3 * (j + 1) // 2)
                                else:
                                    act.wait_ge(S["yT_done"], 2 * i + j // 2 + 1)
                                nc.scalar.activation(yT[:, j % 2, :], bank[6 + j % 2][:, 0:NT], ACT.Copy)\
                                    .then_inc(S["yT_out"], 1)

            for t in range(3):
                r = ROWS[t]
                act.wait_ge(S["logit_out"], 1)
                last = nc.scalar.activation(expo[0:r, t, :], logits[0:r, t, :], ACT.Exp, bias=nfirst[0:r, t:t + 1])
            last.then_inc(S["exp2_out"], 1)
            act.wait_ge(S["rounds_ok"], 1)
            n_rounds = nc.scalar.value_load(rounds[0:1, 0:1], min_val=1, max_val=MAX_ROUNDS)
            with nc.scalar.Fori(0, n_rounds) as r:
                with nc.scalar.Fori(0, NE) as e:
                    q = nc.scalar.snap(r * NE + e)
                    cb = nc.scalar.snap(q * EXP_CH + C_MOE)
                    lap = nc.scalar.snap(q * (EXP_CH // RAWS) + C_MOE // RAWS)
                    g0 = nc.scalar.snap(q * STEPS)

                    def hi(off, extra=0):
                        split_hi(act, cb + off + RAWS * extra, lap + off // RAWS + extra, off % RAWS)

                    def step_silu(s, extra=0):
                        act.wait_ge(chunk_used, cb + 3 * s + 1 + RAWS * extra)
                        nc.scalar.activation(esg[:, s % 2, :], bank[2 + s % 2][:, 0:256], ACT.Silu).then_inc(S["esilu"], 1)

                    def step_turn(s, extra=0):
                        act.wait_ge(S["eT_done"], g0 + s + 1 + 2 * extra)
                        nc.scalar.activation(eT_hi[:, s % 2, :, :].rearrange("p a b -> p (a b)"), bank[4 + s % 2][:, 0:256],
                                             ACT.Copy).then_inc(S["eT_hi_out"], 1)

                    for off in (0, 1, 2):
                        hi(off)
                    for k in range(KD):
                        if k % 4 == 0:
                            act.wait_ge(S["gat_done"], 2 * q + k // 4 + 1)
                        nc.scalar.activation(gT_hi[:, k, :], bank[k // 4][:, (k % 4) * P:(k % 4 + 1) * P], ACT.Copy,
                                             scale=gains[:, 1, G_FFN, k:k + 1]).then_inc(S["gat_hi"], 1)
                    hi(3)
                    act.wait_ge(chunk_used, cb + 2)
                    with nc.scalar.Fori(0, STEPS // 2 - 1) as p:
                        for s in (0, 1):
                            step_silu(s, p)
                            hi(3 * s + 4, p)
                            step_turn(s, p)
                            hi(3 * s + 5, p)
                            hi(3 * s + 6, p)
                    for s in (STEPS - 2, STEPS - 1):
                        step_silu(s)
                        hi(EXP_CH - STEPS + s)
                        step_turn(s)
                    act.wait_ge(chunk_used, cb + EXP_CH)
                    for n in range(2):
                        nc.scalar.activation(y_hi[:, n * 512:(n + 1) * 512], bank[6 + n][:, :], ACT.Copy)\
                            .then_inc(S["y_hi_out"], 1)
            act.wait_ge(S["x_added"], n_rounds * (6 * NE) + 6)
            sum_squares(x, 0, 0)

        @block.vector
        def _(dve):
            V = nc.vector
            n_chain = [0]

            def link(ins):
                n_chain[0] += 1
                ins.then_inc(dve_chain, 1)
                dve.wait_ge(dve_chain, n_chain[0])

            def scale_rows(src, n, tiles=(0, 1, 2)):
                dve.wait_ge(rstd_ok, n + 1)
                for t in tiles:
                    r = ROWS[t]
                    last = V.tensor_scalar(xn[0:r, t, :], src[0:r, t, :], rstd[0:r, n % NORMS, t:t + 1], None, ALU.mult)
                last.then_inc(rows_ok, 1)

            def turn_lo(l, which, n_tok):
                for k in range(KD):
                    dve.wait_ge(turned_hi, KD * use(l, which) + k + 1)
                    V.scalar_tensor_tensor(out=hT_lo[:, k, 0:n_tok], in0=bank[k % 2][:, 0:n_tok],
                                           scalar=gains[:, l, which, k:k + 1], in1=hT_hi[:, k, 0:n_tok].bitcast(F),
                                           op0=ALU.mult, op1=ALU.subtract).then_inc(turned_lo, 1)

            for l in range(DEPTH):
                c0 = l * C_MIX1
                n0 = NORMS * l
                if l == 0:
                    lo_static(dve, c0)
                lo_static(dve, c0 + 1, c0 + 2)
                dve.wait_ge(mem_in, 16 * (l + 1))
                scale_rows(mem, n0 + N_MEM, (0, 1))
                dve.wait_ge(const_in, 16)
                turn_lo(l, G_MEM, NMEM)
                scale_rows(x, n0 + N_MIX)
                dve.wait_ge(chunk_used, c0 + KV_CH)
                for t in range(2):
                    last = V.tensor_copy(kv[:, t, :], bank[2 + t][:, :])
                last.then_inc(S["kv_out"], 1)
                turn_lo(l, G_MIX, NT)
                dve.wait_ge(chunk_used, c0 + 3)
                dve.wait_ge(q_zeroed, l + 1)
                for f in range(2):
                    V.tensor_scalar(qT[:, f, :], bank[4 + f][:, 0:SEQ], HD ** -0.5, None, ALU.mult)
                for f in range(2):
                    for p in range(2):
                        last = V.tensor_scalar(qs_hi[HD * p:HD * p + HD, f, :, 2 * f + p, :],
                                               bank[4 + f][HD * p:HD * p + HD, SEQ:NT].rearrange("p (b t) -> p b t", t=REQT),
                                               HD ** -0.5, None, ALU.mult)
                link(last)
                for f in range(2):
                    for p in range(2):
                        last = V.scalar_tensor_tensor(
                            out=qs_lo[HD * p:HD * p + HD, f, :, 2 * f + p, :],
                            in0=bank[4 + f][HD * p:HD * p + HD, SEQ:NT].rearrange("p (b t) -> p b t", t=REQT),
                            scalar=HD ** -0.5, in1=qs_hi[HD * p:HD * p + HD, f, :, 2 * f + p, :].bitcast(F),
                            op0=ALU.mult, op1=ALU.subtract)
                last.then_inc(S["q_out"], 1)
                dve.wait_ge(S["kT_done"], l + 1)
                V.tensor_copy(kT[:, :, :].rearrange("p a b -> p (a b)"), bank[2][:, :]).then_inc(S["kT_out"], 1)
                lo_static(dve, c0 + 3, c0 + 4)
                for i in range(4):
                    dve.wait_ge(S["sc_done"], 4 * l + i + 1)
                    link(V.reduce_max(mx[:, 2 * i:2 * i + 2], bank[4 + i][:, :].rearrange("p (g m) -> p g m", g=2), AX.X))
                    V.tensor_scalar(nmx[:, 2 * i:2 * i + 2], mx[:, 2 * i:2 * i + 2], -1.0, None, ALU.mult)\
                        .then_inc(S["max_out"], 1)
                dve.wait_ge(chunk_used, c0 + 5)
                V.tensor_copy(sST[:, :, :].rearrange("p a b -> p (a b)"), bank[3][:, 0:256]).then_inc(S["ssc_out"], 1)
                lo_static(dve, c0 + 5, c0 + 6)
                dve.wait_ge(S["sscT_done"], l + 1)
                link(V.reduce_max(mx[:, 8:9], bank[3][:, 256:512], AX.X))
                V.tensor_scalar(nmx[:, 8:9], mx[:, 8:9], -1.0, None, ALU.mult).then_inc(S["smax_out"], 1)
                lo_static(dve, c0 + 7)
                dve.wait_ge(S["sexp_done"], l + 1)
                link(V.reciprocal(rden[:, :], den[:, :]))
                V.tensor_scalar(sP[:, :], sP[:, :], rden[:, 8:9], None, ALU.mult).then_inc(S["sprob_out"], 1)
                lo_static(dve, c0 + 8, c0 + 9)
                for t in range(3):
                    dve.wait_ge(S["xb_done"], 3 * l + t + 1)
                    last = V.tensor_copy(xb[0:ROWS[t], t, :], bank[4 + t][0:ROWS[t], 0:DB])
                last.then_inc(S["xb_out"], 1)
                dve.wait_ge(rstd_ok, n0 + N_V + 1)
                for t in range(3):
                    r = ROWS[t]
                    last = V.scalar_tensor_tensor(out=vg[0:r, t, :], in0=vg[0:r, t, :], scalar=rstd[0:r, N_V, t:t + 1],
                                                  in1=g_v[0:r, l, :], op0=ALU.mult, op1=ALU.mult)
                last.then_inc(S["v_out"], 1)
                for i in range(4):
                    dve.wait_ge(S["PT_done"], 4 * l + i + 1)
                    V.tensor_copy(PT[:, i % 2, :, :].rearrange("p a b -> p (a b)"), bank[(7, 3)[i % 2]][:, :])\
                        .then_inc(S["PT_out"], 1)
                dve.wait_ge(S["sPT_done"], l + 1)
                link(V.tensor_copy(sPT_hi[:, :, :].rearrange("p a b -> p (a b)"), bank[5][:, 0:256]))
                V.tensor_tensor(sPT_lo[:, :, :].rearrange("p a b -> p (a b)"), bank[5][:, 0:256],
                                sPT_hi[:, :, :].rearrange("p a b -> p (a b)").bitcast(F), ALU.subtract)\
                    .then_inc(S["sPT_out"], 1)
                dve.wait_ge(S["o_done"], 4 * l + 4)
                for t in range(2):
                    for p in range(2):
                        by_head = lambda a: a.rearrange("p (f h d) -> p f h d", f=2, h=2)[:, :, p, :]
                        sums = rden[:, 4 * t + 2 * p:4 * t + 2 * p + 2].rearrange("p (f a) -> p f a", a=1)
                        last = V.tensor_tensor(by_head(ob[:, t, :]), by_head(bank[4][:, t * DX:(t + 1) * DX]),
                                               sums.to_broadcast([P, 2, HD]), ALU.mult)
                lo_static(dve, c0 + 10, c0 + 11, c0 + 12)
                dve.wait_ge(chunk_used, c0 + 12)
                for f in range(2):
                    for p in range(2):
                        last = V.tensor_copy(osT[HD * p:HD * p + HD, f, :].rearrange("p (b t) -> p b t", t=REQT),
                                             bank[6][HD * p:HD * p + HD, f * P:(f + 1) * P]
                                             .rearrange("p (b h t) -> p b h t", b=NREQ, h=HEADS)[:, :, 2 * f + p, :])
                last.then_inc(S["osT_out"], 1)
                dve.wait_ge(S["os_done"], l + 1)
                V.tensor_copy(ob[0:NS, 2, :], bank[7][0:NS, 0:DX]).then_inc(S["o_out"], 1)
                for g in range(4):
                    dve.wait_ge(S["dT_done"], 4 * l + g + 1)
                    last = V.tensor_copy(dT[0:GD, g, :], bank[g][0:GD, 0:NT])
                last.then_inc(S["dT_out"], 1)
                dve.wait_ge(S["ug_out"], l + 1)
                for t in range(3):
                    dve.wait_ge(S["mix_done"], 3 * l + t + 1)
                    r = ROWS[t]
                    for h in range(AH):
                        cols = slice(h * AHD, (h + 1) * AHD)
                        last = V.scalar_tensor_tensor(out=ug[0:r, t, cols], in0=bank[4 + t][0:r, cols],
                                                      scalar=bias[0:r, l, t // 2, h:h + 1], in1=ug[0:r, t, cols],
                                                      op0=ALU.add, op1=ALU.mult)
                last.then_inc(S["a_out"], 1)
                dve.wait_ge(S["y_done"], 3 * l + 3)
                for t in range(3):
                    r = ROWS[t]
                    last = V.tensor_tensor(b_rows[0:r, t, :], bank[t][0:r, 0:DB], s_pool[0:r, l, :], ALU.mult)
                last.then_inc(S["b_out"], 1)
                lo_static(dve, c0 + 13, c0 + 14)
                dve.wait_ge(rstd_ok, n0 + N_GROUP + 1)
                for src, a, b, col in ((ug, 0, DA, 0), (b_rows, DA, DA + DB, 3), (ob, DA + DB, D, 6)):
                    for t in range(3):
                        r = ROWS[t]
                        last = V.tensor_scalar(xn[0:r, t, a:b], src[0:r, t, :], rstd[0:r, N_GROUP, col + t:col + t + 1],
                                               None, ALU.mult)
                last.then_inc(rows_ok, 1)
                turn_lo(l, G_GROUP, NT)
                lo_static(dve, c0 + 15)
                if l == 0:
                    lo_static(dve, C_UP)
                for n in range(2):
                    dve.wait_ge(chunk_used, c0 + 14 + 2 * n)
                    for t in range(3):
                        r = ROWS[t]
                        V.tensor_tensor(x[0:r, t, n * 512:(n + 1) * 512], x[0:r, t, n * 512:(n + 1) * 512],
                                        bank[2 + 3 * n + t][0:r, :], ALU.add).then_inc(S["x_mixed"], 1)
                dve.wait_ge(S["x_mixed"], 6 * l + 6)
                scale_rows(x, n0 + N_FFN)
                turn_lo(l, G_FFN, NT)
                dve.wait_ge(stored, 16 * (LAYER_STORES) * (l + 1))

                if l == 0:
                    dve.sem_inc(S["H_out"], 2)

                    def hidden(f, j):
                        dve.wait_ge(S["silu_out"], f + 1)
                        up_ps = bank[3 + 2 * (j % 2)][:, 0:NT]
                        at = bass.ds(f * NT, NT)
                        V.tensor_tensor(HT_hi[:, :, :].rearrange("p a b -> p (a b)")[:, at], sg[:, j % 2, :], up_ps, ALU.mult)
                        V.tensor_tensor(hf[:, j % 2, :], sg[:, j % 2, :], up_ps, ALU.mult).then_inc(S["hf_out"], 1)
                        dve.wait_ge(S["hf_out"], f + 1)
                        V.tensor_tensor(HT_lo[:, :, :].rearrange("p a b -> p (a b)")[:, at], hf[:, j % 2, :],
                                        HT_hi[:, :, :].rearrange("p a b -> p (a b)")[:, at].bitcast(F), ALU.subtract)\
                            .then_inc(S["H_out"], 1)
                    with V.Fori(0, NF // RAWS) as i:
                        for j in range(RAWS):
                            split_lo(dve, C_UP + 1 + RAWS * i + j, (C_UP + 1 + j) % RAWS)
                            hidden(RAWS * i + j, j)
                    for f in range(NF // RAWS * RAWS, NF):
                        lo_static(dve, C_UP + 1 + f)
                        hidden(f, f)
                    dve.sem_inc(S["x_dense"], 2)
                    with V.Fori(0, DOWN_CH // RAWS) as i:
                        for what in (1, 2, 3, "x0", 4, 5, "x1", 6, "x2", "x3"):
                            if isinstance(what, int):
                                at = C_DOWN + what
                                split_lo(dve, at + RAWS * i, at % RAWS)
                            else:
                                j = int(what[1])
                                dve.wait_ge(S["y_turned"], 4 * i + j + 1)
                                for t0, t1, r in ((0, 2, P), (2, 3, NS)):
                                    at = x[0:r, t0:t1, bass.ds((4 * i + j) * P, P)]
                                    last = V.tensor_tensor(at, at, bank[j % 2][0:r, t0 * P:t1 * P]
                                                           .rearrange("p (t d) -> p t d", d=P), ALU.add)
                                last.then_inc(S["x_dense"], 1)

            V.memset(zero[:, :], 0.0)
            V.memset(logits[:, :, :], 0.0)
            V.memset(mask[:, :, :], 0.0)
            V.memset(posm[:, :, :], -FAR)
            dve.wait_ge(late_in, 16)
            link(V.tensor_copy(rt_hi[:, :, :], router))
            V.tensor_tensor(rt_lo[:, :, :], router, rt_hi[:, :, :].bitcast(F), ALU.subtract).then_inc(S["rt_out"], 1)
            for t in range(3):
                r = ROWS[t]
                last = V.tensor_scalar(xm[0:r, t, :], x[0:r, t, :], rstd[0:r, N_FFN, t:t + 1], None, ALU.mult)
            last.then_inc(S["xm_out"], 1)
            dve.wait_ge(S["logit_done"], 1)
            for t in range(3):
                last = V.tensor_copy(logits[0:ROWS[t], t, :], bank[2][0:ROWS[t], t * NE:(t + 1) * NE])
            link(last)
            for t in range(3):
                last = V.max(top[0:ROWS[t], t, :], logits[0:ROWS[t], t, :])
            link(last)
            for t0, t1, r in ((0, 2, P), (2, 3, NS)):
                last = V.tensor_scalar(nfirst[0:r, t0:t1], top[0:r, t0:t1, 0], -1.0, None, ALU.mult)
            last.then_inc(S["logit_out"], 1)
            for t in range(3):
                last = V.memset(top[0:ROWS[t], t, 2:8], -NEVER)
            link(last)
            for t in range(3):
                r = ROWS[t]
                last = V.match_replace(left[0:r, t, :], top[0:r, t, :], logits[0:r, t, :], NEVER)
            link(last)
            for t in range(3):
                r = ROWS[t]
                last = V.tensor_scalar(mask[0:r, t, :], left[0:r, t, :], 0.5 * NEVER, None, ALU.is_le)
            last.then_inc(S["pos_in"], 1)
            dve.wait_ge(S["pos_in"], 1)
            dve.wait_ge(S["exp2_out"], 1)
            for t in range(3):
                r = ROWS[t]
                last = V.tensor_tensor(gate[0:r, t, :], expo[0:r, t, :], mask[0:r, t, :], ALU.mult)
            link(last)
            for t in range(3):
                r = ROWS[t]
                last = V.reduce_sum(gden[0:r, t:t + 1], gate[0:r, t, :], AX.X)
            link(last)
            for t in range(3):
                r = ROWS[t]
                last = V.reciprocal(gden[0:r, t:t + 1], gden[0:r, t:t + 1])
            link(last)
            for t in range(3):
                r = ROWS[t]
                last = V.tensor_scalar(gate[0:r, t, :], gate[0:r, t, :], gden[0:r, t:t + 1], None, ALU.mult)
            link(last)
            for t in range(3):
                r = ROWS[t]
                last = V.tensor_scalar(posm[0:r, t, :], mask[0:r, t, :], FAR, -FAR, ALU.mult, ALU.add)
            link(last)
            dve.wait_ge(S["pos_done"], 1)
            for t in range(3):
                r = ROWS[t]
                last = V.tensor_tensor(posm[0:r, t, :], posm[0:r, t, :], bank[3][0:r, t * NE:(t + 1) * NE], ALU.add)
            link(last)
            link(V.reduce_max(cmax[:, :], bank[3][0:1, 3 * NE:4 * NE], AX.X))
            V.tensor_scalar(over[:, 0:1], cmax[:, :], float(P), 1.0, ALU.is_gt, ALU.add)
            link(V.tensor_scalar(over[:, 1:2], cmax[:, :], float(2 * P), None, ALU.is_gt))
            V.tensor_tensor(rounds[:, :], over[:, 0:1], over[:, 1:2], ALU.add).then_inc(S["rounds_ok"], 1)
            dve.sem_inc(S["eh_out"], 2)
            dve.sem_inc(S["y_out"], 1)
            dve.sem_inc(S["x_added"], 6)
            dve.wait_ge(S["rounds_ok"], 1)
            n_rounds = V.value_load(rounds[0:1, 0:1], min_val=1, max_val=MAX_ROUNDS)
            with V.Fori(0, n_rounds) as r:
                with V.Fori(0, NE) as e:
                    q = V.snap(r * NE + e)
                    cb = V.snap(q * EXP_CH + C_MOE)
                    g0 = V.snap(q * STEPS)

                    def lo(off, extra=0):
                        split_lo(dve, cb + off + RAWS * extra, off % RAWS)

                    def step_hidden(s, extra=0):
                        dve.wait_ge(S["esilu"], g0 + s + 1 + 2 * extra)
                        V.tensor_tensor(eh[:, s % 2, :], esg[:, s % 2, :], bank[2 + s % 2][:, 256:512], ALU.mult)\
                            .then_inc(S["eh_out"], 1)

                    def step_turn(s, extra=0):
                        dve.wait_ge(S["eT_hi_out"], g0 + s + 1 + 2 * extra)
                        V.tensor_tensor(eT_lo[:, s % 2, :, :].rearrange("p a b -> p (a b)"), bank[4 + s % 2][:, 0:256],
                                        eT_hi[:, s % 2, :, :].rearrange("p a b -> p (a b)").bitcast(F), ALU.subtract)\
                            .then_inc(S["eT_out"], 1)

                    for t in range(3):
                        rr = ROWS[t]
                        last = V.tensor_scalar(sel[0:rr, t, :], slots[0:rr, :], posm[0:rr, t, bass.ds(e, 1)], None,
                                               ALU.is_equal)
                    last.then_inc(S["sel_out"], 1)
                    for off in (0, 1, 2):
                        lo(off)
                    for k in range(KD):
                        if k % 4 == 0:
                            dve.wait_ge(S["gat_hi"], KD * q + k + 4)
                        V.scalar_tensor_tensor(out=gT_lo[:, k, :], in0=bank[k // 4][:, (k % 4) * P:(k % 4 + 1) * P],
                                               scalar=gains[:, 1, G_FFN, k:k + 1], in1=gT_hi[:, k, :].bitcast(F),
                                               op0=ALU.mult, op1=ALU.subtract).then_inc(S["gat_lo"], 1)
                    dve.wait_ge(S["selT_done"], q + 1)
                    V.tensor_copy(selT[:, :], bank[5][:, 0:NT]).then_inc(S["selT_out"], 1)
                    lo(3)
                    with V.Fori(0, STEPS // 2 - 1) as p:
                        for s in (0, 1):
                            step_hidden(s, p)
                            lo(3 * s + 4, p)
                            step_turn(s, p)
                            lo(3 * s + 5, p)
                            lo(3 * s + 6, p)
                    for s in (STEPS - 2, STEPS - 1):
                        step_hidden(s)
                        lo(EXP_CH - STEPS + s)
                        step_turn(s)
                    for n in range(2):
                        dve.wait_ge(S["y_hi_out"], 2 * q + n + 1)
                        last = V.tensor_tensor(y_lo[:, n * 512:(n + 1) * 512], bank[6 + n][:, :],
                                               y_hi[:, n * 512:(n + 1) * 512].bitcast(F), ALU.subtract)
                    last.then_inc(S["y_out"], 1)
                    dve.wait_ge(S["x_added"], 6 * q + 6)
                    for m in range(6):
                        t, n = m // 2, m % 2
                        rr = ROWS[t]
                        dve.wait_ge(S["scat_done"], 6 * q + m + 1)
                        at = x[0:rr, t, n * 512:(n + 1) * 512]
                        V.scalar_tensor_tensor(out=at, in0=bank[n][0:rr, :], scalar=gate[0:rr, t, bass.ds(e, 1)], in1=at,
                                               op0=ALU.mult, op1=ALU.add).then_inc(S["x_added"], 1)
                V.tensor_scalar(posm[:, :, :], posm[:, :, :], -float(P), None, ALU.add).then_inc(S["pos_moved"], 1)
                dve.wait_ge(S["pos_moved"], r + 1)
            dve.wait_ge(rstd_ok, NORMS * DEPTH + 1)
            dve.wait_ge(gfin_in, 16)
            for t in range(3):
                rr = ROWS[t]
                last = V.scalar_tensor_tensor(out=xm[0:rr, t, :], in0=x[0:rr, t, :], scalar=rstd[0:rr, 0, t:t + 1],
                                              in1=gfin[0:rr, :], op0=ALU.mult, op1=ALU.mult)
            last.then_inc(S["fin_out"], 1)

        @block.tensor
        def _(pe):
            T = nc.tensor

            def arrived(c):
                pe.wait_ge(lo_ready, c + 1)

            def turn(l, which, tiles=(0, 1, 2)):
                u = use(l, which)
                pe.wait_ge(rows_ok, u + 1)
                if u:
                    pe.wait_ge(turned_lo, KD * u)
                for k in range(KD):
                    if k >= 2:
                        pe.wait_ge(turned_lo, KD * u + k - 1)
                    for t in tiles:
                        r = ROWS[t]
                        last = T.transpose(bank[k % 2][:, t * P:t * P + r], xn[0:r, t, k * P:(k + 1) * P],
                                           ident[0:r, 0:r])
                    last.then_inc(turned, 1)

            def rows_times(c, b, n_blocks, k, banks, first, last_k):
                out = []
                for t in range(3):
                    r = ROWS[t]
                    out.append(mm3(bank[banks + t][0:r, 0:n_blocks * P], hT_hi[:, k, t * P:t * P + r],
                                   hT_lo[:, k, t * P:t * P + r], blk(whi, c, b, n_blocks), blk(wlo, c, b, n_blocks),
                                   first, last_k))
                return out

            pe.wait_ge(const_in, 16)
            for l in range(DEPTH):
                c0 = l * C_MIX1
                if l:
                    pe.wait_ge(S["x_dense"], KD + 2)
                turn(l, G_MEM, (0, 1))
                pe.wait_ge(turned_lo, KD * (use(l, G_MEM) + 1))
                for c in (0, 1):
                    arrived(c0 + c)
                    for k in range(4):
                        for t in range(2):
                            m = mm3(bank[2 + t][:, :], hT_hi[:, 4 * c + k, t * P:(t + 1) * P],
                                    hT_lo[:, 4 * c + k, t * P:(t + 1) * P], blk(whi, c0 + c, 4 * k, 4),
                                    blk(wlo, c0 + c, 4 * k, 4), c == 0 and k == 0, c == 1 and k == 3)
                    m.then_inc(chunk_used, 1)
                turn(l, G_MIX)
                pe.wait_ge(turned_lo, KD * (use(l, G_MIX) + 1))
                arrived(c0 + 2)
                for k in range(KD):
                    for f in range(2):
                        m = mm3(bank[4 + f][:, 0:NT], blk(whi, c0 + 2, 2 * k + f), blk(wlo, c0 + 2, 2 * k + f),
                                hT_hi[:, k, :], hT_lo[:, k, :], k == 0, k == KD - 1)
                m.then_inc(chunk_used, 1)
                pe.wait_ge(S["kv_out"], l + 1)
                for f in range(2):
                    for t in range(2):
                        last = T.transpose(bank[2][:, f * 256 + t * P:f * 256 + (t + 1) * P], kv[:, t, f * P:(f + 1) * P],
                                           ident)
                last.then_inc(S["kT_done"], 1)
                pe.wait_ge(S["q_out"], l + 1)
                pe.wait_ge(S["kT_out"], l + 1)
                for t in range(2):
                    for f in range(2):
                        for p in range(2):
                            m = T.matmul(bank[4 + 2 * t + p][:, f * NMEM:(f + 1) * NMEM],
                                         qT[HD * p:HD * p + HD, f, t * P:(t + 1) * P], kT[HD * p:HD * p + HD, f, :],
                                         start=True, stop=True)
                            if f == 1:
                                m.then_inc(S["sc_done"], 1)
                for c in (0, 1):
                    arrived(c0 + 3 + c)
                    for b in range(4):
                        for mt in range(2):
                            at = mt * P + (4 * c + b) * HEADS * REQT
                            for f in range(2):
                                rhs = [q_[:, f, 4 * c + b, :, :].rearrange("p h t -> p (h t)") for q_ in (qs_hi, qs_lo)]
                                m = mm3(bank[3][:, at:at + HEADS * REQT], blk(whi, c0 + 3 + c, 4 * b + 2 * f + mt),
                                        blk(wlo, c0 + 3 + c, 4 * b + 2 * f + mt), rhs[0], rhs[1], f == 0, f == 1)
                    m.then_inc(chunk_used, 1)
                arrived(c0 + 5)
                for k in range(5):
                    m = rows_times(c0 + 5, 3 * k, 3, k, 0, k == 0, False)[-1]
                m.then_inc(chunk_used, 1)
                arrived(c0 + 6)
                for k in (5, 6, 7):
                    ms_ = rows_times(c0 + 6, 3 * (k - 5), 3, k, 0, False, k == 7)
                for m in ms_:
                    m.then_inc(S["v_done"], 1)
                pe.wait_ge(S["ssc_out"], l + 1)
                for mt in range(2):
                    last = T.transpose(bank[3][:, 256 + mt * P:256 + (mt + 1) * P], sST[:, mt, :], ident)
                last.then_inc(S["sscT_done"], 1)
                pe.wait_ge(S["exp_done"], 4 * l + 4)
                for k in (0, 1):
                    m = rows_times(c0 + 6, 9 + 3 * k, 3, k, 4, k == 0, False)[-1]
                m.then_inc(chunk_used, 1)
                arrived(c0 + 7)
                for k in range(2, 7):
                    m = rows_times(c0 + 7, 3 * (k - 2), 3, k, 4, False, False)[-1]
                m.then_inc(chunk_used, 1)
                arrived(c0 + 8)
                for m in rows_times(c0 + 8, 0, 3, 7, 4, False, True):
                    m.then_inc(S["xb_done"], 1)
                pe.wait_ge(S["vg_out"], l + 1)
                for k in range(4):
                    m = rows_times(c0 + 8, 3 + 3 * k, 3, k, 0, k == 0, False)[-1]
                m.then_inc(chunk_used, 1)
                arrived(c0 + 9)
                for k in range(4, 8):
                    m = rows_times(c0 + 9, 3 * (k - 4), 3, k, 0, False, k == 7)[-1]
                m.then_inc(chunk_used, 1)

                def turn_probs(i):
                    if i == 1:
                        pe.wait_ge(S["sexp_done"], l + 1)
                    if i >= 2:
                        pe.wait_ge(S["PT_out"], 4 * l + i - 1)
                    for f in range(2):
                        for mt in range(2):
                            last = T.transpose(bank[(7, 3)[i % 2]][:, (2 * f + mt) * P:(2 * f + mt + 1) * P],
                                               prob[:, 2 * i + f, mt * P:(mt + 1) * P], ident)
                    last.then_inc(S["PT_done"], 1)

                def attend(i):
                    t, p = i // 2, i % 2
                    pe.wait_ge(S["PT_out"], 4 * l + i + 1)
                    for f in range(2):
                        h = 2 * f + p
                        for mt in range(2):
                            last = T.matmul(bank[4][:, t * DX + h * HD:t * DX + (h + 1) * HD], PT[:, i % 2, 2 * f + mt, :],
                                            kv[:, mt, DX + h * HD:DX + (h + 1) * HD], start=mt == 0, stop=mt == 1)
                    last.then_inc(S["o_done"], 1)

                turn_probs(0)
                turn_probs(1)
                pe.wait_ge(S["xb_out"], l + 1)
                attend(0)
                turn_probs(2)
                attend(1)
                turn_probs(3)
                pe.wait_ge(S["sprob_out"], l + 1)
                for mt in range(2):
                    last = T.transpose(bank[5][:, mt * P:(mt + 1) * P], sP[:, mt * P:(mt + 1) * P], ident)
                last.then_inc(S["sPT_done"], 1)
                attend(2)
                attend(3)
                pe.wait_ge(S["sPT_out"], l + 1)
                for c in (0, 1):
                    arrived(c0 + 10 + c)
                    for b in range(4):
                        for f in range(2):
                            at = f * P + (4 * c + b) * HEADS * REQT
                            cols = slice((4 * c + b) * HEADS * REQT, (4 * c + b + 1) * HEADS * REQT)
                            for mt in range(2):
                                m = mm3(bank[6][:, at:at + HEADS * REQT], blk(whi, c0 + 10 + c, 4 * b + 2 * mt + f),
                                        blk(wlo, c0 + 10 + c, 4 * b + 2 * mt + f), sPT_hi[:, mt, cols], sPT_lo[:, mt, cols],
                                        mt == 0, mt == 1)
                    m.then_inc(chunk_used, 1)
                pe.wait_ge(S["osT_out"], l + 1)
                for f in range(2):
                    last = T.transpose(bank[7][0:NS, f * P:(f + 1) * P], osT[:, f, :], ident)
                last.then_inc(S["os_done"], 1)
                pe.wait_ge(S["ug_out"], l + 1)
                pe.wait_ge(state_in, 16 * (l + 1))
                for g in range(4):
                    ch = slice(g * GD, (g + 1) * GD)
                    T.matmul(bank[g][0:GD, 0:SEQ], xb[:, 0, ch], pool0[:, g, :], start=True, stop=False)
                    T.matmul(bank[g][0:GD, P:SEQ], xb[:, 1, ch], pool1[:, g, :], start=False, stop=True)
                    T.matmul(bank[g][0:GD, SEQ:NT], xb[0:NS, 2, ch], pool_s[:, g, :], start=True, stop=False)
                    T.matmul(bank[g][0:GD, SEQ:NT], state[:, ch], pool_st[:, g, :], start=False, stop=True)\
                        .then_inc(S["dT_done"], 1)
                pe.wait_ge(masked, 1)
                pe.wait_ge(S["v_out"], l + 1)
                pe.wait_ge(S["o_out"], l + 1)
                for t in range(3):
                    r = ROWS[t]
                    w = w_sp if t < 2 else w_sps
                    for h in range(AH):
                        last = T.matmul(bank[4 + t][0:r, h * AHD:(h + 1) * AHD], w[:, l, h, :],
                                        vg[0:r, t, h * AHD:(h + 1) * AHD], start=True, stop=True)
                    last.then_inc(S["mix_done"], 1)
                pe.wait_ge(S["dT_out"], l + 1)
                for t in range(3):
                    r = ROWS[t]
                    for g in range(4):
                        last = T.matmul(bank[t][0:r, g * GD:(g + 1) * GD], dT[0:GD, g, t * P:t * P + r], w_pool[:, l, g, :],
                                        start=True, stop=True)
                    last.then_inc(S["y_done"], 1)
                turn(l, G_GROUP)
                pe.wait_ge(turned_lo, KD * (use(l, G_GROUP) + 1))
                for n in range(2):
                    for c in range(2):
                        arrived(c0 + 12 + 2 * n + c)
                        for k in range(4):
                            m = rows_times(c0 + 12 + 2 * n + c, 4 * k, 4, 4 * c + k, 2 + 3 * n, c == 0 and k == 0,
                                           c == 1 and k == 3)[-1]
                        m.then_inc(chunk_used, 1)
                turn(l, G_FFN)
                pe.wait_ge(turned_lo, KD * (use(l, G_FFN) + 1))

                if l == 0:
                    def up(f, j):
                        arrived(C_UP + f)
                        pe.wait_ge(S["H_out"], f + 1)
                        for k in range(KD):
                            for w in range(2):
                                m = mm3(bank[2 + 2 * (j % 2) + w][:, 0:NT], blk(whi, C_UP + j, 2 * k + w),
                                        blk(wlo, C_UP + j, 2 * k + w), hT_hi[:, k, :], hT_lo[:, k, :], k == 0, k == KD - 1)
                        m.then_inc(chunk_used, 1)
                    with T.Fori(0, NF // RAWS) as i:
                        for j in range(RAWS):
                            up(RAWS * i + j, j)
                    for f in range(NF // RAWS * RAWS, NF):
                        up(f, f)
                    pe.wait_ge(S["H_out"], NF + 2)

                    def down(i, j):
                        pe.wait_ge(S["yT_out"], 4 * i + j + 1)
                        for f in range(NF):
                            b = DOWN_BLOCKS * j + f
                            if b % 16 == 0 or f == 0:
                                arrived(C_DOWN + RAWS * i + b // 16)
                            m = mm3(bank[6 + j % 2][:, 0:NT], blk(whi, C_DOWN + b // 16, b % 16),
                                    blk(wlo, C_DOWN + b // 16, b % 16), HT_hi[:, f, :], HT_lo[:, f, :], f == 0, f == NF - 1)
                            if b % 16 == 15 or (f == NF - 1 and j % 2):
                                m.then_inc(chunk_used, 1)
                        if j % 2 == 0:
                            m.then_inc(S["yT_done"], 1)

                    def turn_back(i, j):
                        pe.wait_ge(S["yT_out"], 4 * i + j + 3)
                        pe.wait_ge(S["x_dense"], 4 * i + j + 1)
                        for t in range(3):
                            r = ROWS[t]
                            last = T.transpose(bank[j % 2][0:r, t * P:(t + 1) * P], yT[:, j % 2, t * P:t * P + r], ident)
                        last.then_inc(S["y_turned"], 1)
                    with T.Fori(0, DOWN_CH // RAWS) as i:
                        down(i, 0)
                        down(i, 1)
                        turn_back(i, 0)
                        down(i, 2)
                        turn_back(i, 1)
                        down(i, 3)
                        turn_back(i, 2)
                        turn_back(i, 3)

            pe.wait_ge(S["rt_out"], 1)
            for t in range(3):
                r = ROWS[t]
                at = bank[2][0:r, t * NE:(t + 1) * NE]
                for k in range(KD):
                    hi_, lo_ = hT_hi[:, k, t * P:t * P + r], hT_lo[:, k, t * P:t * P + r]
                    mm3(at, hi_, lo_, rt_hi[:, k, :], rt_lo[:, k, :], k == 0, False)
                    last = T.matmul(at, lo_, rt_lo[:, k, :], start=False, stop=k == KD - 1)
            last.then_inc(S["logit_done"], 1)
            pe.wait_ge(S["pos_in"], 1)
            for t in range(3):
                r = ROWS[t]
                for s_ in range(t):
                    T.matmul(bank[3][0:r, t * NE:(t + 1) * NE], ones[:, 0:r], mask[:, s_, :], start=s_ == 0, stop=False)
                T.matmul(bank[3][0:r, t * NE:(t + 1) * NE], before[0:r, 0:r], mask[0:r, t, :], start=t == 0, stop=True)
            for t in range(3):
                r = ROWS[t]
                last = T.matmul(bank[3][0:1, 3 * NE:4 * NE], ones[0:r, 0:1], mask[0:r, t, :], start=t == 0, stop=t == 2)
            last.then_inc(S["pos_done"], 1)

            pe.wait_ge(S["rounds_ok"], 1)
            pe.wait_ge(S["xm_out"], 1)
            n_rounds = T.value_load(rounds[0:1, 0:1], min_val=1, max_val=MAX_ROUNDS)
            with T.Fori(0, n_rounds) as r_:
                with T.Fori(0, NE) as e:
                    q = T.snap(r_ * NE + e)
                    cb = T.snap(q * EXP_CH + C_MOE)
                    g0 = T.snap(q * STEPS)

                    def gate_up(off, s, half_, extra=0):
                        pe.wait_ge(lo_ready, cb + off + 1 + RAWS * extra)
                        for k in range(4):
                            kk = 4 * half_ + k
                            m = mm3(bank[2 + s % 2][:, :], gT_hi[:, kk, :], gT_lo[:, kk, :], blk(whi, off, 4 * k, 4),
                                    blk(wlo, off, 4 * k, 4), kk == 0, kk == KD - 1)
                        m.then_inc(chunk_used, 1)

                    def turn_hidden(s, extra=0):
                        pe.wait_ge(S["eh_out"], g0 + s + 3 + 2 * extra)
                        for b in range(2):
                            last = T.transpose(bank[4 + s % 2][:, b * P:(b + 1) * P], eh[:, s % 2, b * P:(b + 1) * P], ident)
                        last.then_inc(S["eT_done"], 1)

                    def down_step(off, s, extra=0):
                        pe.wait_ge(lo_ready, cb + off + 1 + RAWS * extra)
                        pe.wait_ge(S["eT_out"], g0 + s + 1 + 2 * extra)
                        for b in range(2):
                            for n in range(2):
                                m = mm3(bank[6 + n][:, :], eT_hi[:, s % 2, b, :], eT_lo[:, s % 2, b, :],
                                        blk(whi, off, 8 * b + 4 * n, 4), blk(wlo, off, 8 * b + 4 * n, 4), False, False,
                                        skip_group_check=True)
                        m.then_inc(chunk_used, 1)

                    pe.wait_ge(S["sel_out"], q + 1)
                    pe.wait_ge(S["x_added"], 6 * q + 6)
                    for k in range(KD):
                        for t in range(3):
                            r = ROWS[t]
                            last = T.matmul(bank[k // 4][:, (k % 4) * P:(k % 4 + 1) * P], xm[0:r, t, k * P:(k + 1) * P],
                                            sel[0:r, t, :], start=t == 0, stop=t == 2)
                        if k % 4 == 3:
                            last.then_inc(S["gat_done"], 1)
                    for t in range(3):
                        r = ROWS[t]
                        last = T.transpose(bank[5][:, t * P:t * P + r], sel[0:r, t, :], ident[0:r, 0:r])
                    last.then_inc(S["selT_done"], 1)
                    pe.wait_ge(S["y_out"], q + 1)
                    for n in range(2):
                        T.matmul(bank[6 + n][:, :], zero[:, 0:P], zero[:, :], start=True, stop=True)
                    pe.wait_ge(S["gat_lo"], KD * q + KD)
                    gate_up(0, 0, 0)
                    gate_up(1, 0, 1)
                    with T.Fori(0, STEPS // 2 - 1) as p:
                        for s in (0, 1):
                            gate_up(3 * s + 2, s + 1, 0, p)
                            turn_hidden(s, p)
                            gate_up(3 * s + 3, s + 1, 1, p)
                            down_step(3 * s + 4, s, p)
                    s = STEPS - 2
                    gate_up(3 * s + 2, s + 1, 0)
                    turn_hidden(s)
                    gate_up(3 * s + 3, s + 1, 1)
                    down_step(3 * s + 4, s)
                    turn_hidden(s + 1)
                    down_step(EXP_CH - 1, s + 1)
                    pe.wait_ge(S["y_out"], q + 2)
                    pe.wait_ge(S["selT_out"], q + 1)
                    for m_ in range(6):
                        t, n = m_ // 2, m_ % 2
                        r = ROWS[t]
                        pe.wait_ge(S["x_added"], 6 * q + m_ + 5)
                        T.matmul(bank[n][0:r, :], selT[:, t * P:t * P + r], y_hi[:, n * 512:(n + 1) * 512], start=True, stop=False)
                        T.matmul(bank[n][0:r, :], selT[:, t * P:t * P + r], y_lo[:, n * 512:(n + 1) * 512], start=False, stop=True)\
                            .then_inc(S["scat_done"], 1)


def _pool_tables():
    full = np.zeros((4, SEQ, SEQ), np.float32)
    req = np.zeros((4, PBUF + REQT, REQT), np.float32)
    for g, w in enumerate(WINDOWS):
        for t in range(SEQ):
            first = max(0, t - w + 1)
            full[g, first:t + 1, t] = 1.0 / (t + 1 - first)
            full[g, t, t] -= 1.0
        for t in range(REQT):
            req[g, PBUF + t - w + 1:PBUF + t + 1, t] = 1.0 / w
            req[g, PBUF + t, t] -= 1.0
    own = np.zeros((4, NS, NS), np.float32)
    old = np.zeros((4, NREQ * PBUF, NS), np.float32)
    for b in range(NREQ):
        own[:, b * REQT:(b + 1) * REQT, b * REQT:(b + 1) * REQT] = req[:, PBUF:]
        old[:, b * PBUF:(b + 1) * PBUF, b * REQT:(b + 1) * REQT] = req[:, :PBUF]
    return full, own, old


def _constants(v):
    table = np.zeros((P, N_CONST), np.float32)

    def put(name, a):
        a = np.asarray(a).reshape(a.shape[0], -1)
        lo, hi = COL[name]
        assert a.shape[1] == hi - lo, name
        table[:a.shape[0], lo:hi] = a

    put("ident", np.eye(P, dtype=np.float32))
    g = np.stack([v["g_mem"], v["g_mix_norm"], v["g_group"], v["g_ffn_norm"]], 1)
    put("gains", g.reshape(DEPTH, 4, KD, P).transpose(3, 0, 1, 2))
    full, own, old = _pool_tables()
    put("pool0", full[:, 0:P].transpose(1, 0, 2))
    put("pool1", full[:, P:, P:].transpose(1, 0, 2))
    put("pool_s", own.transpose(1, 0, 2))
    put("pool_st", old.transpose(1, 0, 2))
    bias = np.zeros((P, DEPTH, 2, AH), np.float32)
    bias[:, :, 0] = v["b_spatial"].transpose(2, 0, 1)
    bias[:NS, :, 1] = np.tile(v["b_spatial"][:, :, :REQT].transpose(2, 0, 1), (NREQ, 1, 1))
    put("bias", bias)
    put("w_pool", v["w_pool"].transpose(2, 0, 1, 3))
    put("w_sp", v["w_spatial"].transpose(3, 0, 1, 2))
    small = np.zeros((NS, DEPTH, AH, NS), np.float32)
    for b in range(NREQ):
        at = slice(b * REQT, (b + 1) * REQT)
        small[at, :, :, at] = v["w_spatial"][:, :, :REQT, :REQT].transpose(3, 0, 1, 2)
    put("w_sps", small)
    put("g_v", np.tile(v["g_v"].reshape(1, -1), (P, 1)))
    put("s_pool", np.tile(v["s_pool"].reshape(1, -1), (P, 1)))
    return table


def _late(v):
    router = v["w_router"][0].reshape(KD, P, NE).transpose(1, 0, 2).reshape(P, KD * NE)
    return np.concatenate([np.triu(np.ones((P, P), np.float32), 1), np.ones((P, P), np.float32),
                           np.tile(np.arange(P, dtype=np.float32), (P, 1)), router], axis=1)


def _stream(v):
    out = np.zeros((N_CH, P, CW), np.float32)
    n = 0

    def put(a):
        nonlocal n
        out[n:n + len(a), :, :a.shape[2]] = a
        n += len(a)

    def columns4(w):
        m = w.shape[1] // 512
        return w.reshape(2, 4, P, m, 512).transpose(3, 0, 2, 1, 4).reshape(2 * m, P, CW)

    for l in range(DEPTH):
        put(columns4(v["w_mem_kv"][l]))
        w = v["w_in"][l].reshape(KD, P, -1)
        put(w[:, :, 2 * DA + DB:].transpose(1, 0, 2).reshape(1, P, CW))
        put(v["cache_mem_k"][l].reshape(2, 4, NMEM, 2, P).transpose(0, 4, 1, 3, 2).reshape(2, P, CW))
        rows = np.concatenate([w[:, :, DA:2 * DA], w[:, :, 2 * DA:2 * DA + DB], w[:, :, 0:DA]])
        for a, b in ((0, 5), (5, 10), (10, 15), (15, 20), (20, 24)):
            put(rows[a:b].transpose(1, 0, 2).reshape(1, P, -1))
        put(v["cache_mem_v"][l].reshape(2, 4, 2, P, DX).transpose(0, 3, 1, 2, 4).reshape(2, P, CW))
        put(columns4(v["w_out"][l]))
        if l == 0:
            gu = np.stack([v["w_dense_gate"][0], v["w_dense_up"][0]]).reshape(2, KD, P, NF, P)
            put(gu.transpose(3, 2, 1, 0, 4).reshape(NF, P, CW))
            d = np.zeros((KD, DOWN_BLOCKS, P, P), np.float32)
            d[:, :NF] = v["w_dense_down"][0].reshape(NF, P, KD, P).transpose(2, 0, 1, 3)
            put(d.reshape(DOWN_CH, 16, P, P).transpose(0, 2, 1, 3).reshape(DOWN_CH, P, CW))
    assert n == C_MOE
    for e in range(NE):
        gu = np.stack([v["w_moe_gate"][0, e], v["w_moe_up"][0, e]])
        gu = gu.reshape(2, 2, 4, P, STEPS, 256).transpose(4, 1, 3, 2, 0, 5).reshape(STEPS, 2, P, CW)
        dn = v["w_moe_down"][0, e].reshape(STEPS, 2, P, D).transpose(0, 2, 1, 3).reshape(STEPS, 1, P, CW)
        put(gu[0])
        for s in range(STEPS - 1):
            put(gu[s + 1])
            put(dn[s])
        put(dn[STEPS - 1])
    assert n == N_CH
    return out.reshape(N_CH * P, CW)


def kernel(**inputs):
    import concourse.bacc as bacc
    from concourse.bass_utils import run_bass_kernel_spmd

    v = {k: np.asarray(a) for k, a in inputs.items()}
    arrays = {
        "stream": _stream(v),
        "const": _constants(v),
        "late": _late(v),
        "mem": v["mem_prompt"].reshape(NMEM, D),
        "x_prompt": v["x_prompt"].reshape(SEQ, D),
        "x_sample": v["x_sample"].reshape(NS, D),
        "state": v["state_pool"].reshape(DEPTH, NREQ * PBUF, DB),
        "g_final": np.tile(v["g_final"].reshape(1, D), (P, 1)),
    }
    outs = {
        "y_prompt": (SEQ, D), "y_sample": (NS, D), "pool_prompt": (DEPTH, PBUF, DB), "mem_k": (DEPTH, NMEM, DX),
        "mem_v": (DEPTH, NMEM, DX), "pool_sample": (DEPTH, NREQ, PBUF, DB), "v_rows": (DEPTH, NS, DA),
    }
    nc = bacc.Bacc("TRN2", target_bir_lowering=False, num_devices=1)
    io = {}
    for name, a in arrays.items():
        arrays[name] = np.ascontiguousarray(a)
        io[name] = nc.dram_tensor(f"in_{name}", a.shape, mybir.dt.float32, kind="ExternalInput").ap()
    for name, shape in outs.items():
        io[name] = nc.dram_tensor(f"out_{name}", shape, mybir.dt.float32, kind="ExternalOutput").ap()
    build(nc, io)
    r = run_bass_kernel_spmd(nc, [{f"in_{name}": a for name, a in arrays.items()}], core_ids=[0]).results[0]
    return (
        r["out_y_prompt"].reshape(1, SEQ, D), r["out_y_sample"].reshape(NREQ, REQT, D), r["out_pool_prompt"].reshape(DEPTH, 1, PBUF, DB),
        r["out_mem_k"].reshape(DEPTH, 1, NMEM, HEADS, HD), r["out_mem_v"].reshape(DEPTH, 1, NMEM, HEADS, HD), r["out_pool_sample"],
        r["out_v_rows"].reshape(DEPTH, NREQ, REQT, DA),
    )
```

```python
from contextlib import ExitStack

import concourse.bass as bass
import concourse.mybir as mybir
import numpy as np

D, SEQ, DEPTH, NREQ, REQT = 1024, 256, 2, 8, 4
DA = DB = 384
DX, HEADS, HD, NMEM = 256, 4, 64, 256
AH, AHD = 4, 96
WINDOWS, GD, PBUF = (2, 4, 8, 16), 96, 15
FF, NE, FFE = 2816, 8, 3584
EPS = 1e-6
P = 128
KD = D // P
NS = NREQ * REQT
NT = SEQ + NS
ROWS = (P, P, NS)
CW = 2048

RAWS, SPL = 6, 3
KV_CH, Q_CH, CK_CH, UV_CH, CV_CH, WO_CH = 2, 1, 2, 5, 2, 4
MIX_CH = KV_CH + Q_CH + CK_CH + UV_CH + CV_CH + WO_CH
NF = FF // P
UP_CH = NF
DOWN_BLOCKS = 24
DOWN_CH = KD * DOWN_BLOCKS // 16
C_UP = MIX_CH
C_DOWN = C_UP + UP_CH
C_MIX1 = C_DOWN + DOWN_CH
C_MOE = C_MIX1 + MIX_CH
STEPS = FFE // 256
EXP_CH = 3 * STEPS
ROUND_CH = NE * EXP_CH
N_CH = C_MOE + ROUND_CH
DIAG = P + HEADS * REQT
MAX_ROUNDS = -(-NT // P)
FAR = 8192.0
NEVER = -3.0e38
NORMS = 5
N_MEM, N_MIX, N_V, N_GROUP, N_FFN = range(NORMS)
LAYER_STORES = 6

def _columns():
    at, n = {}, 0
    for name, width in (("ident", P), ("gains", DEPTH * 4 * KD),
                        ("pool0", 4 * SEQ), ("pool1", 4 * P), ("pool_s", 4 * NS), ("pool_st", 4 * NS),
                        ("bias", DEPTH * 2 * AH), ("fold", HEADS * NS), ("w_pool", DEPTH * 4 * GD),
                        ("w_sp", DEPTH * AH * P), ("w_sps", DEPTH * AH * NS),
                        ("g_v", DEPTH * DA), ("s_pool", DEPTH * DB)):
        at[name] = (n, n + width)
        n += width
    return at, n


COL, N_CONST = _columns()
N_LATE = 3 * P + KD * NE
G_MEM, G_MIX, G_GROUP, G_FFN = range(4)


def build(nc, io):
    F, FR, I32 = mybir.dt.float32, mybir.dt.float32r, mybir.dt.int32
    ACT, ALU, AX = mybir.ActivationFunctionType, mybir.AluOpType, mybir.AxisListType
    ctx = ExitStack()
    with ctx:
        sb = lambda n, s, d=F: ctx.enter_context(nc.sbuf_tensor(n, s, d))
        sem = lambda n: ctx.enter_context(nc.semaphore(n))

        raw = sb("raw", [P, RAWS, CW])
        whi = sb("whi", [P, SPL, CW], FR)
        wlo = sb("wlo", [P, SPL, CW], FR)
        x = sb("x", [P, 3, D])
        hT_hi = sb("hT_hi", [P, KD, NT], FR)
        hT_lo = sb("hT_lo", [P, KD, NT], FR)
        const = sb("const", [P, N_CONST])
        ss = sb("ss", [P, NORMS, 9])
        ms = sb("ms", [P, NORMS, 9])
        rstd = sb("rstd", [P, NORMS, 9])
        half = sb("half", [P, 9])
        junk = sb("junk", [P, D], mybir.dt.bfloat16)

        def phase():
            return ExitStack()

        with phase() as room:
            ph = lambda n, s, d=F: room.enter_context(nc.sbuf_tensor(n, s, d))
            xn = ph("xn", [P, 3, D])
            stage = ph("stage", [P, 6, DA])
            kv = ph("kv", [P, 2, 2 * DX])
            kT = ph("kT", [P, 2, NMEM])
            qT = ph("qT", [P, 2, SEQ])
            state = ph("state", [NREQ * PBUF, DB])
            sP = ph("sP", [P, NMEM])
            mx = ph("mx", [P, 9])
            nmx = ph("nmx", [P, 9])
            den = ph("den", [P, 9])
            rden = ph("rden", [P, 9])
            with phase() as first_half:
                ph = lambda n, s, d=F: first_half.enter_context(nc.sbuf_tensor(n, s, d))
                qs_hi = ph("qs_hi", [P, 2, NREQ * DIAG], FR)
                qs_lo = ph("qs_lo", [P, 2, NREQ * DIAG], FR)
            with phase() as second_half:
                ph = lambda n, s, d=F: second_half.enter_context(nc.sbuf_tensor(n, s, d))
                PT = ph("PT", [P, 2, 4, P])
                xb = ph("xb", [P, 3, DB])
                dT = ph("dT", [P, 4, NT])
                ob = ph("ob", [P, 3, DX])
                os_rows = ph("os_rows", [P, DX])
        qs = [t[:, :, :].rearrange("p f c -> p (f c)") for t in (qs_hi, qs_lo)]
        sPT = [t[:, :, :].rearrange("p k t -> p (k t)") for t in (hT_hi, hT_lo)]
        mem = stage[:, :, :].rearrange("p a b -> p (a b)")[:, 0:2 * D].rearrange("p (t d) -> p t d", t=2)
        b_rows = dT[:, :, :].rearrange("p a b -> p (a b)").rearrange("p (t d) -> p t d", t=3)
        vg, ug = stage[:, 0:3, :], stage[:, 3:6, :]
        prob = xn[:, :, :].rearrange("p a b -> p (a b)")[:, 0:8 * NMEM].rearrange("p (g m) -> p g m", g=8)

        with phase() as room:
            ph = lambda n, s, d=F: room.enter_context(nc.sbuf_tensor(n, s, d))
            HT_hi = ph("HT_hi", [P, NF, NT], FR)
            HT_lo = ph("HT_lo", [P, NF, NT], FR)
            sg = ph("sg", [P, 2, NT])
            hf = ph("hf", [P, 2, NT])
            yT = ph("yT", [P, 2, NT])

        with phase() as room:
            ph = lambda n, s, d=F: room.enter_context(nc.sbuf_tensor(n, s, d))
            xm = ph("xm", [P, 3, D])
            gT_hi = ph("gT_hi", [P, 2, KD, P], FR)
            gT_lo = ph("gT_lo", [P, 2, KD, P], FR)
            sel = ph("sel", [P, 3, P])
            selT = ph("selT", [P, 2, NT], FR)
            esg = ph("esg", [P, 2, 256])
            eh = ph("eh", [P, 2, 256])
            eT_hi = ph("eT_hi", [P, 2, 2, P], FR)
            eT_lo = ph("eT_lo", [P, 2, 2, P], FR)
            y_hi = ph("y_hi", [P, D], FR)
            y_lo = ph("y_lo", [P, D], FR)
            late = ph("late", [P, N_LATE])
            logits = ph("logits", [P, 3, NE])
            top = ph("top", [P, 3, 8])
            nfirst = ph("nfirst", [P, 3])
            left = ph("left", [P, 3, NE])
            mask = ph("mask", [P, 3, NE])
            expo = ph("expo", [P, 3, NE])
            gden = ph("gden", [P, 3])
            gate = ph("gate", [P, 3, NE])
            posm = ph("posm", [P, 3, NE])
            cmax = ph("cmax", [1, 1])
            over = ph("over", [1, 2])
            rounds = ph("rounds", [1, 1], I32)
            rt_hi = ph("rt_hi", [P, KD, NE], FR)
            rt_lo = ph("rt_lo", [P, KD, NE], FR)
            g_rows = ph("g_rows", [P, D])

        bank = [ctx.enter_context(nc.psum_tensor(f"bank{i}", [P, 512], F)) for i in range(8)]

        def C(name, rows=P):
            a, b = COL[name]
            return const[0:rows, a:b]

        ident = C("ident")
        gains = C("gains").rearrange("p (l g k) -> p l g k", l=DEPTH, g=4)
        pool0 = C("pool0").rearrange("p (g t) -> p g t", g=4)
        pool1 = C("pool1").rearrange("p (g t) -> p g t", g=4)
        pool_s = C("pool_s", NS).rearrange("p (g t) -> p g t", g=4)
        pool_st = C("pool_st", NREQ * PBUF).rearrange("p (g t) -> p g t", g=4)
        bias = C("bias").rearrange("p (l s h) -> p l s h", l=DEPTH, s=2)
        fold = C("fold").rearrange("p (h t) -> p h t", h=HEADS)
        before, ones, slots = late[:, 0:P], late[:, P:2 * P], late[:, 2 * P:3 * P]
        router = late[:, 3 * P:].rearrange("p (k e) -> p k e", k=KD)
        w_pool = C("w_pool", GD).rearrange("p (l g d) -> p l g d", l=DEPTH, g=4)
        w_sp = C("w_sp").rearrange("p (l h t) -> p l h t", l=DEPTH, h=AH)
        w_sps = C("w_sps", NS).rearrange("p (l h t) -> p l h t", l=DEPTH, h=AH)
        g_v = C("g_v").rearrange("p (l d) -> p l d", l=DEPTH)
        s_pool = C("s_pool").rearrange("p (l d) -> p l d", l=DEPTH)

        raw_full = [sem(f"raw_full{i}") for i in range(RAWS)]
        hi_ready, lo_ready, chunk_used = sem("hi_ready"), sem("lo_ready"), sem("chunk_used")
        const_in, mem_in, state_in, x_in, gain_in, late_in = (sem(n) for n in ("const_in", "mem_in", "state_in", "x_in", "gain_in", "late_in"))
        preset, masked, zeroed = sem("preset"), sem("masked"), sem("zeroed")
        squares, rstd_ok, rows_ok = sem("squares"), sem("rstd_ok"), sem("rows_ok")
        turned, turned_hi, turned_lo = sem("turned"), sem("turned_hi"), sem("turned_lo")
        act_chain, dve_chain, pool_chain = sem("act_chain"), sem("dve_chain"), sem("pool_chain")
        S = {n: sem(n) for n in (
            "kv_out", "q_out", "kT_done", "kT_out", "sc_done", "max_out", "exp_done", "smax_out",
            "sexp_done", "v_done", "vg_out", "v_out", "xb_done", "xb_out", "PT_done", "PT_out", "sPT_done",
            "sPT_out", "ug_out", "o_done", "os_rows_out", "os_done", "o_out", "dT_done", "dT_out", "mix_done", "a_out",
            "y_done", "b_out", "x_mixed", "silu_out", "hf_out", "H_out", "yT_done", "yT_out", "y_turned", "x_dense",
            "rt_out", "xm_out", "logit_done", "logit_out", "exp2_out", "pos_in", "pos_done", "rounds_ok", "pos_moved", "sel_out",
            "selT_done", "selT_out", "gat_done", "gat_hi", "gat_lo", "esilu", "eh_out", "eT_done", "eT_hi_out", "eT_out",
            "y_hi_out", "y_out", "scat_done", "x_added", "fin_out")}
        stored = sem("stored")

        block = ctx.enter_context(nc.Block())

        def load_chunk(sp, c, slot):
            c, row = c
            if not (isinstance(c, int) and c < RAWS):
                sp.wait_ge(lo_ready, c - RAWS + 1)
            sp.dma_start(raw[:, slot, :], io["stream"][bass.ds(row * P, P), :]).then_inc(raw_full[slot], 16)

        def split_hi(act, c, lap, slot):
            act.wait_ge(raw_full[slot], 16 * lap + 16)
            if not (isinstance(c, int) and c < SPL):
                act.wait_ge(chunk_used, c - SPL + 1)
            nc.scalar.activation(whi[:, slot % SPL, :], raw[:, slot, :], ACT.Copy).then_inc(hi_ready, 1)

        def split_lo(dve, c, slot):
            dve.wait_ge(hi_ready, c + 1)
            nc.vector.tensor_tensor(wlo[:, slot % SPL, :], raw[:, slot, :], whi[:, slot % SPL, :].bitcast(F),
                                    ALU.subtract).then_inc(lo_ready, 1)

        def hi_static(act, *cs):
            for c in cs:
                split_hi(act, c, c // RAWS, c % RAWS)

        def lo_static(dve, *cs):
            for c in cs:
                split_lo(dve, c, c % RAWS)

        def mm3(out, a_hi, a_lo, b_hi, b_lo, start, stop, **kw):
            nc.tensor.matmul(out, a_hi, b_hi, start=start, stop=False, **kw)
            nc.tensor.matmul(out, a_hi, b_lo, start=False, stop=False, **kw)
            return nc.tensor.matmul(out, a_lo, b_hi, start=False, stop=stop, **kw)

        def blk(ring, slot, b, n=1):
            return ring[:, slot % SPL, b * P:(b + n) * P]

        def own_columns(z):
            return z.rearrange("p (f b c) -> p f b c", f=2, c=DIAG)[:, :, :, 0:HEADS * REQT]

        def only(z, f, r):
            return z[:, f * NREQ * DIAG + r * P:f * NREQ * DIAG + (r + 1) * P]

        def use(l, which):
            return 4 * l + which

        @block.sync
        def _(sp):
            def mix_chunks(base):
                for c in range(base, base + MIX_CH):
                    load_chunk(sp, (c, c), c % RAWS)
            sp.dma_start(const[:, :], io["const"]).then_inc(const_in, 16)
            sp.dma_start(mem, io["mem"].rearrange("(t p) d -> p t d", p=P)).then_inc(mem_in, 16)
            for c in range(2):
                load_chunk(sp, (c, c), c % RAWS)
            sp.dma_start(x[:, 0:2, :], io["x_prompt"].rearrange("(t p) d -> p t d", p=P)).then_inc(x_in, 16)
            sp.dma_start(x[0:NS, 2, :], io["x_sample"]).then_inc(x_in, 16)
            sp.dma_start(state[:, :], io["state"][0]).then_inc(state_in, 16)
            for c in range(2, MIX_CH):
                load_chunk(sp, (c, c), c % RAWS)
            with nc.sync.Fori(0, UP_CH // RAWS) as i:
                for j in range(RAWS):
                    c = C_UP + RAWS * i + j
                    load_chunk(sp, (c, c), (C_UP + j) % RAWS)
            for c in range(C_UP + UP_CH // RAWS * RAWS, C_DOWN):
                load_chunk(sp, (c, c), c % RAWS)
            with nc.sync.Fori(0, DOWN_CH // RAWS) as i:
                for j in range(RAWS):
                    c = C_DOWN + RAWS * i + j
                    load_chunk(sp, (c, c), (C_DOWN + j) % RAWS)
            load_chunk(sp, (C_MIX1, C_MIX1), C_MIX1 % RAWS)
            sp.wait_ge(S["x_dense"], KD + 2)
            sp.dma_start(mem, io["mem"].rearrange("(t p) d -> p t d", p=P)).then_inc(mem_in, 16)
            sp.dma_start(state[:, :], io["state"][1]).then_inc(state_in, 16)
            for c in range(C_MIX1 + 1, C_MOE):
                load_chunk(sp, (c, c), c % RAWS)
            sp.wait_ge(turned_lo, KD * use(DEPTH, 0))
            sp.wait_ge(stored, 16 * LAYER_STORES * DEPTH)
            sp.dma_start(late[:, :], io["late"]).then_inc(late_in, 16)
            sp.dma_start(g_rows[:, :], io["g_moe"]).then_inc(gain_in, 16)

            for c in range(C_MOE, C_MOE + RAWS):
                load_chunk(sp, (c, c), c % RAWS)
            sp.wait_ge(S["rounds_ok"], 1)
            n_rounds = nc.sync.value_load(rounds[0:1, 0:1], min_val=1, max_val=MAX_ROUNDS)
            with nc.sync.Fori(0, n_rounds) as r:
                done = nc.sync.snap(1 >> r)
                with nc.sync.Fori(done, ROUND_CH // RAWS) as i:
                    for j in range(RAWS):
                        row = C_MOE + RAWS * i + j
                        load_chunk(sp, (row + ROUND_CH * r, row), (C_MOE + j) % RAWS)
            sp.dma_start(g_rows[:, :], io["g_final"]).then_inc(gain_in, 16)

        @block.gpsimd
        def _(pool):
            n_chain = [0]

            def link(ins):
                n_chain[0] += 1
                ins.then_inc(pool_chain, 1)
                pool.wait_ge(pool_chain, n_chain[0])

            nc.gpsimd.memset(ss[:, :, :], 1.0)
            nc.gpsimd.memset(half[:, :], -0.5).then_inc(preset, 1)
            pool.wait_ge(preset, 1)

            def power(n, parts):
                pool.wait_ge(squares, n + 1)
                n %= NORMS
                for a, b, width in parts:
                    last = nc.gpsimd.tensor_scalar(ms[:, n, a:b], ss[:, n, a:b], 1.0 / width, EPS, ALU.mult, ALU.add)
                link(last)
                b = parts[-1][1]
                nc.gpsimd.tensor_tensor(rstd[:, n, 0:b], ms[:, n, 0:b], half[:, 0:b], ALU.pow).then_inc(rstd_ok, 1)

            def zero_pair(pair):
                for z in pair:
                    last = nc.gpsimd.memset(z.bitcast(F), 0.0)
                last.then_inc(zeroed, 1)

            def store(out, in_):
                pool.dma_start(out, in_).then_inc(stored, 16)

            for l in range(DEPTH):
                n0 = NORMS * l
                if l:
                    pool.wait_ge(S["x_dense"], KD + 2)
                zero_pair(qs)
                power(n0 + N_MEM, [(0, 3, D)])
                power(n0 + N_MIX, [(0, 3, D)])
                if l == 0:
                    pool.wait_ge(const_in, 16)
                    for k in range(DEPTH):
                        for h in range(AH):
                            nc.gpsimd.affine_select(out=w_sp[:, k, h, :], in_=w_sp[:, k, h, :], compare_op=ALU.is_ge,
                                                    fill=0.0, base=0, pattern=[[1, P]], channel_multiplier=-1)
                            last = nc.gpsimd.affine_select(out=w_sps[:, k, h, :], in_=w_sps[:, k, h, :],
                                                           compare_op=ALU.is_ge, fill=0.0, base=0, pattern=[[1, NS]],
                                                           channel_multiplier=-1)
                    last.then_inc(masked, 1)
                pool.wait_ge(S["kv_out"], l + 1)
                store(io["mem_k"][l].rearrange("(t p) d -> p t d", p=P), kv[:, :, 0:DX])
                store(io["mem_v"][l].rearrange("(t p) d -> p t d", p=P), kv[:, :, DX:2 * DX])
                power(n0 + N_V, [(0, 3, DA)])
                pool.wait_ge(S["xb_out"], l + 1)
                store(io["pool_prompt"][l], xb[P - PBUF:P, 1, :])
                store(io["pool_sample"][l, :, PBUF - REQT:PBUF, :], xb[0:NS, 2, :])
                store(io["pool_sample"][l, :, 0:PBUF - REQT, :],
                      io["state"][l].rearrange("(b r) d -> b r d", r=PBUF)[:, REQT:PBUF, :])
                pool.wait_ge(chunk_used, l * C_MIX1 + 10)
                zero_pair(sPT)
                pool.wait_ge(S["v_out"], l + 1)
                store(io["v_rows"][l], vg[0:NS, 2, :])
                power(n0 + N_GROUP, [(0, 6, DA), (6, 9, DX)])
                power(n0 + N_FFN, [(0, 3, D)])
            power(NORMS * DEPTH, [(0, 3, D)])
            pool.wait_ge(S["fin_out"], 1)
            store(io["y_prompt"].rearrange("(t p) d -> p t d", p=P), xm[:, 0:2, :])
            store(io["y_sample"], xm[0:NS, 2, :])
            pool.wait_ge(stored, 16 * (DEPTH * (LAYER_STORES) + 2))

        @block.scalar
        def _(act):
            n_chain = [0]

            def link(ins):
                n_chain[0] += 1
                ins.then_inc(act_chain, 1)
                act.wait_ge(act_chain, n_chain[0])

            def sum_squares(src, n, col, tiles=(0, 1, 2), signal=True):
                for t in tiles:
                    r = ROWS[t]
                    last = nc.scalar.activation(junk[0:r, 0:src.shape[-1]], src[0:r, t, :], ACT.Square,
                                                accum_out=ss[0:r, n, col + t:col + t + 1])
                    link(last)
                if signal:
                    act.sem_inc(squares, 1)

            def turn_hi(l, which, n_tok):
                for k in range(KD):
                    act.wait_ge(turned, KD * use(l, which) + k + 1)
                    nc.scalar.activation(hT_hi[:, k, 0:n_tok], bank[k % 2][:, 0:n_tok], ACT.Copy,
                                         scale=gains[:, l, which, k:k + 1]).then_inc(turned_hi, 1)

            act.wait_ge(preset, 1)
            for l in range(DEPTH):
                c0 = l * C_MIX1
                if l == 0:
                    hi_static(act, c0)
                hi_static(act, c0 + 1, c0 + 2)
                act.wait_ge(mem_in, 16 * (l + 1))
                sum_squares(mem, N_MEM, 0, (0, 1))
                act.wait_ge(const_in, 16)
                turn_hi(l, G_MEM, NMEM)
                act.wait_ge(x_in, 32)
                sum_squares(x, N_MIX, 0)
                act.wait_ge(chunk_used, c0 + KV_CH)
                turn_hi(l, G_MIX, NT)
                hi_static(act, c0 + 3, c0 + 4)
                for i in range(4):
                    act.wait_ge(S["max_out"], 4 * l + i + 1)
                    for g in (2 * i, 2 * i + 1):
                        last = nc.scalar.activation(prob[:, g, :], bank[4 + i][:, (g % 2) * NMEM:(g % 2 + 1) * NMEM],
                                                    ACT.Exp, bias=nmx[:, g:g + 1], accum_out=den[:, g:g + 1])
                    last.then_inc(S["exp_done"], 1)
                hi_static(act, c0 + 5, c0 + 6)
                act.wait_ge(S["smax_out"], l + 1)
                nc.scalar.activation(sP[:, :], bank[3][:, 0:NMEM], ACT.Exp, bias=nmx[:, 8:9],
                                     accum_out=den[:, 8:9]).then_inc(S["sexp_done"], 1)
                hi_static(act, c0 + 7)
                for t in range(3):
                    act.wait_ge(S["v_done"], 3 * l + t + 1)
                    last = nc.scalar.activation(vg[0:ROWS[t], t, :], bank[t][0:ROWS[t], 0:DA], ACT.Gelu_apprx_tanh)
                last.then_inc(S["vg_out"], 1)
                act.wait_ge(S["vg_out"], l + 1)
                sum_squares(vg, N_V, 0)
                hi_static(act, c0 + 8, c0 + 9)
                act.wait_ge(chunk_used, c0 + 10)
                for t in range(3):
                    last = nc.scalar.activation(ug[0:ROWS[t], t, :], bank[t][0:ROWS[t], 0:DA], ACT.Gelu_apprx_tanh)
                last.then_inc(S["ug_out"], 1)
                hi_static(act, c0 + 10, c0 + 11, c0 + 12)
                act.wait_ge(S["o_out"], l + 1)
                sum_squares(ob, N_GROUP, 6, signal=False)
                act.wait_ge(S["a_out"], l + 1)
                sum_squares(ug, N_GROUP, 0, signal=False)
                act.wait_ge(S["b_out"], l + 1)
                sum_squares(b_rows, N_GROUP, 3)
                hi_static(act, c0 + 13, c0 + 14)
                turn_hi(l, G_GROUP, NT)
                hi_static(act, c0 + 15)
                if l == 0:
                    hi_static(act, C_UP)
                act.wait_ge(S["x_mixed"], 6 * l + 6)
                sum_squares(x, N_FFN, 0)
                turn_hi(l, G_FFN, NT)

                if l == 0:
                    with nc.scalar.Fori(0, NF // RAWS) as i:
                        for j in range(RAWS):
                            c = C_UP + 1 + RAWS * i + j
                            at = C_UP + 1 + j
                            split_hi(act, c, i + at // RAWS, at % RAWS)
                            act.wait_ge(chunk_used, C_UP + RAWS * i + j + 1)
                            nc.scalar.activation(sg[:, j % 2, :], bank[2 + 2 * (j % 2)][:, 0:NT], ACT.Silu)\
                                .then_inc(S["silu_out"], 1)
                    for f in range(NF // RAWS * RAWS, NF):
                        hi_static(act, C_UP + 1 + f)
                        act.wait_ge(chunk_used, C_UP + f + 1)
                        nc.scalar.activation(sg[:, f % 2, :], bank[2 + 2 * (f % 2)][:, 0:NT], ACT.Silu)\
                            .then_inc(S["silu_out"], 1)
                    act.sem_inc(S["yT_out"], 2)
                    with nc.scalar.Fori(0, DOWN_CH // RAWS) as i:
                        for what in (1, 2, "y0", 3, "y1", 4, 5, "y2", 6, "y3"):
                            if isinstance(what, int):
                                at = C_DOWN + what
                                split_hi(act, at + RAWS * i, i + at // RAWS, at % RAWS)
                            else:
                                j = int(what[1])
                                if j % 2:
                                    act.wait_ge(chunk_used, C_DOWN + RAWS * i + 3 * (j + 1) // 2)
                                else:
                                    act.wait_ge(S["yT_done"], 2 * i + j // 2 + 1)
                                nc.scalar.activation(yT[:, j % 2, :], bank[6 + j % 2][:, 0:NT], ACT.Copy)\
                                    .then_inc(S["yT_out"], 1)

            for t in range(3):
                r = ROWS[t]
                act.wait_ge(S["logit_out"], 1)
                last = nc.scalar.activation(expo[0:r, t, :], logits[0:r, t, :], ACT.Exp, bias=nfirst[0:r, t:t + 1])
            last.then_inc(S["exp2_out"], 1)
            act.wait_ge(S["rounds_ok"], 1)
            n_rounds = nc.scalar.value_load(rounds[0:1, 0:1], min_val=1, max_val=MAX_ROUNDS)
            with nc.scalar.Fori(0, n_rounds) as r:
                def regs(e):
                    q = nc.scalar.snap(r * NE + e)
                    return (q, nc.scalar.snap(q * EXP_CH + (C_MOE + 2)),
                            nc.scalar.snap(q * (EXP_CH // RAWS) + C_MOE // RAWS), nc.scalar.snap(q * STEPS))

                def hi(cb, lap, off, extra=0):
                    split_hi(act, cb + off + RAWS * extra, lap + (off + 2) // RAWS + extra, (off + 2) % RAWS)

                def gathered_hi(q, j, b):
                    act.wait_ge(S["gat_done"], 2 * q + b + 1)
                    nc.scalar.activation(gT_hi[:, j, 4 * b:4 * b + 4, :].rearrange("p a b -> p (a b)"), bank[b][:, :],
                                         ACT.Copy).then_inc(S["gat_hi"], 1)

                def silu_of(cb, s, extra=0):
                    act.wait_ge(chunk_used, cb + 3 * s - 1 + RAWS * extra)
                    nc.scalar.activation(esg[:, s % 2, :], bank[2 + s % 2][:, 0:256], ACT.Silu).then_inc(S["esilu"], 1)

                def turned_of(g0, s, extra=0):
                    act.wait_ge(S["eT_done"], g0 + s + 1 + 2 * extra)
                    nc.scalar.activation(eT_hi[:, s % 2, :, :].rearrange("p a b -> p (a b)"), bank[4 + s % 2][:, 0:256],
                                         ACT.Copy).then_inc(S["eT_hi_out"], 1)

                def y_hi_of():
                    for n in range(2):
                        nc.scalar.activation(y_hi[:, n * 512:(n + 1) * 512], bank[6 + n][:, :], ACT.Copy)\
                            .then_inc(S["y_hi_out"], 1)

                def step(cb, lap, g0, s, extra=0):
                    silu_of(cb, s, extra)
                    hi(cb, lap, 3 * s + 2, extra)
                    turned_of(g0, s, extra)
                    hi(cb, lap, 3 * s + 3, extra)
                    hi(cb, lap, 3 * s + 4, extra)

                def expert(e, j, last):
                    q, cb, lap, g0 = regs(e)
                    with nc.scalar.Fori(0, STEPS // 2 - 2) as p:
                        step(cb, lap, g0, 2, p)
                        step(cb, lap, g0, 3, p)
                    s = STEPS - 2
                    silu_of(cb, s)
                    hi(cb, lap, 3 * s + 2)
                    if last:
                        turned_of(g0, s)
                        hi(cb, lap, 3 * s + 3)
                        silu_of(cb, s + 1)
                        turned_of(g0, s + 1)
                        act.wait_ge(chunk_used, cb + EXP_CH - 2)
                        y_hi_of()
                        return
                    gathered_hi(q + 1, 1 - j, 0)
                    turned_of(g0, s)
                    gathered_hi(q + 1, 1 - j, 1)
                    hi(cb, lap, 3 * s + 3)
                    hi(cb, lap, 3 * s + 4)
                    step(cb, lap, g0, s + 1)
                    s = STEPS
                    silu_of(cb, s)
                    act.wait_ge(chunk_used, cb + EXP_CH)
                    y_hi_of()
                    hi(cb, lap, 3 * s + 2)
                    turned_of(g0, s)
                    hi(cb, lap, 3 * s + 3)
                    hi(cb, lap, 3 * s + 4)
                    step(cb, lap, g0, s + 1)

                q, cb, lap, g0 = regs(0)
                for off in (-2, -1, 0):
                    hi(cb, lap, off)
                for b in range(2):
                    gathered_hi(q, 0, b)
                hi(cb, lap, 1)
                act.wait_ge(chunk_used, cb)
                step(cb, lap, g0, 0)
                step(cb, lap, g0, 1)
                with nc.scalar.Fori(0, NE // 2 - 1) as pair:
                    for j in range(2):
                        expert(2 * pair + j, j, False)
                for j in range(2):
                    expert(NE - 2 + j, j, j == 1)
            act.wait_ge(S["x_added"], n_rounds * (6 * NE) + 2)
            sum_squares(x, 0, 0)

        @block.vector
        def _(dve):
            V = nc.vector
            n_chain = [0]

            def link(ins):
                n_chain[0] += 1
                ins.then_inc(dve_chain, 1)
                dve.wait_ge(dve_chain, n_chain[0])

            def scale_rows(src, n, tiles=(0, 1, 2)):
                dve.wait_ge(rstd_ok, n + 1)
                for t in tiles:
                    r = ROWS[t]
                    last = V.tensor_scalar(xn[0:r, t, :], src[0:r, t, :], rstd[0:r, n % NORMS, t:t + 1], None, ALU.mult)
                last.then_inc(rows_ok, 1)

            def turn_lo(l, which, n_tok):
                for k in range(KD):
                    dve.wait_ge(turned_hi, KD * use(l, which) + k + 1)
                    V.scalar_tensor_tensor(out=hT_lo[:, k, 0:n_tok], in0=bank[k % 2][:, 0:n_tok],
                                           scalar=gains[:, l, which, k:k + 1], in1=hT_hi[:, k, 0:n_tok].bitcast(F),
                                           op0=ALU.mult, op1=ALU.subtract).then_inc(turned_lo, 1)

            for l in range(DEPTH):
                c0 = l * C_MIX1
                n0 = NORMS * l
                if l == 0:
                    lo_static(dve, c0)
                lo_static(dve, c0 + 1, c0 + 2)
                dve.wait_ge(mem_in, 16 * (l + 1))
                scale_rows(mem, n0 + N_MEM, (0, 1))
                dve.wait_ge(const_in, 16)
                turn_lo(l, G_MEM, NMEM)
                scale_rows(x, n0 + N_MIX)
                dve.wait_ge(chunk_used, c0 + KV_CH)
                for t in range(2):
                    last = V.tensor_copy(kv[:, t, :], bank[2 + t][:, :])
                last.then_inc(S["kv_out"], 1)
                turn_lo(l, G_MIX, NT)
                dve.wait_ge(chunk_used, c0 + 3)
                dve.wait_ge(zeroed, 2 * l + 1)
                for f in range(2):
                    V.tensor_scalar(qT[:, f, :], bank[4 + f][:, 0:SEQ], HD ** -0.5, None, ALU.mult)

                def own(q_, f, p):
                    h = 2 * f + p
                    return own_columns(q_)[HD * p:HD * p + HD, f, :, h * REQT:(h + 1) * REQT]

                def sample_q(f, p):
                    return bank[4 + f][HD * p:HD * p + HD, SEQ:NT].rearrange("p (b t) -> p b t", t=REQT)
                halves = [(f, p) for f in range(2) for p in range(2)]
                for f, p in halves:
                    last = V.tensor_scalar(own(qs[0], f, p), sample_q(f, p), HD ** -0.5, None, ALU.mult)
                link(last)
                for f, p in halves:
                    last = V.scalar_tensor_tensor(out=own(qs[1], f, p), in0=sample_q(f, p), scalar=HD ** -0.5,
                                                  in1=own(qs[0], f, p).bitcast(F), op0=ALU.mult, op1=ALU.subtract)
                last.then_inc(S["q_out"], 1)
                dve.wait_ge(S["kT_done"], l + 1)
                V.tensor_copy(kT[:, :, :].rearrange("p a b -> p (a b)"), bank[2][:, :]).then_inc(S["kT_out"], 1)
                lo_static(dve, c0 + 3, c0 + 4)
                for i in range(4):
                    dve.wait_ge(S["sc_done"], 4 * l + i + 1)
                    link(V.reduce_max(mx[:, 2 * i:2 * i + 2], bank[4 + i][:, :].rearrange("p (g m) -> p g m", g=2), AX.X))
                    V.tensor_scalar(nmx[:, 2 * i:2 * i + 2], mx[:, 2 * i:2 * i + 2], -1.0, None, ALU.mult)\
                        .then_inc(S["max_out"], 1)
                lo_static(dve, c0 + 5, c0 + 6)
                dve.wait_ge(chunk_used, c0 + 5)
                link(V.reduce_max(mx[:, 8:9], bank[3][:, 0:NMEM], AX.X))
                V.tensor_scalar(nmx[:, 8:9], mx[:, 8:9], -1.0, None, ALU.mult).then_inc(S["smax_out"], 1)
                lo_static(dve, c0 + 7)
                dve.wait_ge(S["sexp_done"], l + 1)
                link(V.reciprocal(rden[:, :], den[:, :]))
                lo_static(dve, c0 + 8, c0 + 9)
                for t in range(3):
                    dve.wait_ge(S["xb_done"], 3 * l + t + 1)
                    last = V.tensor_copy(xb[0:ROWS[t], t, :], bank[4 + t][0:ROWS[t], 0:DB])
                last.then_inc(S["xb_out"], 1)
                dve.wait_ge(rstd_ok, n0 + N_V + 1)
                for t in range(3):
                    r = ROWS[t]
                    last = V.scalar_tensor_tensor(out=vg[0:r, t, :], in0=vg[0:r, t, :], scalar=rstd[0:r, N_V, t:t + 1],
                                                  in1=g_v[0:r, l, :], op0=ALU.mult, op1=ALU.mult)
                last.then_inc(S["v_out"], 1)
                for i in range(4):
                    dve.wait_ge(S["PT_done"], 4 * l + i + 1)
                    V.tensor_copy(PT[:, i % 2, :, :].rearrange("p a b -> p (a b)"), bank[(7, 3)[i % 2]][:, :])\
                        .then_inc(S["PT_out"], 1)
                dve.wait_ge(S["sPT_done"], l + 1)
                dve.wait_ge(zeroed, 2 * l + 2)
                turned_p = bank[5][:, 0:256].rearrange("p (f b c) -> p f b c", f=2, b=NREQ)
                link(V.tensor_copy(own_columns(sPT[0]), turned_p))
                V.tensor_tensor(own_columns(sPT[1]), turned_p, own_columns(sPT[0]).bitcast(F), ALU.subtract)\
                    .then_inc(S["sPT_out"], 1)
                dve.wait_ge(S["o_done"], 4 * l + 4)
                for t in range(2):
                    for p in range(2):
                        by_head = lambda a: a.rearrange("p (f h d) -> p f h d", f=2, h=2)[:, :, p, :]
                        sums = rden[:, 4 * t + 2 * p:4 * t + 2 * p + 2].rearrange("p (f a) -> p f a", a=1)
                        last = V.tensor_tensor(by_head(ob[:, t, :]), by_head(bank[4][:, t * DX:(t + 1) * DX]),
                                               sums.to_broadcast([P, 2, HD]), ALU.mult)
                lo_static(dve, c0 + 10, c0 + 11, c0 + 12)
                dve.wait_ge(chunk_used, c0 + 12)
                V.tensor_scalar(os_rows[:, :], bank[6][:, 0:DX], rden[:, 8:9], None, ALU.mult).then_inc(S["os_rows_out"], 1)
                dve.wait_ge(S["os_done"], l + 1)
                V.tensor_copy(ob[0:NS, 2, :], bank[7][0:NS, 0:DX]).then_inc(S["o_out"], 1)
                for g in range(4):
                    dve.wait_ge(S["dT_done"], 4 * l + g + 1)
                    last = V.tensor_copy(dT[0:GD, g, :], bank[g][0:GD, 0:NT])
                last.then_inc(S["dT_out"], 1)
                dve.wait_ge(S["ug_out"], l + 1)
                for t in range(3):
                    dve.wait_ge(S["mix_done"], 3 * l + t + 1)
                    r = ROWS[t]
                    for h in range(AH):
                        cols = slice(h * AHD, (h + 1) * AHD)
                        last = V.scalar_tensor_tensor(out=ug[0:r, t, cols], in0=bank[4 + t][0:r, cols],
                                                      scalar=bias[0:r, l, t // 2, h:h + 1], in1=ug[0:r, t, cols],
                                                      op0=ALU.add, op1=ALU.mult)
                last.then_inc(S["a_out"], 1)
                dve.wait_ge(S["y_done"], 3 * l + 3)
                for t in range(3):
                    r = ROWS[t]
                    last = V.tensor_tensor(b_rows[0:r, t, :], bank[t][0:r, 0:DB], s_pool[0:r, l, :], ALU.mult)
                last.then_inc(S["b_out"], 1)
                lo_static(dve, c0 + 13, c0 + 14)
                dve.wait_ge(rstd_ok, n0 + N_GROUP + 1)
                for src, a, b, col in ((ug, 0, DA, 0), (b_rows, DA, DA + DB, 3), (ob, DA + DB, D, 6)):
                    for t in range(3):
                        r = ROWS[t]
                        last = V.tensor_scalar(xn[0:r, t, a:b], src[0:r, t, :], rstd[0:r, N_GROUP, col + t:col + t + 1],
                                               None, ALU.mult)
                last.then_inc(rows_ok, 1)
                turn_lo(l, G_GROUP, NT)
                lo_static(dve, c0 + 15)
                if l == 0:
                    lo_static(dve, C_UP)
                for n in range(2):
                    dve.wait_ge(chunk_used, c0 + 14 + 2 * n)
                    for t in range(3):
                        r = ROWS[t]
                        V.tensor_tensor(x[0:r, t, n * 512:(n + 1) * 512], x[0:r, t, n * 512:(n + 1) * 512],
                                        bank[2 + 3 * n + t][0:r, :], ALU.add).then_inc(S["x_mixed"], 1)
                dve.wait_ge(S["x_mixed"], 6 * l + 6)
                scale_rows(x, n0 + N_FFN)
                turn_lo(l, G_FFN, NT)
                dve.wait_ge(stored, 16 * (LAYER_STORES) * (l + 1))

                if l == 0:
                    dve.sem_inc(S["H_out"], 2)

                    def hidden(f, j):
                        dve.wait_ge(S["silu_out"], f + 1)
                        up_ps = bank[3 + 2 * (j % 2)][:, 0:NT]
                        at = bass.ds(f * NT, NT)
                        V.tensor_tensor(HT_hi[:, :, :].rearrange("p a b -> p (a b)")[:, at], sg[:, j % 2, :], up_ps, ALU.mult)
                        V.tensor_tensor(hf[:, j % 2, :], sg[:, j % 2, :], up_ps, ALU.mult).then_inc(S["hf_out"], 1)
                        dve.wait_ge(S["hf_out"], f + 1)
                        V.tensor_tensor(HT_lo[:, :, :].rearrange("p a b -> p (a b)")[:, at], hf[:, j % 2, :],
                                        HT_hi[:, :, :].rearrange("p a b -> p (a b)")[:, at].bitcast(F), ALU.subtract)\
                            .then_inc(S["H_out"], 1)
                    with V.Fori(0, NF // RAWS) as i:
                        for j in range(RAWS):
                            split_lo(dve, C_UP + 1 + RAWS * i + j, (C_UP + 1 + j) % RAWS)
                            hidden(RAWS * i + j, j)
                    for f in range(NF // RAWS * RAWS, NF):
                        lo_static(dve, C_UP + 1 + f)
                        hidden(f, f)
                    dve.sem_inc(S["x_dense"], 2)
                    with V.Fori(0, DOWN_CH // RAWS) as i:
                        for what in (1, 2, 3, "x0", 4, 5, "x1", 6, "x2", "x3"):
                            if isinstance(what, int):
                                at = C_DOWN + what
                                split_lo(dve, at + RAWS * i, at % RAWS)
                            else:
                                j = int(what[1])
                                dve.wait_ge(S["y_turned"], 4 * i + j + 1)
                                for t0, t1, r in ((0, 2, P), (2, 3, NS)):
                                    at = x[0:r, t0:t1, bass.ds((4 * i + j) * P, P)]
                                    last = V.tensor_tensor(at, at, bank[j % 2][0:r, t0 * P:t1 * P]
                                                           .rearrange("p (t d) -> p t d", d=P), ALU.add)
                                last.then_inc(S["x_dense"], 1)

            V.memset(logits[:, :, :], 0.0)
            V.memset(mask[:, :, :], 0.0)
            V.memset(posm[:, :, :], -FAR)
            dve.wait_ge(late_in, 16)
            link(V.tensor_copy(rt_hi[:, :, :], router))
            V.tensor_tensor(rt_lo[:, :, :], router, rt_hi[:, :, :].bitcast(F), ALU.subtract).then_inc(S["rt_out"], 1)
            dve.wait_ge(gain_in, 16)
            for t in range(3):
                r = ROWS[t]
                last = V.scalar_tensor_tensor(out=xm[0:r, t, :], in0=x[0:r, t, :], scalar=rstd[0:r, N_FFN, t:t + 1],
                                              in1=g_rows[0:r, :], op0=ALU.mult, op1=ALU.mult)
            last.then_inc(S["xm_out"], 1)
            dve.wait_ge(S["logit_done"], 1)
            for t in range(3):
                last = V.tensor_copy(logits[0:ROWS[t], t, :], bank[2][0:ROWS[t], t * NE:(t + 1) * NE])
            link(last)
            for t in range(3):
                last = V.max(top[0:ROWS[t], t, :], logits[0:ROWS[t], t, :])
            link(last)
            for t0, t1, r in ((0, 2, P), (2, 3, NS)):
                last = V.tensor_scalar(nfirst[0:r, t0:t1], top[0:r, t0:t1, 0], -1.0, None, ALU.mult)
            last.then_inc(S["logit_out"], 1)
            for t in range(3):
                last = V.memset(top[0:ROWS[t], t, 2:8], -NEVER)
            link(last)
            for t in range(3):
                r = ROWS[t]
                last = V.match_replace(left[0:r, t, :], top[0:r, t, :], logits[0:r, t, :], NEVER)
            link(last)
            for t in range(3):
                r = ROWS[t]
                last = V.tensor_scalar(mask[0:r, t, :], left[0:r, t, :], 0.5 * NEVER, None, ALU.is_le)
            last.then_inc(S["pos_in"], 1)
            dve.wait_ge(S["pos_in"], 1)
            dve.wait_ge(S["exp2_out"], 1)
            for t in range(3):
                r = ROWS[t]
                last = V.tensor_tensor(gate[0:r, t, :], expo[0:r, t, :], mask[0:r, t, :], ALU.mult)
            link(last)
            for t in range(3):
                r = ROWS[t]
                last = V.reduce_sum(gden[0:r, t:t + 1], gate[0:r, t, :], AX.X)
            link(last)
            for t in range(3):
                r = ROWS[t]
                last = V.reciprocal(gden[0:r, t:t + 1], gden[0:r, t:t + 1])
            link(last)
            for t in range(3):
                r = ROWS[t]
                last = V.tensor_scalar(gate[0:r, t, :], gate[0:r, t, :], gden[0:r, t:t + 1], None, ALU.mult)
            link(last)
            for t in range(3):
                r = ROWS[t]
                last = V.tensor_scalar(posm[0:r, t, :], mask[0:r, t, :], FAR, -FAR, ALU.mult, ALU.add)
            link(last)
            dve.wait_ge(S["pos_done"], 1)
            for t in range(3):
                r = ROWS[t]
                last = V.tensor_tensor(posm[0:r, t, :], posm[0:r, t, :], bank[3][0:r, t * NE:(t + 1) * NE], ALU.add)
            link(last)
            link(V.reduce_max(cmax[:, :], bank[3][0:1, 3 * NE:4 * NE], AX.X))
            V.tensor_scalar(over[:, 0:1], cmax[:, :], float(P), 1.0, ALU.is_gt, ALU.add)
            link(V.tensor_scalar(over[:, 1:2], cmax[:, :], float(2 * P), None, ALU.is_gt))
            V.tensor_tensor(rounds[:, :], over[:, 0:1], over[:, 1:2], ALU.add).then_inc(S["rounds_ok"], 1)
            dve.sem_inc(S["x_added"], 2)
            dve.wait_ge(S["rounds_ok"], 1)
            n_rounds = V.value_load(rounds[0:1, 0:1], min_val=1, max_val=MAX_ROUNDS)
            with V.Fori(0, n_rounds) as r:
                def regs(e):
                    q = V.snap(r * NE + e)
                    return q, V.snap(q * EXP_CH + (C_MOE + 2)), V.snap(q * STEPS)

                def lo(cb, off, extra=0):
                    split_lo(dve, cb + off + RAWS * extra, (off + 2) % RAWS)

                def select(e):
                    for t in range(3):
                        rr = ROWS[t]
                        last = V.tensor_scalar(sel[0:rr, t, :], slots[0:rr, :], posm[0:rr, t, bass.ds(e, 1)], None,
                                               ALU.is_equal)
                    last.then_inc(S["sel_out"], 1)

                def gathered_lo(q, j, b):
                    dve.wait_ge(S["gat_hi"], 2 * q + b + 1)
                    V.tensor_tensor(gT_lo[:, j, 4 * b:4 * b + 4, :].rearrange("p a b -> p (a b)"), bank[b][:, :],
                                    gT_hi[:, j, 4 * b:4 * b + 4, :].rearrange("p a b -> p (a b)").bitcast(F), ALU.subtract)\
                        .then_inc(S["gat_lo"], 1)

                def keep_selT(q, j):
                    dve.wait_ge(S["selT_done"], q + 1)
                    V.tensor_copy(selT[:, j, :], bank[0][:, 0:NT]).then_inc(S["selT_out"], 1)

                def hidden_of(g0, s, extra=0):
                    dve.wait_ge(S["esilu"], g0 + s + 1 + 2 * extra)
                    V.tensor_tensor(eh[:, s % 2, :], esg[:, s % 2, :], bank[2 + s % 2][:, 256:512], ALU.mult)\
                        .then_inc(S["eh_out"], 1)

                def turned_of(g0, s, extra=0):
                    dve.wait_ge(S["eT_hi_out"], g0 + s + 1 + 2 * extra)
                    V.tensor_tensor(eT_lo[:, s % 2, :, :].rearrange("p a b -> p (a b)"), bank[4 + s % 2][:, 0:256],
                                    eT_hi[:, s % 2, :, :].rearrange("p a b -> p (a b)").bitcast(F), ALU.subtract)\
                        .then_inc(S["eT_out"], 1)

                def y_lo_of(q):
                    for n in range(2):
                        dve.wait_ge(S["y_hi_out"], 2 * q + n + 1)
                        last = V.tensor_tensor(y_lo[:, n * 512:(n + 1) * 512], bank[6 + n][:, :],
                                               y_hi[:, n * 512:(n + 1) * 512].bitcast(F), ALU.subtract)
                    last.then_inc(S["y_out"], 1)

                def add(q, e, *ms_):
                    for m in ms_:
                        t, n = m // 2, m % 2
                        rr = ROWS[t]
                        dve.wait_ge(S["scat_done"], 6 * q + m + 1)
                        at = x[0:rr, t, n * 512:(n + 1) * 512]
                        V.scalar_tensor_tensor(out=at, in0=bank[n][0:rr, :], scalar=gate[0:rr, t, bass.ds(e, 1)], in1=at,
                                               op0=ALU.mult, op1=ALU.add).then_inc(S["x_added"], 1)

                def step(cb, g0, s, extra=0):
                    hidden_of(g0, s, extra)
                    lo(cb, 3 * s + 2, extra)
                    turned_of(g0, s, extra)
                    lo(cb, 3 * s + 3, extra)
                    lo(cb, 3 * s + 4, extra)

                def expert(e, j, last):
                    q, cb, g0 = regs(e)
                    if not last:
                        select(e + 1)
                    with V.Fori(0, STEPS // 2 - 2) as p:
                        step(cb, g0, 2, p)
                        step(cb, g0, 3, p)
                    s = STEPS - 2
                    hidden_of(g0, s)
                    lo(cb, 3 * s + 2)
                    if last:
                        turned_of(g0, s)
                        lo(cb, 3 * s + 3)
                        hidden_of(g0, s + 1)
                        turned_of(g0, s + 1)
                        y_lo_of(q)
                        add(q, e, 0, 1, 2, 3, 4, 5)
                        return
                    gathered_lo(q + 1, 1 - j, 0)
                    turned_of(g0, s)
                    gathered_lo(q + 1, 1 - j, 1)
                    lo(cb, 3 * s + 3)
                    lo(cb, 3 * s + 4)
                    s = STEPS - 1
                    hidden_of(g0, s)
                    lo(cb, 3 * s + 2)
                    turned_of(g0, s)
                    lo(cb, 3 * s + 3)
                    keep_selT(q + 1, 1 - j)
                    lo(cb, 3 * s + 4)
                    s = STEPS
                    hidden_of(g0, s)
                    y_lo_of(q)
                    lo(cb, 3 * s + 2)
                    turned_of(g0, s)
                    lo(cb, 3 * s + 3)
                    add(q, e, 0, 1)
                    lo(cb, 3 * s + 4)
                    s = STEPS + 1
                    hidden_of(g0, s)
                    lo(cb, 3 * s + 2)
                    add(q, e, 2, 3)
                    turned_of(g0, s)
                    lo(cb, 3 * s + 3)
                    add(q, e, 4, 5)
                    lo(cb, 3 * s + 4)

                select(0)
                q, cb, g0 = regs(0)
                for off in (-2, -1, 0):
                    lo(cb, off)
                for b in range(2):
                    gathered_lo(q, 0, b)
                keep_selT(q, 0)
                lo(cb, 1)
                step(cb, g0, 0)
                step(cb, g0, 1)
                with V.Fori(0, NE // 2 - 1) as pair:
                    for j in range(2):
                        expert(2 * pair + j, j, False)
                for j in range(2):
                    expert(NE - 2 + j, j, j == 1)
                V.tensor_scalar(posm[:, :, :], posm[:, :, :], -float(P), None, ALU.add).then_inc(S["pos_moved"], 1)
                dve.wait_ge(S["pos_moved"], r + 1)
            dve.wait_ge(rstd_ok, NORMS * DEPTH + 1)
            dve.wait_ge(gain_in, 32)
            for t in range(3):
                rr = ROWS[t]
                last = V.scalar_tensor_tensor(out=xm[0:rr, t, :], in0=x[0:rr, t, :], scalar=rstd[0:rr, 0, t:t + 1],
                                              in1=g_rows[0:rr, :], op0=ALU.mult, op1=ALU.mult)
            last.then_inc(S["fin_out"], 1)

        @block.tensor
        def _(pe):
            T = nc.tensor

            def arrived(c):
                pe.wait_ge(lo_ready, c + 1)

            def turn(l, which, tiles=(0, 1, 2)):
                u = use(l, which)
                pe.wait_ge(rows_ok, u + 1)
                if u:
                    pe.wait_ge(turned_lo, KD * u)
                for k in range(KD):
                    if k >= 2:
                        pe.wait_ge(turned_lo, KD * u + k - 1)
                    for t in tiles:
                        r = ROWS[t]
                        last = T.transpose(bank[k % 2][:, t * P:t * P + r], xn[0:r, t, k * P:(k + 1) * P],
                                           ident[0:r, 0:r])
                    last.then_inc(turned, 1)

            def rows_times(c, b, n_blocks, k, banks, first, last_k):
                out = []
                for t in range(3):
                    r = ROWS[t]
                    out.append(mm3(bank[banks + t][0:r, 0:n_blocks * P], hT_hi[:, k, t * P:t * P + r],
                                   hT_lo[:, k, t * P:t * P + r], blk(whi, c, b, n_blocks), blk(wlo, c, b, n_blocks),
                                   first, last_k))
                return out

            pe.wait_ge(const_in, 16)
            for l in range(DEPTH):
                c0 = l * C_MIX1
                if l:
                    pe.wait_ge(S["x_dense"], KD + 2)
                turn(l, G_MEM, (0, 1))
                pe.wait_ge(turned_lo, KD * (use(l, G_MEM) + 1))
                for c in (0, 1):
                    arrived(c0 + c)
                    for k in range(4):
                        for t in range(2):
                            m = mm3(bank[2 + t][:, :], hT_hi[:, 4 * c + k, t * P:(t + 1) * P],
                                    hT_lo[:, 4 * c + k, t * P:(t + 1) * P], blk(whi, c0 + c, 4 * k, 4),
                                    blk(wlo, c0 + c, 4 * k, 4), c == 0 and k == 0, c == 1 and k == 3)
                    m.then_inc(chunk_used, 1)
                turn(l, G_MIX)
                pe.wait_ge(turned_lo, KD * (use(l, G_MIX) + 1))
                arrived(c0 + 2)
                for k in range(KD):
                    for f in range(2):
                        m = mm3(bank[4 + f][:, 0:NT], blk(whi, c0 + 2, 2 * k + f), blk(wlo, c0 + 2, 2 * k + f),
                                hT_hi[:, k, :], hT_lo[:, k, :], k == 0, k == KD - 1)
                m.then_inc(chunk_used, 1)
                pe.wait_ge(S["kv_out"], l + 1)
                for f in range(2):
                    for t in range(2):
                        last = T.transpose(bank[2][:, f * 256 + t * P:f * 256 + (t + 1) * P], kv[:, t, f * P:(f + 1) * P],
                                           ident)
                last.then_inc(S["kT_done"], 1)
                pe.wait_ge(S["q_out"], l + 1)
                pe.wait_ge(S["kT_out"], l + 1)
                for t in range(2):
                    for f in range(2):
                        for p in range(2):
                            m = T.matmul(bank[4 + 2 * t + p][:, f * NMEM:(f + 1) * NMEM],
                                         qT[HD * p:HD * p + HD, f, t * P:(t + 1) * P], kT[HD * p:HD * p + HD, f, :],
                                         start=True, stop=True)
                            if f == 1:
                                m.then_inc(S["sc_done"], 1)
                for c in (0, 1):
                    arrived(c0 + 3 + c)
                    for b in range(4):
                        for f in range(2):
                            r = 4 * c + b
                            m = mm3(bank[3][:, 0:NMEM], only(qs[0], f, r), only(qs[1], f, r),
                                    blk(whi, c0 + 3 + c, 4 * b + 2 * f, 2), blk(wlo, c0 + 3 + c, 4 * b + 2 * f, 2),
                                    r == 0 and f == 0, r == NREQ - 1 and f == 1)
                    m.then_inc(chunk_used, 1)
                arrived(c0 + 5)
                for k in range(5):
                    m = rows_times(c0 + 5, 3 * k, 3, k, 0, k == 0, False)[-1]
                m.then_inc(chunk_used, 1)
                arrived(c0 + 6)
                for k in (5, 6, 7):
                    ms_ = rows_times(c0 + 6, 3 * (k - 5), 3, k, 0, False, k == 7)
                for m in ms_:
                    m.then_inc(S["v_done"], 1)
                pe.wait_ge(S["exp_done"], 4 * l + 4)
                for k in (0, 1):
                    m = rows_times(c0 + 6, 9 + 3 * k, 3, k, 4, k == 0, False)[-1]
                m.then_inc(chunk_used, 1)
                arrived(c0 + 7)
                for k in range(2, 7):
                    m = rows_times(c0 + 7, 3 * (k - 2), 3, k, 4, False, False)[-1]
                m.then_inc(chunk_used, 1)
                arrived(c0 + 8)
                for m in rows_times(c0 + 8, 0, 3, 7, 4, False, True):
                    m.then_inc(S["xb_done"], 1)
                pe.wait_ge(S["vg_out"], l + 1)
                for k in range(4):
                    m = rows_times(c0 + 8, 3 + 3 * k, 3, k, 0, k == 0, False)[-1]
                m.then_inc(chunk_used, 1)
                arrived(c0 + 9)
                for k in range(4, 8):
                    m = rows_times(c0 + 9, 3 * (k - 4), 3, k, 0, False, k == 7)[-1]
                m.then_inc(chunk_used, 1)

                def turn_probs(i):
                    if i == 1:
                        pe.wait_ge(S["sexp_done"], l + 1)
                    if i >= 2:
                        pe.wait_ge(S["PT_out"], 4 * l + i - 1)
                    for f in range(2):
                        for mt in range(2):
                            last = T.transpose(bank[(7, 3)[i % 2]][:, (2 * f + mt) * P:(2 * f + mt + 1) * P],
                                               prob[:, 2 * i + f, mt * P:(mt + 1) * P], ident)
                    last.then_inc(S["PT_done"], 1)

                def attend(i):
                    t, p = i // 2, i % 2
                    pe.wait_ge(S["PT_out"], 4 * l + i + 1)
                    for f in range(2):
                        h = 2 * f + p
                        for mt in range(2):
                            last = T.matmul(bank[4][:, t * DX + h * HD:t * DX + (h + 1) * HD], PT[:, i % 2, 2 * f + mt, :],
                                            kv[:, mt, DX + h * HD:DX + (h + 1) * HD], start=mt == 0, stop=mt == 1)
                    last.then_inc(S["o_done"], 1)

                turn_probs(0)
                turn_probs(1)
                pe.wait_ge(S["xb_out"], l + 1)
                attend(0)
                turn_probs(2)
                attend(1)
                turn_probs(3)
                pe.wait_ge(S["sexp_done"], l + 1)
                for mt in range(2):
                    last = T.transpose(bank[5][:, mt * P:(mt + 1) * P], sP[:, mt * P:(mt + 1) * P], ident)
                last.then_inc(S["sPT_done"], 1)
                attend(2)
                attend(3)
                pe.wait_ge(S["sPT_out"], l + 1)
                for c in (0, 1):
                    arrived(c0 + 10 + c)
                    for b in range(4):
                        for mt in range(2):
                            r = 4 * c + b
                            m = mm3(bank[6][:, 0:DX], only(sPT[0], mt, r), only(sPT[1], mt, r),
                                    blk(whi, c0 + 10 + c, 4 * b + 2 * mt, 2), blk(wlo, c0 + 10 + c, 4 * b + 2 * mt, 2),
                                    r == 0 and mt == 0, r == NREQ - 1 and mt == 1)
                    m.then_inc(chunk_used, 1)
                pe.wait_ge(S["os_rows_out"], l + 1)
                for h in range(HEADS):
                    last = T.matmul(bank[7][0:NS, h * HD:(h + 1) * HD], fold[:, h, :], os_rows[:, h * HD:(h + 1) * HD],
                                    start=True, stop=True)
                last.then_inc(S["os_done"], 1)
                pe.wait_ge(S["ug_out"], l + 1)
                pe.wait_ge(state_in, 16 * (l + 1))
                for g in range(4):
                    ch = slice(g * GD, (g + 1) * GD)
                    T.matmul(bank[g][0:GD, 0:SEQ], xb[:, 0, ch], pool0[:, g, :], start=True, stop=False)
                    T.matmul(bank[g][0:GD, P:SEQ], xb[:, 1, ch], pool1[:, g, :], start=False, stop=True)
                    T.matmul(bank[g][0:GD, SEQ:NT], xb[0:NS, 2, ch], pool_s[:, g, :], start=True, stop=False)
                    T.matmul(bank[g][0:GD, SEQ:NT], state[:, ch], pool_st[:, g, :], start=False, stop=True)\
                        .then_inc(S["dT_done"], 1)
                pe.wait_ge(masked, 1)
                pe.wait_ge(S["v_out"], l + 1)
                pe.wait_ge(S["o_out"], l + 1)
                for t in range(3):
                    r = ROWS[t]
                    w = w_sp if t < 2 else w_sps
                    for h in range(AH):
                        last = T.matmul(bank[4 + t][0:r, h * AHD:(h + 1) * AHD], w[:, l, h, :],
                                        vg[0:r, t, h * AHD:(h + 1) * AHD], start=True, stop=True)
                    last.then_inc(S["mix_done"], 1)
                pe.wait_ge(S["dT_out"], l + 1)
                for t in range(3):
                    r = ROWS[t]
                    for g in range(4):
                        last = T.matmul(bank[t][0:r, g * GD:(g + 1) * GD], dT[0:GD, g, t * P:t * P + r], w_pool[:, l, g, :],
                                        start=True, stop=True)
                    last.then_inc(S["y_done"], 1)
                turn(l, G_GROUP)
                pe.wait_ge(turned_lo, KD * (use(l, G_GROUP) + 1))
                for n in range(2):
                    for c in range(2):
                        arrived(c0 + 12 + 2 * n + c)
                        for k in range(4):
                            m = rows_times(c0 + 12 + 2 * n + c, 4 * k, 4, 4 * c + k, 2 + 3 * n, c == 0 and k == 0,
                                           c == 1 and k == 3)[-1]
                        m.then_inc(chunk_used, 1)
                turn(l, G_FFN)
                pe.wait_ge(turned_lo, KD * (use(l, G_FFN) + 1))

                if l == 0:
                    def up(f, j):
                        arrived(C_UP + f)
                        pe.wait_ge(S["H_out"], f + 1)
                        for k in range(KD):
                            for w in range(2):
                                m = mm3(bank[2 + 2 * (j % 2) + w][:, 0:NT], blk(whi, C_UP + j, 2 * k + w),
                                        blk(wlo, C_UP + j, 2 * k + w), hT_hi[:, k, :], hT_lo[:, k, :], k == 0, k == KD - 1)
                        m.then_inc(chunk_used, 1)
                    with T.Fori(0, NF // RAWS) as i:
                        for j in range(RAWS):
                            up(RAWS * i + j, j)
                    for f in range(NF // RAWS * RAWS, NF):
                        up(f, f)
                    pe.wait_ge(S["H_out"], NF + 2)

                    def down(i, j):
                        pe.wait_ge(S["yT_out"], 4 * i + j + 1)
                        for f in range(NF):
                            b = DOWN_BLOCKS * j + f
                            if b % 16 == 0 or f == 0:
                                arrived(C_DOWN + RAWS * i + b // 16)
                            m = mm3(bank[6 + j % 2][:, 0:NT], blk(whi, C_DOWN + b // 16, b % 16),
                                    blk(wlo, C_DOWN + b // 16, b % 16), HT_hi[:, f, :], HT_lo[:, f, :], f == 0, f == NF - 1)
                            if b % 16 == 15 or (f == NF - 1 and j % 2):
                                m.then_inc(chunk_used, 1)
                        if j % 2 == 0:
                            m.then_inc(S["yT_done"], 1)

                    def turn_back(i, j):
                        pe.wait_ge(S["yT_out"], 4 * i + j + 3)
                        pe.wait_ge(S["x_dense"], 4 * i + j + 1)
                        for t in range(3):
                            r = ROWS[t]
                            last = T.transpose(bank[j % 2][0:r, t * P:(t + 1) * P], yT[:, j % 2, t * P:t * P + r], ident)
                        last.then_inc(S["y_turned"], 1)
                    with T.Fori(0, DOWN_CH // RAWS) as i:
                        down(i, 0)
                        down(i, 1)
                        turn_back(i, 0)
                        down(i, 2)
                        turn_back(i, 1)
                        down(i, 3)
                        turn_back(i, 2)
                        turn_back(i, 3)

            pe.wait_ge(S["rt_out"], 1)
            for t in range(3):
                r = ROWS[t]
                at = bank[2][0:r, t * NE:(t + 1) * NE]
                for k in range(KD):
                    hi_, lo_ = hT_hi[:, k, t * P:t * P + r], hT_lo[:, k, t * P:t * P + r]
                    mm3(at, hi_, lo_, rt_hi[:, k, :], rt_lo[:, k, :], k == 0, False)
                    last = T.matmul(at, lo_, rt_lo[:, k, :], start=False, stop=k == KD - 1)
            last.then_inc(S["logit_done"], 1)
            pe.wait_ge(S["pos_in"], 1)
            for t in range(3):
                r = ROWS[t]
                for s_ in range(t):
                    T.matmul(bank[3][0:r, t * NE:(t + 1) * NE], ones[:, 0:r], mask[:, s_, :], start=s_ == 0, stop=False)
                T.matmul(bank[3][0:r, t * NE:(t + 1) * NE], before[0:r, 0:r], mask[0:r, t, :], start=t == 0, stop=True)
            for t in range(3):
                r = ROWS[t]
                last = T.matmul(bank[3][0:1, 3 * NE:4 * NE], ones[0:r, 0:1], mask[0:r, t, :], start=t == 0, stop=t == 2)
            last.then_inc(S["pos_done"], 1)

            pe.wait_ge(S["rounds_ok"], 1)
            pe.wait_ge(S["xm_out"], 1)
            n_rounds = T.value_load(rounds[0:1, 0:1], min_val=1, max_val=MAX_ROUNDS)
            with T.Fori(0, n_rounds) as r:
                def regs(e):
                    q = T.snap(r * NE + e)
                    return q, T.snap(q * EXP_CH + (C_MOE + 2)), T.snap(q * STEPS)

                def gather(b):
                    for k in range(4 * b, 4 * b + 4):
                        for t in range(3):
                            rr = ROWS[t]
                            last = T.matmul(bank[b][:, (k % 4) * P:(k % 4 + 1) * P], xm[0:rr, t, k * P:(k + 1) * P],
                                            sel[0:rr, t, :], start=t == 0, stop=t == 2)
                    last.then_inc(S["gat_done"], 1)

                def turn_sel(q):
                    pe.wait_ge(S["gat_lo"], 2 * q + 2)
                    for t in range(3):
                        rr = ROWS[t]
                        last = T.transpose(bank[0][:, t * P:t * P + rr], sel[0:rr, t, :], ident[0:rr, 0:rr])
                    last.then_inc(S["selT_done"], 1)

                def gate_up(cb, off, s, half_, j, extra=0):
                    pe.wait_ge(lo_ready, cb + off + 1 + RAWS * extra)
                    for k in range(4):
                        kk = 4 * half_ + k
                        m = mm3(bank[2 + s % 2][:, :], gT_hi[:, j, kk, :], gT_lo[:, j, kk, :], blk(whi, off + 2, 4 * k, 4),
                                blk(wlo, off + 2, 4 * k, 4), kk == 0, kk == KD - 1)
                    m.then_inc(chunk_used, 1)

                def turn_hidden(g0, s, extra=0):
                    pe.wait_ge(S["eh_out"], g0 + s + 1 + 2 * extra)
                    for b in range(2):
                        last = T.transpose(bank[4 + s % 2][:, b * P:(b + 1) * P], eh[:, s % 2, b * P:(b + 1) * P], ident)
                    last.then_inc(S["eT_done"], 1)

                def down(cb, g0, off, s, extra=0):
                    pe.wait_ge(lo_ready, cb + off + 1 + RAWS * extra)
                    pe.wait_ge(S["eT_out"], g0 + s + 1 + 2 * extra)
                    for b in range(2):
                        for n in range(2):
                            m = mm3(bank[6 + n][:, :], eT_hi[:, s % 2, b, :], eT_lo[:, s % 2, b, :],
                                    blk(whi, off + 2, 8 * b + 4 * n, 4), blk(wlo, off + 2, 8 * b + 4 * n, 4),
                                    s % STEPS == 0 and b == 0, s == STEPS - 1 and b == 1, skip_group_check=True)
                    m.then_inc(chunk_used, 1)

                def scatter(q, j, *ms_):
                    for m_ in ms_:
                        t, n = m_ // 2, m_ % 2
                        rr = ROWS[t]
                        pe.wait_ge(S["x_added"], 6 * q + m_ + 1)
                        T.matmul(bank[n][0:rr, :], selT[:, j, t * P:t * P + rr], y_hi[:, n * 512:(n + 1) * 512],
                                 start=True, stop=False)
                        T.matmul(bank[n][0:rr, :], selT[:, j, t * P:t * P + rr], y_lo[:, n * 512:(n + 1) * 512],
                                 start=False, stop=True).then_inc(S["scat_done"], 1)

                def step(cb, g0, s, j, extra=0):
                    gate_up(cb, 3 * s, s + 1, 0, j, extra)
                    turn_hidden(g0, s, extra)
                    gate_up(cb, 3 * s + 1, s + 1, 1, j, extra)
                    down(cb, g0, 3 * s + 2, s, extra)

                def expert(e, j, last):
                    q, cb, g0 = regs(e)
                    with T.Fori(0, STEPS // 2 - 2) as p:
                        step(cb, g0, 2, j, p)
                        step(cb, g0, 3, j, p)
                    s = STEPS - 2
                    if last:
                        step(cb, g0, s, j)
                        turn_hidden(g0, s + 1)
                        down(cb, g0, 3 * s + 3, s + 1)
                        pe.wait_ge(S["y_out"], q + 1)
                        pe.wait_ge(S["selT_out"], q + 1)
                        scatter(q, j, 0, 1, 2, 3, 4, 5)
                        return
                    pe.wait_ge(S["sel_out"], q + 2)
                    pe.wait_ge(S["selT_out"], q + 1)
                    pe.wait_ge(S["x_added"], 6 * q + 2)
                    gather(0)
                    gate_up(cb, 3 * s, s + 1, 0, j)
                    turn_hidden(g0, s)
                    gather(1)
                    gate_up(cb, 3 * s + 1, s + 1, 1, j)
                    down(cb, g0, 3 * s + 2, s)
                    s = STEPS - 1
                    pe.wait_ge(S["gat_lo"], 2 * q + 4)
                    gate_up(cb, 3 * s, s + 1, 0, 1 - j)
                    turn_hidden(g0, s)
                    turn_sel(q + 1)
                    gate_up(cb, 3 * s + 1, s + 1, 1, 1 - j)
                    down(cb, g0, 3 * s + 2, s)
                    s = STEPS
                    gate_up(cb, 3 * s, s + 1, 0, 1 - j)
                    turn_hidden(g0, s)
                    gate_up(cb, 3 * s + 1, s + 1, 1, 1 - j)
                    pe.wait_ge(S["y_out"], q + 1)
                    pe.wait_ge(S["selT_out"], q + 2)
                    scatter(q, j, 0, 1)
                    down(cb, g0, 3 * s + 2, s)
                    s = STEPS + 1
                    gate_up(cb, 3 * s, s + 1, 0, 1 - j)
                    scatter(q, j, 2, 3)
                    turn_hidden(g0, s)
                    gate_up(cb, 3 * s + 1, s + 1, 1, 1 - j)
                    scatter(q, j, 4, 5)
                    down(cb, g0, 3 * s + 2, s)

                q, cb, g0 = regs(0)
                pe.wait_ge(S["sel_out"], q + 1)
                pe.wait_ge(S["x_added"], 6 * q + 2)
                gather(0)
                gather(1)
                turn_sel(q)
                gate_up(cb, -2, 0, 0, 0)
                gate_up(cb, -1, 0, 1, 0)
                step(cb, g0, 0, 0)
                step(cb, g0, 1, 0)
                with T.Fori(0, NE // 2 - 1) as pair:
                    for j in range(2):
                        expert(2 * pair + j, j, False)
                for j in range(2):
                    expert(NE - 2 + j, j, j == 1)


def _pool_tables():
    full = np.zeros((4, SEQ, SEQ), np.float32)
    req = np.zeros((4, PBUF + REQT, REQT), np.float32)
    for g, w in enumerate(WINDOWS):
        for t in range(SEQ):
            first = max(0, t - w + 1)
            full[g, first:t + 1, t] = 1.0 / (t + 1 - first)
            full[g, t, t] -= 1.0
        for t in range(REQT):
            req[g, PBUF + t - w + 1:PBUF + t + 1, t] = 1.0 / w
            req[g, PBUF + t, t] -= 1.0
    own = np.zeros((4, NS, NS), np.float32)
    old = np.zeros((4, NREQ * PBUF, NS), np.float32)
    for b in range(NREQ):
        own[:, b * REQT:(b + 1) * REQT, b * REQT:(b + 1) * REQT] = req[:, PBUF:]
        old[:, b * PBUF:(b + 1) * PBUF, b * REQT:(b + 1) * REQT] = req[:, :PBUF]
    return full, own, old


def _constants(v):
    table = np.zeros((P, N_CONST), np.float32)

    def put(name, a):
        a = np.asarray(a).reshape(a.shape[0], -1)
        lo, hi = COL[name]
        assert a.shape[1] == hi - lo, name
        table[:a.shape[0], lo:hi] = a

    put("ident", np.eye(P, dtype=np.float32))
    g = np.stack([v["g_mem"], v["g_mix_norm"], v["g_group"], v["g_ffn_norm"]], 1)
    put("gains", g.reshape(DEPTH, 4, KD, P).transpose(3, 0, 1, 2))
    full, own, old = _pool_tables()
    put("pool0", full[:, 0:P].transpose(1, 0, 2))
    put("pool1", full[:, P:, P:].transpose(1, 0, 2))
    put("pool_s", own.transpose(1, 0, 2))
    put("pool_st", old.transpose(1, 0, 2))
    bias = np.zeros((P, DEPTH, 2, AH), np.float32)
    bias[:, :, 0] = v["b_spatial"].transpose(2, 0, 1)
    bias[:NS, :, 1] = np.tile(v["b_spatial"][:, :, :REQT].transpose(2, 0, 1), (NREQ, 1, 1))
    put("bias", bias)
    fold = np.zeros((NREQ, HEADS, REQT, HEADS, NREQ, REQT), np.float32)
    for b in range(NREQ):
        for h in range(HEADS):
            fold[b, h, :, h, b, :] = np.eye(REQT)
    put("fold", fold.reshape(P, -1))
    put("w_pool", v["w_pool"].transpose(2, 0, 1, 3))
    put("w_sp", v["w_spatial"].transpose(3, 0, 1, 2))
    small = np.zeros((NS, DEPTH, AH, NS), np.float32)
    for b in range(NREQ):
        at = slice(b * REQT, (b + 1) * REQT)
        small[at, :, :, at] = v["w_spatial"][:, :, :REQT, :REQT].transpose(3, 0, 1, 2)
    put("w_sps", small)
    put("g_v", np.tile(v["g_v"].reshape(1, -1), (P, 1)))
    put("s_pool", np.tile(v["s_pool"].reshape(1, -1), (P, 1)))
    return table


def _late(v):
    router = v["w_router"][0].reshape(KD, P, NE).transpose(1, 0, 2).reshape(P, KD * NE)
    return np.concatenate([np.triu(np.ones((P, P), np.float32), 1), np.ones((P, P), np.float32),
                           np.tile(np.arange(P, dtype=np.float32), (P, 1)), router], axis=1)


def _stream(v):
    out = np.zeros((N_CH, P, CW), np.float32)
    n = 0

    def put(a):
        nonlocal n
        out[n:n + len(a), :, :a.shape[2]] = a
        n += len(a)

    def columns4(w):
        m = w.shape[1] // 512
        return w.reshape(2, 4, P, m, 512).transpose(3, 0, 2, 1, 4).reshape(2 * m, P, CW)

    for l in range(DEPTH):
        put(columns4(v["w_mem_kv"][l]))
        w = v["w_in"][l].reshape(KD, P, -1)
        put(w[:, :, 2 * DA + DB:].transpose(1, 0, 2).reshape(1, P, CW))
        put(v["cache_mem_k"][l].reshape(2, 4, NMEM, 2, P).transpose(0, 4, 1, 3, 2).reshape(2, P, CW))
        rows = np.concatenate([w[:, :, DA:2 * DA], w[:, :, 2 * DA:2 * DA + DB], w[:, :, 0:DA]])
        for a, b in ((0, 5), (5, 10), (10, 15), (15, 20), (20, 24)):
            put(rows[a:b].transpose(1, 0, 2).reshape(1, P, -1))
        put(v["cache_mem_v"][l].reshape(2, 4, 2, P, DX).transpose(0, 3, 1, 2, 4).reshape(2, P, CW))
        put(columns4(v["w_out"][l]))
        if l == 0:
            gu = np.stack([v["w_dense_gate"][0], v["w_dense_up"][0]]).reshape(2, KD, P, NF, P)
            put(gu.transpose(3, 2, 1, 0, 4).reshape(NF, P, CW))
            d = np.zeros((KD, DOWN_BLOCKS, P, P), np.float32)
            d[:, :NF] = v["w_dense_down"][0].reshape(NF, P, KD, P).transpose(2, 0, 1, 3)
            put(d.reshape(DOWN_CH, 16, P, P).transpose(0, 2, 1, 3).reshape(DOWN_CH, P, CW))
    assert n == C_MOE
    gate_up, down = [], []
    for e in range(NE):
        gu = np.stack([v["w_moe_gate"][0, e], v["w_moe_up"][0, e]])
        gate_up.append(gu.reshape(2, 2, 4, P, STEPS, 256).transpose(4, 1, 3, 2, 0, 5).reshape(STEPS, 2, P, CW))
        down.append(v["w_moe_down"][0, e].reshape(STEPS, 2, P, D).transpose(0, 2, 1, 3).reshape(STEPS, 1, P, CW))
    gate_up, down = np.concatenate(gate_up), np.concatenate(down)
    put(gate_up[0])
    for s in range(NE * STEPS):
        if s + 1 < NE * STEPS:
            put(gate_up[s + 1])
        put(down[s])
    assert n == N_CH
    return out.reshape(N_CH * P, CW)


def kernel(**inputs):
    import concourse.bacc as bacc
    from concourse.bass_utils import run_bass_kernel_spmd

    v = {k: np.asarray(a) for k, a in inputs.items()}
    arrays = {
        "stream": _stream(v),
        "const": _constants(v),
        "late": _late(v),
        "mem": v["mem_prompt"].reshape(NMEM, D),
        "x_prompt": v["x_prompt"].reshape(SEQ, D),
        "x_sample": v["x_sample"].reshape(NS, D),
        "state": v["state_pool"].reshape(DEPTH, NREQ * PBUF, DB),
        "g_moe": np.tile(v["g_ffn_norm"][DEPTH - 1].reshape(1, D), (P, 1)),
        "g_final": np.tile(v["g_final"].reshape(1, D), (P, 1)),
    }
    outs = {
        "y_prompt": (SEQ, D), "y_sample": (NS, D), "pool_prompt": (DEPTH, PBUF, DB), "mem_k": (DEPTH, NMEM, DX),
        "mem_v": (DEPTH, NMEM, DX), "pool_sample": (DEPTH, NREQ, PBUF, DB), "v_rows": (DEPTH, NS, DA),
    }
    nc = bacc.Bacc("TRN2", target_bir_lowering=False, num_devices=1)
    io = {}
    for name, a in arrays.items():
        arrays[name] = np.ascontiguousarray(a)
        io[name] = nc.dram_tensor(f"in_{name}", a.shape, mybir.dt.float32, kind="ExternalInput").ap()
    for name, shape in outs.items():
        io[name] = nc.dram_tensor(f"out_{name}", shape, mybir.dt.float32, kind="ExternalOutput").ap()
    build(nc, io)
    r = run_bass_kernel_spmd(nc, [{f"in_{name}": a for name, a in arrays.items()}], core_ids=[0]).results[0]
    return (
        r["out_y_prompt"].reshape(1, SEQ, D), r["out_y_sample"].reshape(NREQ, REQT, D), r["out_pool_prompt"].reshape(DEPTH, 1, PBUF, DB),
        r["out_mem_k"].reshape(DEPTH, 1, NMEM, HEADS, HD), r["out_mem_v"].reshape(DEPTH, 1, NMEM, HEADS, HD), r["out_pool_sample"],
        r["out_v_rows"].reshape(DEPTH, NREQ, REQT, DA),
    )
```

```python
from contextlib import ExitStack

import concourse.bass as bass
import concourse.mybir as mybir
import numpy as np

D, SEQ, DEPTH, NREQ, REQT = 1024, 256, 2, 8, 4
DA = DB = 384
DX, HEADS, HD, NMEM = 256, 4, 64, 256
AH, AHD = 4, 96
WINDOWS, GD, PBUF = (2, 4, 8, 16), 96, 15
FF, NE, FFE = 2816, 8, 3584
EPS = 1e-6
P = 128
KD = D // P
NS = NREQ * REQT
NT = SEQ + NS
ROWS = (P, P, NS)
CW = 2048

RAWS, SPL = 6, 3
KV_CH, Q_CH, CK_CH, UV_CH, CV_CH, WO_CH = 2, 1, 2, 5, 2, 4
MIX_CH = Q_CH + CK_CH + UV_CH + CV_CH + WO_CH
NF = FF // P
UP_CH = NF
DOWN_BLOCKS = 24
DOWN_CH = KD * DOWN_BLOCKS // 16
C_UP = DEPTH * KV_CH + MIX_CH
C_DOWN = C_UP + UP_CH
C_MIX1 = C_DOWN + DOWN_CH
C_MOE = C_MIX1 + MIX_CH
C_LAYER = (DEPTH * KV_CH - KV_CH, C_MIX1 - KV_CH)
STEPS = FFE // 256
EXP_CH = 3 * STEPS
ROUND_CH = NE * EXP_CH
N_CH = C_MOE + ROUND_CH
DIAG = P + HEADS * REQT
MAX_ROUNDS = -(-NT // P)
FAR = 8192.0
NEVER = -3.0e38
NORMS = 8
N_MEM, N_MIX, N_V, N_A, N_B, N_O, N_FFN, N_FFN2 = range(NORMS)
EVENTS = 8
E_MIX01, E_MIX2, E_V, E_A, E_B, E_O, E_FFN01, E_FFN2 = range(1, EVENTS + 1)
R_MIX, R_A, R_B, R_O, R_FFN = range(1, 6)
TURNS = DEPTH + 3 * DEPTH
LAYER_STORES, MEM_STORES = 4, 2 * DEPTH

def _columns():
    at, n = {}, 0
    for name, width in (("ident", P), ("gains", DEPTH * 4 * KD),
                        ("pool0", 4 * SEQ), ("pool1", 4 * P), ("pool_s", 4 * NS), ("pool_st", 4 * NS),
                        ("bias", DEPTH * 2 * AH), ("fold", HEADS * NS),
                        ("before", P), ("ones", P), ("slots", P), ("router", KD * NE)):
        at[name] = (n, n + width)
        n += width
    return at, n


COL, N_CONST = _columns()
N_FIRST = COL["gains"][1]
W_POOL, W_SP, W_SPS, G_V, S_POOL = 4 * GD, AH * P, AH * NS, DA, DB
N_LAYER = W_POOL + W_SP + W_SPS + G_V + S_POOL
G_MEM, G_MIX, G_GROUP, G_FFN = range(4)


def build(nc, io):
    F, FR, I32 = mybir.dt.float32, mybir.dt.float32r, mybir.dt.int32
    ACT, ALU, AX = mybir.ActivationFunctionType, mybir.AluOpType, mybir.AxisListType
    ctx = ExitStack()
    with ctx:
        sb = lambda n, s, d=F: ctx.enter_context(nc.sbuf_tensor(n, s, d))
        sem = lambda n: ctx.enter_context(nc.semaphore(n))

        raw = sb("raw", [P, RAWS, CW])
        whi = sb("whi", [P, SPL, CW], FR)
        wlo = sb("wlo", [P, SPL, CW], FR)
        x = sb("x", [P, 3, D])
        hT_hi = sb("hT_hi", [P, KD, NT], FR)
        hT_lo = sb("hT_lo", [P, KD, NT], FR)
        const = sb("const", [P, N_CONST])
        ss = sb("ss", [P, NORMS, 3])
        ms = sb("ms", [P, NORMS, 3])
        rstd = sb("rstd", [P, NORMS, 3])
        half = sb("half", [P, 3])
        kv = sb("kv", [P, DEPTH, 2, 2 * DX])
        rt_hi = sb("rt_hi", [P, KD, NE], FR)
        rt_lo = sb("rt_lo", [P, KD, NE], FR)
        junk = sb("junk", [P, D], mybir.dt.bfloat16)

        def phase():
            return ExitStack()

        with phase() as room:
            ph = lambda n, s, d=F: room.enter_context(nc.sbuf_tensor(n, s, d))
            xn = ph("xn", [P, 3, D])
            stage = ph("stage", [P, 6, DA])
            table = ph("table", [P, N_LAYER])
            kT = ph("kT", [P, 2, NMEM])
            qT = ph("qT", [P, 2, SEQ])
            state = ph("state", [NREQ * PBUF, DB])
            sP = ph("sP", [P, NMEM])
            mx = ph("mx", [P, 9])
            nmx = ph("nmx", [P, 9])
            den = ph("den", [P, 9])
            rden = ph("rden", [P, 9])
            with phase() as first_half:
                ph = lambda n, s, d=F: first_half.enter_context(nc.sbuf_tensor(n, s, d))
                qs_hi = ph("qs_hi", [P, 2, NREQ * DIAG], FR)
                qs_lo = ph("qs_lo", [P, 2, NREQ * DIAG], FR)
            with phase() as second_half:
                ph = lambda n, s, d=F: second_half.enter_context(nc.sbuf_tensor(n, s, d))
                PT = ph("PT", [P, 2, 4, P])
                xb = ph("xb", [P, 3, DB])
                dT = ph("dT", [P, 4, NT])
                ob = ph("ob", [P, 3, DX])
                os_rows = ph("os_rows", [P, DX])
        qs = [t[:, :, :].rearrange("p f c -> p (f c)") for t in (qs_hi, qs_lo)]
        sPT = [t[:, :, :].rearrange("p k t -> p (k t)") for t in (hT_hi, hT_lo)]
        mem = stage[:, :, :].rearrange("p a b -> p (a b)")[:, 0:2 * D].rearrange("p (t d) -> p t d", t=2)
        b_rows = dT[:, :, :].rearrange("p a b -> p (a b)").rearrange("p (t d) -> p t d", t=3)
        vg, ug = stage[:, 0:3, :], stage[:, 3:6, :]
        prob = xn[:, :, :].rearrange("p a b -> p (a b)")[:, 0:8 * NMEM].rearrange("p (g m) -> p g m", g=8)

        with phase() as room:
            ph = lambda n, s, d=F: room.enter_context(nc.sbuf_tensor(n, s, d))
            HT_hi = ph("HT_hi", [P, NF, NT], FR)
            HT_lo = ph("HT_lo", [P, NF, NT], FR)
            sg = ph("sg", [P, 2, NT])
            hf = ph("hf", [P, 2, NT])
            yT = ph("yT", [P, 2, NT])

        with phase() as room:
            ph = lambda n, s, d=F: room.enter_context(nc.sbuf_tensor(n, s, d))
            xm = ph("xm", [P, 3, D])
            gT_hi = ph("gT_hi", [P, 2, KD, P], FR)
            gT_lo = ph("gT_lo", [P, 2, KD, P], FR)
            sel = ph("sel", [P, 3, P])
            selT = ph("selT", [P, 2, NT], FR)
            esg = ph("esg", [P, 2, 256])
            eh = ph("eh", [P, 2, 256])
            eT_hi = ph("eT_hi", [P, 2, 2, P], FR)
            eT_lo = ph("eT_lo", [P, 2, 2, P], FR)
            y_hi = ph("y_hi", [P, D], FR)
            y_lo = ph("y_lo", [P, D], FR)
            logitsT = ph("logitsT", [NE, NT])
            logits = ph("logits", [P, 3, NE])
            top = ph("top", [P, 3, 8])
            nfirst = ph("nfirst", [P, 3])
            left = ph("left", [P, 3, NE])
            mask = ph("mask", [P, 3, NE])
            expo = ph("expo", [P, 3, NE])
            gden = ph("gden", [P, 3])
            gate = ph("gate", [P, 3, NE])
            posm = ph("posm", [P, 3, NE])
            cmax = ph("cmax", [1, 1])
            over = ph("over", [1, 2])
            rounds = ph("rounds", [1, 1], I32)

        bank = [ctx.enter_context(nc.psum_tensor(f"bank{i}", [P, 512], F)) for i in range(8)]

        def C(name, rows=P):
            a, b = COL[name]
            return const[0:rows, a:b]

        ident = C("ident")
        gains = C("gains").rearrange("p (l g k) -> p l g k", l=DEPTH, g=4)
        g_rows = C("pool0")
        pool0 = C("pool0").rearrange("p (g t) -> p g t", g=4)
        pool1 = C("pool1").rearrange("p (g t) -> p g t", g=4)
        pool_s = C("pool_s", NS).rearrange("p (g t) -> p g t", g=4)
        pool_st = C("pool_st", NREQ * PBUF).rearrange("p (g t) -> p g t", g=4)
        bias = C("bias").rearrange("p (l s h) -> p l s h", l=DEPTH, s=2)
        fold = C("fold").rearrange("p (h t) -> p h t", h=HEADS)
        before, ones, slots = C("before"), C("ones"), C("slots")
        router = C("router").rearrange("p (k e) -> p k e", k=KD)
        at = 0
        parts = []
        for width in (W_POOL, W_SP, W_SPS, G_V, S_POOL):
            parts.append(table[:, at:at + width])
            at += width
        w_pool = parts[0][0:GD, :].rearrange("p (g d) -> p g d", g=4)
        w_sp = parts[1].rearrange("p (h t) -> p h t", h=AH)
        w_sps = parts[2][0:NS, :].rearrange("p (h t) -> p h t", h=AH)
        g_v, s_pool = parts[3], parts[4]

        raw_full = [sem(f"raw_full{i}") for i in range(RAWS)]
        hi_ready, lo_ready, chunk_used = sem("hi_ready"), sem("lo_ready"), sem("chunk_used")
        mem_in = [sem(f"mem_in{t}") for t in range(2)]
        first_in, table_in = sem("first_in"), sem("table_in")
        const_in, state_in, x_in, gain_in = (sem(n) for n in ("const_in", "state_in", "x_in", "gain_in"))
        preset, masked, zeroed = sem("preset"), sem("masked"), sem("zeroed")
        squares, rstd_ok, rows_ok = sem("squares"), sem("rstd_ok"), sem("rows_ok")
        turned, turned_hi, turned_lo = sem("turned"), sem("turned_hi"), sem("turned_lo")
        act_chain, dve_chain, pool_chain = sem("act_chain"), sem("dve_chain"), sem("pool_chain")
        S = {n: sem(n) for n in (
            "kv_out", "q_out", "qs_out", "kT_done", "kT_out", "sc_done", "max_out", "exp_done", "smax_out",
            "sexp_done", "v_done", "vg_out", "v_out", "xb_done", "xb_out", "PT_done", "PT_out", "sPT_done",
            "sPT_out", "ug_out", "o_done", "os_rows_out", "os_done", "o_out", "dT_done", "dT_out", "mix_done", "a_out",
            "y_done", "b_out", "op_out", "tile_done", "x_mixed", "silu_out", "hf_out", "H_out", "yT_done", "yT_out",
            "y_turned", "x_dense", "rt_out", "xm_out", "xm_tile1_out", "logit_done", "logitT_out", "logit_turned",
            "logit_out", "exp2_out", "pos_in", "pos_done", "rounds_ok", "pos_moved", "sel_out",
            "selT_done", "selT_out", "gat_done", "gat_hi", "gat_lo", "esilu", "eh_out", "eT_done", "eT_hi_out", "eT_out",
            "y_hi_out", "y_out", "scat_done", "x_added", "fin_out")}
        stored, final_stored = sem("stored"), sem("final_stored")

        block = ctx.enter_context(nc.Block())

        def load_chunk(sp, c, slot):
            c, row = c
            if not (isinstance(c, int) and c < RAWS):
                sp.wait_ge(lo_ready, c - RAWS + 1)
            sp.dma_start(raw[:, slot, :], io["stream"][bass.ds(row * P, P), :]).then_inc(raw_full[slot], 16)

        def split_hi(act, c, lap, slot):
            act.wait_ge(raw_full[slot], 16 * lap + 16)
            if not (isinstance(c, int) and c < SPL):
                act.wait_ge(chunk_used, c - SPL + 1)
            nc.scalar.activation(whi[:, slot % SPL, :], raw[:, slot, :], ACT.Copy).then_inc(hi_ready, 1)

        def split_lo(dve, c, slot):
            dve.wait_ge(hi_ready, c + 1)
            nc.vector.tensor_tensor(wlo[:, slot % SPL, :], raw[:, slot, :], whi[:, slot % SPL, :].bitcast(F),
                                    ALU.subtract).then_inc(lo_ready, 1)

        def hi_static(act, *cs):
            for c in cs:
                split_hi(act, c, c // RAWS, c % RAWS)

        def lo_static(dve, *cs):
            for c in cs:
                split_lo(dve, c, c % RAWS)

        def mm3(out, a_hi, a_lo, b_hi, b_lo, start, stop, **kw):
            nc.tensor.matmul(out, a_hi, b_hi, start=start, stop=False, **kw)
            nc.tensor.matmul(out, a_hi, b_lo, start=False, stop=False, **kw)
            return nc.tensor.matmul(out, a_lo, b_hi, start=False, stop=stop, **kw)

        def blk(ring, slot, b, n=1):
            return ring[:, slot % SPL, b * P:(b + n) * P]

        def own_columns(z):
            return z.rearrange("p (f b c) -> p f b c", f=2, c=DIAG)[:, :, :, 0:HEADS * REQT]

        def only(z, f, r):
            return z[:, f * NREQ * DIAG + r * P:f * NREQ * DIAG + (r + 1) * P]

        def use(l, which):
            return l if which == G_MEM else DEPTH + 3 * l + which - G_MIX

        def event(l, e):
            return 1 + EVENTS * l + e

        def ready(l, r):
            return 1 + 5 * l + r

        @block.sync
        def _(sp):
            sp.dma_start(const[:, 0:N_FIRST], io["const"][:, 0:N_FIRST]).then_inc(first_in, 16)
            for t in range(2):
                sp.dma_start(mem[:, t, :], io["mem"][t * P:(t + 1) * P, :]).then_inc(mem_in[t], 16)
            for c in (0, 1):
                load_chunk(sp, (c, c), c)
            sp.dma_start(x[:, 0:2, :], io["x_prompt"].rearrange("(t p) d -> p t d", p=P)).then_inc(x_in, 16)
            sp.dma_start(x[0:NS, 2, :], io["x_sample"]).then_inc(x_in, 16)
            for c in range(2, RAWS):
                load_chunk(sp, (c, c), c % RAWS)
            sp.dma_start(const[:, N_FIRST:], io["const"][:, N_FIRST:]).then_inc(const_in, 16)
            sp.dma_start(table[:, :], io["table"][0]).then_inc(table_in, 16)
            sp.dma_start(state[:, :], io["state"][0]).then_inc(state_in, 16)
            for c in range(RAWS, C_UP):
                load_chunk(sp, (c, c), c % RAWS)
            with nc.sync.Fori(0, UP_CH // RAWS) as i:
                for j in range(RAWS):
                    c = C_UP + RAWS * i + j
                    load_chunk(sp, (c, c), (C_UP + j) % RAWS)
            for c in range(C_UP + UP_CH // RAWS * RAWS, C_DOWN):
                load_chunk(sp, (c, c), c % RAWS)
            with nc.sync.Fori(0, DOWN_CH // RAWS) as i:
                for j in range(RAWS):
                    c = C_DOWN + RAWS * i + j
                    load_chunk(sp, (c, c), (C_DOWN + j) % RAWS)
            for c in range(C_MIX1, C_MIX1 + 2):
                load_chunk(sp, (c, c), c % RAWS)
            sp.wait_ge(S["x_dense"], KD + 2)
            sp.dma_start(table[:, :], io["table"][1]).then_inc(table_in, 16)
            sp.dma_start(state[:, :], io["state"][1]).then_inc(state_in, 16)
            for c in range(C_MIX1 + 2, C_MOE):
                load_chunk(sp, (c, c), c % RAWS)
            sp.wait_ge(S["dT_done"], 4 * DEPTH)
            sp.dma_start(g_rows, io["g_moe"]).then_inc(gain_in, 16)
            for c in range(C_MOE, C_MOE + RAWS):
                load_chunk(sp, (c, c), c % RAWS)
            sp.wait_ge(S["rounds_ok"], 1)
            n_rounds = nc.sync.value_load(rounds[0:1, 0:1], min_val=1, max_val=MAX_ROUNDS)
            with nc.sync.Fori(0, n_rounds) as r:
                done = nc.sync.snap(1 >> r)
                with nc.sync.Fori(done, ROUND_CH // RAWS) as i:
                    for j in range(RAWS):
                        row = C_MOE + RAWS * i + j
                        load_chunk(sp, (row + ROUND_CH * r, row), (C_MOE + j) % RAWS)
            sp.dma_start(g_rows, io["g_final"]).then_inc(gain_in, 16)
            for t in range(3):
                out = io["y_prompt"][t * P:(t + 1) * P, :] if t < 2 else io["y_sample"]
                sp.wait_ge(S["fin_out"], t + 1)
                sp.dma_start(out, xm[0:ROWS[t], t, :]).then_inc(final_stored, 16)
            sp.wait_ge(final_stored, 16 * 3)
            sp.wait_ge(stored, 16 * (MEM_STORES + DEPTH * LAYER_STORES))

        @block.gpsimd
        def _(pool):
            n_chain = [0]

            def link(ins):
                n_chain[0] += 1
                ins.then_inc(pool_chain, 1)
                pool.wait_ge(pool_chain, n_chain[0])

            nc.gpsimd.memset(ss[:, :, :], 1.0)
            nc.gpsimd.memset(half[:, :], -0.5).then_inc(preset, 1)
            pool.wait_ge(preset, 1)

            def power(done, n, width, a=0, b=3, second=None):
                pool.wait_ge(squares, done)
                sums = ss
                if second is not None:
                    link(nc.gpsimd.tensor_tensor(ms[:, n, a:b], ss[:, n, a:b], ss[:, second, a:b], ALU.add))
                    sums = ms
                link(nc.gpsimd.tensor_scalar(ms[:, n, a:b], sums[:, n, a:b], 1.0 / width, EPS, ALU.mult, ALU.add))
                nc.gpsimd.tensor_tensor(rstd[:, n, a:b], ms[:, n, a:b], half[:, a:b], ALU.pow).then_inc(rstd_ok, 1)

            def zero_pair(pair):
                for z in pair:
                    last = nc.gpsimd.memset(z.bitcast(F), 0.0)
                last.then_inc(zeroed, 1)

            def store(out, in_):
                pool.dma_start(out, in_).then_inc(stored, 16)

            zero_pair(qs)
            power(1, N_MEM, D)
            for l in range(DEPTH):
                second = N_FFN2 if l else None
                power(event(l, E_MIX01), N_MIX, D, 0, 2, second)
                power(event(l, E_MIX2), N_MIX, D, 2, 3, second)
                if l:
                    pool.wait_ge(S["x_dense"], KD + 2)
                    zero_pair(qs)
                pool.wait_ge(table_in, 16 * (l + 1))
                for h in range(AH):
                    for w, n in ((w_sp, P), (w_sps, NS)):
                        last = nc.gpsimd.affine_select(out=w[:, h, :], in_=w[:, h, :], compare_op=ALU.is_ge, fill=0.0, base=0,
                                                       pattern=[[1, n]], channel_multiplier=-1)
                last.then_inc(masked, 1)
                if l == 0:
                    for k in range(DEPTH):
                        pool.wait_ge(S["kv_out"], k + 1)
                        store(io["mem_k"][k].rearrange("(t p) d -> p t d", p=P), kv[:, k, :, 0:DX])
                        store(io["mem_v"][k].rearrange("(t p) d -> p t d", p=P), kv[:, k, :, DX:2 * DX])
                power(event(l, E_V), N_V, DA)
                pool.wait_ge(S["xb_out"], l + 1)
                store(io["pool_prompt"][l], xb[P - PBUF:P, 1, :])
                store(io["pool_sample"][l, :, PBUF - REQT:PBUF, :], xb[0:NS, 2, :])
                store(io["pool_sample"][l, :, 0:PBUF - REQT, :],
                      io["state"][l].rearrange("(b r) d -> b r d", r=PBUF)[:, REQT:PBUF, :])
                pool.wait_ge(chunk_used, C_LAYER[l] + 10)
                zero_pair(sPT)
                pool.wait_ge(S["v_out"], l + 1)
                store(io["v_rows"][l], vg[0:NS, 2, :])
                power(event(l, E_A), N_A, DA)
                power(event(l, E_B), N_B, DB)
                power(event(l, E_O), N_O, DX)
                power(event(l, E_FFN01), N_FFN, D, 0, 2, N_FFN2)
                power(event(l, E_FFN2), N_FFN, D, 2, 3, N_FFN2)
            pool.wait_ge(turned_lo, KD * TURNS)
            pool.wait_ge(stored, 16 * (MEM_STORES + LAYER_STORES * DEPTH))
            pool.wait_ge(gain_in, 16)
            link(nc.gpsimd.tensor_scalar(xm[:, 1, :], x[:, 1, :], rstd[:, N_FFN, 1:2], None, ALU.mult))
            nc.gpsimd.tensor_tensor(xm[:, 1, :], xm[:, 1, :], g_rows, ALU.mult).then_inc(S["xm_tile1_out"], 1)
            for t in range(3):
                power(event(DEPTH, 1 + t), N_MEM, D, t, t + 1)

        @block.scalar
        def _(act):
            n_chain = [0]

            def link(ins):
                n_chain[0] += 1
                ins.then_inc(act_chain, 1)
                act.wait_ge(act_chain, n_chain[0])

            def sum_squares(src, n, tiles=(0, 1, 2), signal=True):
                for t in tiles:
                    r = ROWS[t]
                    last = nc.scalar.activation(junk[0:r, 0:src.shape[-1]], src[0:r, t, :], ACT.Square,
                                                accum_out=ss[0:r, n, t:t + 1])
                    link(last)
                if signal:
                    act.sem_inc(squares, 1)

            def turn_hi(l, which, n_tok, blocks=range(KD)):
                for k in blocks:
                    act.wait_ge(turned, KD * use(l, which) + k + 1)
                    nc.scalar.activation(hT_hi[:, k, 0:n_tok], bank[k % 2][:, 0:n_tok], ACT.Copy,
                                         scale=gains[:, l, which, k:k + 1]).then_inc(turned_hi, 1)

            def keep_kv(l):
                for t in range(2):
                    last = nc.scalar.activation(kv[:, l, t, :], bank[(2, 6)[l] + t][:, :], ACT.Copy)
                last.then_inc(S["kv_out"], 1)

            act.wait_ge(preset, 1)
            for t in range(2):
                act.wait_ge(mem_in[t], 16)
                sum_squares(mem, N_MEM, (t,), signal=t == 1)
            act.wait_ge(first_in, 16)
            turn_hi(0, G_MEM, NMEM, (0, 1))
            hi_static(act, 0)
            turn_hi(0, G_MEM, NMEM, (2, 3))
            hi_static(act, 1)
            turn_hi(0, G_MEM, NMEM, (4,))
            act.wait_ge(x_in, 32)
            sum_squares(x, N_MIX, (0, 1))
            turn_hi(0, G_MEM, NMEM, (5, 6))
            sum_squares(x, N_MIX, (2,))
            turn_hi(0, G_MEM, NMEM, (7,))
            hi_static(act, 2)
            act.wait_ge(chunk_used, KV_CH)
            turn_hi(1, G_MEM, NMEM, (0, 1, 2))
            hi_static(act, 3)
            turn_hi(1, G_MEM, NMEM, (3, 4, 5))
            hi_static(act, 4)
            turn_hi(1, G_MEM, NMEM, (6, 7))
            keep_kv(0)
            for l in range(DEPTH):
                c0 = C_LAYER[l]
                if l:
                    act.wait_ge(S["x_dense"], KD + 2)
                    sum_squares(x[:, :, D - 2 * P:D], N_FFN2, (0, 1))
                    sum_squares(x[:, :, D - 2 * P:D], N_FFN2, (2,))
                act.wait_ge(chunk_used, c0 + KV_CH)
                turn_hi(l, G_MIX, NT)
                if l == 0:
                    keep_kv(1)
                if l == 0:
                    hi_static(act, c0 + 3)
                hi_static(act, c0 + 4, c0 + 5)
                for n, i in enumerate((2, 3, 0, 1)):
                    act.wait_ge(S["max_out"], 4 * l + n + 1)
                    for g in (2 * i, 2 * i + 1):
                        last = nc.scalar.activation(prob[:, g, :], bank[4 + i][:, (g % 2) * NMEM:(g % 2 + 1) * NMEM],
                                                    ACT.Exp, bias=nmx[:, g:g + 1], accum_out=den[:, g:g + 1])
                    last.then_inc(S["exp_done"], 1)
                hi_static(act, c0 + 6)
                act.wait_ge(S["smax_out"], l + 1)
                nc.scalar.activation(sP[:, :], bank[3][:, 0:NMEM], ACT.Exp, bias=nmx[:, 8:9],
                                     accum_out=den[:, 8:9]).then_inc(S["sexp_done"], 1)
                hi_static(act, c0 + 7)
                for t in range(3):
                    act.wait_ge(S["v_done"], 3 * l + t + 1)
                    last = nc.scalar.activation(vg[0:ROWS[t], t, :], bank[t][0:ROWS[t], 0:DA], ACT.Gelu_apprx_tanh)
                last.then_inc(S["vg_out"], 1)
                act.wait_ge(S["vg_out"], l + 1)
                sum_squares(vg, N_V)
                hi_static(act, c0 + 8, c0 + 9)
                act.wait_ge(chunk_used, c0 + 10)
                for t in range(3):
                    last = nc.scalar.activation(ug[0:ROWS[t], t, :], bank[t][0:ROWS[t], 0:DA], ACT.Gelu_apprx_tanh)
                last.then_inc(S["ug_out"], 1)
                hi_static(act, c0 + 10)
                for g in range(4):
                    act.wait_ge(S["dT_done"], 4 * l + g + 1)
                    last = nc.scalar.activation(dT[0:GD, g, :], bank[g][0:GD, 0:NT], ACT.Copy)
                last.then_inc(S["dT_out"], 1)
                hi_static(act, c0 + 11, c0 + 12)
                act.wait_ge(S["a_out"], l + 1)
                sum_squares(ug, N_A)
                act.wait_ge(S["b_out"], l + 1)
                sum_squares(b_rows, N_B)
                act.wait_ge(chunk_used, c0 + 12)
                nc.scalar.activation(os_rows[:, :], bank[6][:, 0:DX], ACT.Copy, scale=rden[:, 8:9])\
                    .then_inc(S["os_rows_out"], 1)
                turn_hi(l, G_GROUP, NT, (0, 1))
                hi_static(act, c0 + 13)
                act.wait_ge(S["os_done"], l + 1)
                nc.scalar.activation(ob[0:NS, 2, :], bank[7][0:NS, 0:DX], ACT.Copy).then_inc(S["o_out"], 1)
                act.wait_ge(S["op_out"], l + 1)
                act.wait_ge(S["o_out"], l + 1)
                sum_squares(ob, N_O)
                turn_hi(l, G_GROUP, NT, (2, 3, 4, 5))
                hi_static(act, c0 + 14)
                turn_hi(l, G_GROUP, NT, (6, 7))
                hi_static(act, c0 + 15)
                if l == 0:
                    hi_static(act, C_UP)
                act.wait_ge(S["x_mixed"], 6 * l + 3)
                sum_squares(x[:, :, 0:512], N_FFN, signal=False)
                if l == 0:
                    hi_static(act, C_UP + 1)
                for t in range(3):
                    act.wait_ge(S["x_mixed"], 6 * l + 4 + t)
                    sum_squares(x[:, :, 512:D], N_FFN2, (t,), signal=t > 0)
                turn_hi(l, G_FFN, NT)

                if l == 0:
                    with nc.scalar.Fori(0, NF // RAWS) as i:
                        for j in range(RAWS):
                            c = C_UP + 2 + RAWS * i + j
                            at = C_UP + 2 + j
                            split_hi(act, c, i + at // RAWS, at % RAWS)
                            act.wait_ge(chunk_used, C_UP + RAWS * i + j + 1)
                            nc.scalar.activation(sg[:, j % 2, :], bank[2 + 2 * (j % 2)][:, 0:NT], ACT.Silu)\
                                .then_inc(S["silu_out"], 1)
                    for f in range(NF // RAWS * RAWS, NF):
                        hi_static(act, C_UP + 2 + f)
                        act.wait_ge(chunk_used, C_UP + f + 1)
                        nc.scalar.activation(sg[:, f % 2, :], bank[2 + 2 * (f % 2)][:, 0:NT], ACT.Silu)\
                            .then_inc(S["silu_out"], 1)
                    act.sem_inc(S["yT_out"], 2)
                    for i in range(DOWN_CH // RAWS):
                        for what in (2, 3, "y0", 4, "y1", 5, 6, "y2", 7, "y3"):
                            if isinstance(what, int):
                                hi_static(act, C_DOWN + RAWS * i + what)
                                continue
                            j = int(what[1])
                            if 4 * i + j == KD - 1:
                                act.wait_ge(S["x_dense"], KD)
                                sum_squares(x[:, :, 0:D - 2 * P], N_MIX, signal=False)
                            if j % 2:
                                act.wait_ge(chunk_used, C_DOWN + RAWS * i + 3 * (j + 1) // 2)
                            else:
                                act.wait_ge(S["yT_done"], 2 * i + j // 2 + 1)
                            nc.scalar.activation(yT[:, j % 2, :], bank[6 + j % 2][:, 0:NT], ACT.Copy)\
                                .then_inc(S["yT_out"], 1)

            for t in range(3):
                r = ROWS[t]
                act.wait_ge(S["logit_out"], 1)
                last = nc.scalar.activation(expo[0:r, t, :], logits[0:r, t, :], ACT.Exp, bias=nfirst[0:r, t:t + 1])
            last.then_inc(S["exp2_out"], 1)
            act.wait_ge(S["rounds_ok"], 1)
            n_rounds = nc.scalar.value_load(rounds[0:1, 0:1], min_val=1, max_val=MAX_ROUNDS)
            with nc.scalar.Fori(0, n_rounds) as r:
                def regs(e):
                    q = nc.scalar.snap(r * NE + e)
                    return (q, nc.scalar.snap(q * EXP_CH + (C_MOE + 2)),
                            nc.scalar.snap(q * (EXP_CH // RAWS) + C_MOE // RAWS), nc.scalar.snap(q * STEPS))

                def hi(cb, lap, off, extra=0):
                    split_hi(act, cb + off + RAWS * extra, lap + (off + 2) // RAWS + extra, (off + 2) % RAWS)

                def gathered_hi(q, j, b):
                    act.wait_ge(S["gat_done"], 2 * q + b + 1)
                    nc.scalar.activation(gT_hi[:, j, 4 * b:4 * b + 4, :].rearrange("p a b -> p (a b)"), bank[b][:, :],
                                         ACT.Copy).then_inc(S["gat_hi"], 1)

                def silu_of(cb, s, extra=0):
                    act.wait_ge(chunk_used, cb + 3 * s - 1 + RAWS * extra)
                    nc.scalar.activation(esg[:, s % 2, :], bank[2 + s % 2][:, 0:256], ACT.Silu).then_inc(S["esilu"], 1)

                def turned_of(g0, s, extra=0):
                    act.wait_ge(S["eT_done"], g0 + s + 1 + 2 * extra)
                    nc.scalar.activation(eT_hi[:, s % 2, :, :].rearrange("p a b -> p (a b)"), bank[4 + s % 2][:, 0:256],
                                         ACT.Copy).then_inc(S["eT_hi_out"], 1)

                def y_hi_of():
                    for n in range(2):
                        nc.scalar.activation(y_hi[:, n * 512:(n + 1) * 512], bank[6 + n][:, :], ACT.Copy)\
                            .then_inc(S["y_hi_out"], 1)

                def step(cb, lap, g0, s, extra=0):
                    silu_of(cb, s, extra)
                    hi(cb, lap, 3 * s + 2, extra)
                    turned_of(g0, s, extra)
                    hi(cb, lap, 3 * s + 3, extra)
                    hi(cb, lap, 3 * s + 4, extra)

                def expert(e, j, last):
                    q, cb, lap, g0 = regs(e)
                    with nc.scalar.Fori(0, STEPS // 2 - 2) as p:
                        step(cb, lap, g0, 2, p)
                        step(cb, lap, g0, 3, p)
                    s = STEPS - 2
                    silu_of(cb, s)
                    hi(cb, lap, 3 * s + 2)
                    if last:
                        turned_of(g0, s)
                        hi(cb, lap, 3 * s + 3)
                        silu_of(cb, s + 1)
                        turned_of(g0, s + 1)
                        act.wait_ge(chunk_used, cb + EXP_CH - 2)
                        y_hi_of()
                        return
                    gathered_hi(q + 1, 1 - j, 0)
                    turned_of(g0, s)
                    gathered_hi(q + 1, 1 - j, 1)
                    hi(cb, lap, 3 * s + 3)
                    hi(cb, lap, 3 * s + 4)
                    step(cb, lap, g0, s + 1)
                    s = STEPS
                    silu_of(cb, s)
                    act.wait_ge(chunk_used, cb + EXP_CH)
                    y_hi_of()
                    hi(cb, lap, 3 * s + 2)
                    turned_of(g0, s)
                    hi(cb, lap, 3 * s + 3)
                    hi(cb, lap, 3 * s + 4)
                    step(cb, lap, g0, s + 1)

                q, cb, lap, g0 = regs(0)
                for off in (-2, -1, 0):
                    hi(cb, lap, off)
                for b in range(2):
                    gathered_hi(q, 0, b)
                hi(cb, lap, 1)
                act.wait_ge(chunk_used, cb)
                step(cb, lap, g0, 0)
                step(cb, lap, g0, 1)
                with nc.scalar.Fori(0, NE // 2 - 1) as pair:
                    for j in range(2):
                        expert(2 * pair + j, j, False)
                for j in range(2):
                    expert(NE - 2 + j, j, j == 1)
            for t in range(3):
                act.wait_ge(S["x_added"], n_rounds * (6 * NE) + (2 if t == 2 else 0))
                sum_squares(x, N_MEM, (t,))

        @block.vector
        def _(dve):
            V = nc.vector
            n_chain = [0]

            def link(ins):
                n_chain[0] += 1
                ins.then_inc(dve_chain, 1)
                dve.wait_ge(dve_chain, n_chain[0])

            def scale_rows(src, done, n, tiles=(0, 1, 2), cols=slice(0, D), signal=True):
                dve.wait_ge(rstd_ok, done)
                for t in tiles:
                    r = ROWS[t]
                    last = V.tensor_scalar(xn[0:r, t, cols], src[0:r, t, :], rstd[0:r, n, t:t + 1], None, ALU.mult)
                if signal:
                    last.then_inc(rows_ok, 1)

            def turn_lo(l, which, n_tok, blocks=range(KD)):
                for k in blocks:
                    dve.wait_ge(turned_hi, KD * use(l, which) + k + 1)
                    V.scalar_tensor_tensor(out=hT_lo[:, k, 0:n_tok], in0=bank[k % 2][:, 0:n_tok],
                                           scalar=gains[:, l, which, k:k + 1], in1=hT_hi[:, k, 0:n_tok].bitcast(F),
                                           op0=ALU.mult, op1=ALU.subtract).then_inc(turned_lo, 1)

            for t in range(2):
                dve.wait_ge(mem_in[t], 16)
            scale_rows(mem, 1, N_MEM, (0, 1))
            dve.wait_ge(first_in, 16)
            turn_lo(0, G_MEM, NMEM, (0, 1))
            lo_static(dve, 0)
            turn_lo(0, G_MEM, NMEM, (2, 3))
            lo_static(dve, 1)
            turn_lo(0, G_MEM, NMEM, (4, 5, 6, 7))
            lo_static(dve, 2)
            turn_lo(1, G_MEM, NMEM, (0, 1, 2))
            lo_static(dve, 3)
            turn_lo(1, G_MEM, NMEM, (3, 4, 5))
            lo_static(dve, 4)
            turn_lo(1, G_MEM, NMEM, (6, 7))
            for l in range(DEPTH):
                c0 = C_LAYER[l]
                if l == 0:
                    dve.wait_ge(x_in, 32)
                else:
                    link(V.tensor_copy(rt_hi[:, :, :], router))
                    V.tensor_tensor(rt_lo[:, :, :], router, rt_hi[:, :, :].bitcast(F), ALU.subtract).then_inc(S["rt_out"], 1)
                scale_rows(x, event(l, E_MIX01), N_MIX, (0, 1), signal=False)
                scale_rows(x, event(l, E_MIX2), N_MIX, (2,))
                turn_lo(l, G_MIX, NT)
                dve.wait_ge(chunk_used, c0 + 3)
                dve.wait_ge(zeroed, 2 * l + 1)
                for f in range(2):
                    last = V.tensor_scalar(qT[:, f, :], bank[4 + f][:, 0:SEQ], HD ** -0.5, None, ALU.mult)
                last.then_inc(S["q_out"], 1)
                dve.wait_ge(S["kT_done"], l + 1)
                V.tensor_copy(kT[:, :, :].rearrange("p a b -> p (a b)"), bank[2][:, :]).then_inc(S["kT_out"], 1)

                def own(q_, f, p):
                    h = 2 * f + p
                    return own_columns(q_)[HD * p:HD * p + HD, f, :, h * REQT:(h + 1) * REQT]

                def sample_q(f, p):
                    return bank[4 + f][HD * p:HD * p + HD, SEQ:NT].rearrange("p (b t) -> p b t", t=REQT)
                halves = [(f, p) for f in range(2) for p in range(2)]
                for f, p in halves:
                    last = V.tensor_scalar(own(qs[0], f, p), sample_q(f, p), HD ** -0.5, None, ALU.mult)
                link(last)
                for f, p in halves:
                    last = V.scalar_tensor_tensor(out=own(qs[1], f, p), in0=sample_q(f, p), scalar=HD ** -0.5,
                                                  in1=own(qs[0], f, p).bitcast(F), op0=ALU.mult, op1=ALU.subtract)
                last.then_inc(S["qs_out"], 1)
                if l == 0:
                    lo_static(dve, c0 + 3)
                lo_static(dve, c0 + 4)
                for n, i in enumerate((2, 3, 0, 1)):
                    dve.wait_ge(S["sc_done"], 4 * l + n + 1)
                    link(V.reduce_max(mx[:, 2 * i:2 * i + 2], bank[4 + i][:, :].rearrange("p (g m) -> p g m", g=2), AX.X))
                    V.tensor_scalar(nmx[:, 2 * i:2 * i + 2], mx[:, 2 * i:2 * i + 2], -1.0, None, ALU.mult)\
                        .then_inc(S["max_out"], 1)
                    if n == 1:
                        lo_static(dve, c0 + 5)
                lo_static(dve, c0 + 6)
                dve.wait_ge(chunk_used, c0 + 5)
                link(V.reduce_max(mx[:, 8:9], bank[3][:, 0:NMEM], AX.X))
                V.tensor_scalar(nmx[:, 8:9], mx[:, 8:9], -1.0, None, ALU.mult).then_inc(S["smax_out"], 1)
                lo_static(dve, c0 + 7)
                dve.wait_ge(S["sexp_done"], l + 1)
                link(V.reciprocal(rden[:, :], den[:, :]))
                lo_static(dve, c0 + 8, c0 + 9)
                for t in range(3):
                    dve.wait_ge(S["xb_done"], 3 * l + t + 1)
                    last = V.tensor_copy(xb[0:ROWS[t], t, :], bank[4 + t][0:ROWS[t], 0:DB])
                last.then_inc(S["xb_out"], 1)
                dve.wait_ge(rstd_ok, event(l, E_V))
                dve.wait_ge(table_in, 16 * (l + 1))
                for t in range(3):
                    r = ROWS[t]
                    last = V.scalar_tensor_tensor(out=vg[0:r, t, :], in0=vg[0:r, t, :], scalar=rstd[0:r, N_V, t:t + 1],
                                                  in1=g_v[0:r, :], op0=ALU.mult, op1=ALU.mult)
                last.then_inc(S["v_out"], 1)
                for i in range(4):
                    dve.wait_ge(S["PT_done"], 4 * l + i + 1)
                    V.tensor_copy(PT[:, i % 2, :, :].rearrange("p a b -> p (a b)"), bank[(7, 3)[i % 2]][:, :])\
                        .then_inc(S["PT_out"], 1)
                dve.wait_ge(S["sPT_done"], l + 1)
                dve.wait_ge(zeroed, 2 * l + 2)
                turned_p = bank[5][:, 0:256].rearrange("p (f b c) -> p f b c", f=2, b=NREQ)
                link(V.tensor_copy(own_columns(sPT[0]), turned_p))
                V.tensor_tensor(own_columns(sPT[1]), turned_p, own_columns(sPT[0]).bitcast(F), ALU.subtract)\
                    .then_inc(S["sPT_out"], 1)
                dve.wait_ge(S["o_done"], 4 * l + 4)
                for t in range(2):
                    for p in range(2):
                        by_head = lambda a: a.rearrange("p (f h d) -> p f h d", f=2, h=2)[:, :, p, :]
                        sums = rden[:, 4 * t + 2 * p:4 * t + 2 * p + 2].rearrange("p (f a) -> p f a", a=1)
                        last = V.tensor_tensor(by_head(ob[:, t, :]), by_head(bank[4][:, t * DX:(t + 1) * DX]),
                                               sums.to_broadcast([P, 2, HD]), ALU.mult)
                last.then_inc(S["op_out"], 1)
                lo_static(dve, c0 + 10, c0 + 11)
                dve.wait_ge(S["ug_out"], l + 1)
                dve.wait_ge(const_in, 16)
                for t in range(3):
                    dve.wait_ge(S["mix_done"], 3 * l + t + 1)
                    r = ROWS[t]
                    for h in range(AH):
                        cols = slice(h * AHD, (h + 1) * AHD)
                        last = V.scalar_tensor_tensor(out=ug[0:r, t, cols], in0=bank[t][0:r, cols],
                                                      scalar=bias[0:r, l, t // 2, h:h + 1], in1=ug[0:r, t, cols],
                                                      op0=ALU.add, op1=ALU.mult)
                last.then_inc(S["a_out"], 1)
                lo_static(dve, c0 + 12)
                dve.wait_ge(S["y_done"], 3 * l + 3)
                for t in range(3):
                    r = ROWS[t]
                    last = V.tensor_tensor(b_rows[0:r, t, :], bank[3 + t][0:r, 0:DB], s_pool[0:r, :], ALU.mult)
                last.then_inc(S["b_out"], 1)
                scale_rows(ug, event(l, E_A), N_A, cols=slice(0, DA))
                scale_rows(b_rows, event(l, E_B), N_B, cols=slice(DA, DA + DB))
                turn_lo(l, G_GROUP, NT, (0, 1))
                lo_static(dve, c0 + 13)
                turn_lo(l, G_GROUP, NT, (2,))
                scale_rows(ob, event(l, E_O), N_O, cols=slice(DA + DB, D))
                turn_lo(l, G_GROUP, NT, (3, 4, 5))
                lo_static(dve, c0 + 14)
                turn_lo(l, G_GROUP, NT, (6, 7))
                lo_static(dve, c0 + 15)
                for n in range(2):
                    if n == 0:
                        dve.wait_ge(chunk_used, c0 + 14)
                    elif l == 0:
                        lo_static(dve, C_UP, C_UP + 1)
                    for t in range(3):
                        r = ROWS[t]
                        if n and t < 2:
                            dve.wait_ge(S["tile_done"], 2 * l + t + 1)
                        elif n:
                            dve.wait_ge(chunk_used, c0 + 16)
                        V.tensor_tensor(x[0:r, t, n * 512:(n + 1) * 512], x[0:r, t, n * 512:(n + 1) * 512],
                                        bank[2 + 3 * n + t][0:r, :], ALU.add).then_inc(S["x_mixed"], 1)
                dve.wait_ge(S["x_mixed"], 6 * l + 6)
                scale_rows(x, event(l, E_FFN01), N_FFN, (0, 1), signal=False)
                scale_rows(x, event(l, E_FFN2), N_FFN, (2,))
                turn_lo(l, G_FFN, NT)
                dve.wait_ge(stored, 16 * (MEM_STORES + LAYER_STORES * (l + 1)))

                if l == 0:
                    dve.sem_inc(S["H_out"], 2)

                    def hidden(f, j):
                        dve.wait_ge(S["silu_out"], f + 1)
                        up_ps = bank[3 + 2 * (j % 2)][:, 0:NT]
                        at = bass.ds(f * NT, NT)
                        V.tensor_tensor(HT_hi[:, :, :].rearrange("p a b -> p (a b)")[:, at], sg[:, j % 2, :], up_ps, ALU.mult)
                        V.tensor_tensor(hf[:, j % 2, :], sg[:, j % 2, :], up_ps, ALU.mult).then_inc(S["hf_out"], 1)
                        dve.wait_ge(S["hf_out"], f + 1)
                        V.tensor_tensor(HT_lo[:, :, :].rearrange("p a b -> p (a b)")[:, at], hf[:, j % 2, :],
                                        HT_hi[:, :, :].rearrange("p a b -> p (a b)")[:, at].bitcast(F), ALU.subtract)\
                            .then_inc(S["H_out"], 1)
                    with V.Fori(0, NF // RAWS) as i:
                        for j in range(RAWS):
                            split_lo(dve, C_UP + 2 + RAWS * i + j, (C_UP + 2 + j) % RAWS)
                            hidden(RAWS * i + j, j)
                    for f in range(NF // RAWS * RAWS, NF):
                        lo_static(dve, C_UP + 2 + f)
                        hidden(f, f)
                    dve.sem_inc(S["x_dense"], 2)
                    with V.Fori(0, DOWN_CH // RAWS) as i:
                        for what in (2, 3, 4, "x0", 5, 6, "x1", 7, "x2", "x3"):
                            if isinstance(what, int):
                                at = C_DOWN + what
                                split_lo(dve, at + RAWS * i, at % RAWS)
                            else:
                                j = int(what[1])
                                dve.wait_ge(S["y_turned"], 4 * i + j + 1)
                                for t0, t1, r in ((0, 2, P), (2, 3, NS)):
                                    at = x[0:r, t0:t1, bass.ds((4 * i + j) * P, P)]
                                    last = V.tensor_tensor(at, at, bank[j % 2][0:r, t0 * P:t1 * P]
                                                           .rearrange("p (t d) -> p t d", d=P), ALU.add)
                                last.then_inc(S["x_dense"], 1)

            V.memset(logits[:, :, :], 0.0)
            V.memset(mask[:, :, :], 0.0)
            V.memset(posm[:, :, :], -FAR)
            dve.wait_ge(S["logit_done"], 1)
            V.tensor_copy(logitsT[:, :], bank[2][0:NE, 0:NT]).then_inc(S["logitT_out"], 1)

            def gather_rows(t):
                r = ROWS[t]
                V.scalar_tensor_tensor(out=xm[0:r, t, :], in0=x[0:r, t, :], scalar=rstd[0:r, N_FFN, t:t + 1],
                                       in1=g_rows[0:r, :], op0=ALU.mult, op1=ALU.mult).then_inc(S["xm_out"], 1)
            dve.wait_ge(gain_in, 16)
            gather_rows(0)
            dve.wait_ge(S["logit_turned"], 1)
            for t in range(3):
                last = V.tensor_copy(logits[0:ROWS[t], t, :], bank[4][0:ROWS[t], t * NE:(t + 1) * NE])
            link(last)
            for t in range(3):
                last = V.max(top[0:ROWS[t], t, :], logits[0:ROWS[t], t, :])
            link(last)
            for t0, t1, r in ((0, 2, P), (2, 3, NS)):
                last = V.tensor_scalar(nfirst[0:r, t0:t1], top[0:r, t0:t1, 0], -1.0, None, ALU.mult)
            last.then_inc(S["logit_out"], 1)
            for t in range(3):
                last = V.memset(top[0:ROWS[t], t, 2:8], -NEVER)
            link(last)
            for t in range(3):
                r = ROWS[t]
                last = V.match_replace(left[0:r, t, :], top[0:r, t, :], logits[0:r, t, :], NEVER)
            link(last)
            for t in range(3):
                r = ROWS[t]
                last = V.tensor_scalar(mask[0:r, t, :], left[0:r, t, :], 0.5 * NEVER, None, ALU.is_le)
            last.then_inc(S["pos_in"], 1)
            dve.wait_ge(S["pos_in"], 1)
            dve.wait_ge(S["exp2_out"], 1)
            for t in range(3):
                r = ROWS[t]
                last = V.tensor_tensor(gate[0:r, t, :], expo[0:r, t, :], mask[0:r, t, :], ALU.mult)
            link(last)
            for t in range(3):
                r = ROWS[t]
                last = V.reduce_sum(gden[0:r, t:t + 1], gate[0:r, t, :], AX.X)
            link(last)
            for t in range(3):
                r = ROWS[t]
                last = V.reciprocal(gden[0:r, t:t + 1], gden[0:r, t:t + 1])
            link(last)
            for t in range(3):
                r = ROWS[t]
                last = V.tensor_scalar(gate[0:r, t, :], gate[0:r, t, :], gden[0:r, t:t + 1], None, ALU.mult)
            link(last)
            for t in range(3):
                r = ROWS[t]
                last = V.tensor_scalar(posm[0:r, t, :], mask[0:r, t, :], FAR, -FAR, ALU.mult, ALU.add)
            link(last)
            dve.wait_ge(S["pos_done"], 1)
            for t in range(3):
                r = ROWS[t]
                last = V.tensor_tensor(posm[0:r, t, :], posm[0:r, t, :], bank[3][0:r, t * NE:(t + 1) * NE], ALU.add)
            link(last)
            link(V.reduce_max(cmax[:, :], bank[3][0:1, 3 * NE:4 * NE], AX.X))
            V.tensor_scalar(over[:, 0:1], cmax[:, :], float(P), 1.0, ALU.is_gt, ALU.add)
            link(V.tensor_scalar(over[:, 1:2], cmax[:, :], float(2 * P), None, ALU.is_gt))
            V.tensor_tensor(rounds[:, :], over[:, 0:1], over[:, 1:2], ALU.add).then_inc(S["rounds_ok"], 1)
            dve.sem_inc(S["x_added"], 2)
            dve.wait_ge(S["rounds_ok"], 1)
            gather_rows(2)
            n_rounds = V.value_load(rounds[0:1, 0:1], min_val=1, max_val=MAX_ROUNDS)
            with V.Fori(0, n_rounds) as r:
                def regs(e):
                    q = V.snap(r * NE + e)
                    return q, V.snap(q * EXP_CH + (C_MOE + 2)), V.snap(q * STEPS)

                def lo(cb, off, extra=0):
                    split_lo(dve, cb + off + RAWS * extra, (off + 2) % RAWS)

                def select(e):
                    for t in range(3):
                        rr = ROWS[t]
                        last = V.tensor_scalar(sel[0:rr, t, :], slots[0:rr, :], posm[0:rr, t, bass.ds(e, 1)], None,
                                               ALU.is_equal)
                    last.then_inc(S["sel_out"], 1)

                def gathered_lo(q, j, b):
                    dve.wait_ge(S["gat_hi"], 2 * q + b + 1)
                    V.tensor_tensor(gT_lo[:, j, 4 * b:4 * b + 4, :].rearrange("p a b -> p (a b)"), bank[b][:, :],
                                    gT_hi[:, j, 4 * b:4 * b + 4, :].rearrange("p a b -> p (a b)").bitcast(F), ALU.subtract)\
                        .then_inc(S["gat_lo"], 1)

                def keep_selT(q, j):
                    dve.wait_ge(S["selT_done"], q + 1)
                    V.tensor_copy(selT[:, j, :], bank[0][:, 0:NT]).then_inc(S["selT_out"], 1)

                def hidden_of(g0, s, extra=0):
                    dve.wait_ge(S["esilu"], g0 + s + 1 + 2 * extra)
                    V.tensor_tensor(eh[:, s % 2, :], esg[:, s % 2, :], bank[2 + s % 2][:, 256:512], ALU.mult)\
                        .then_inc(S["eh_out"], 1)

                def turned_of(g0, s, extra=0):
                    dve.wait_ge(S["eT_hi_out"], g0 + s + 1 + 2 * extra)
                    V.tensor_tensor(eT_lo[:, s % 2, :, :].rearrange("p a b -> p (a b)"), bank[4 + s % 2][:, 0:256],
                                    eT_hi[:, s % 2, :, :].rearrange("p a b -> p (a b)").bitcast(F), ALU.subtract)\
                        .then_inc(S["eT_out"], 1)

                def y_lo_of(q):
                    for n in range(2):
                        dve.wait_ge(S["y_hi_out"], 2 * q + n + 1)
                        last = V.tensor_tensor(y_lo[:, n * 512:(n + 1) * 512], bank[6 + n][:, :],
                                               y_hi[:, n * 512:(n + 1) * 512].bitcast(F), ALU.subtract)
                    last.then_inc(S["y_out"], 1)

                def add(q, e, *ms_):
                    for m in ms_:
                        t, n = m // 2, m % 2
                        rr = ROWS[t]
                        dve.wait_ge(S["scat_done"], 6 * q + m + 1)
                        at = x[0:rr, t, n * 512:(n + 1) * 512]
                        V.scalar_tensor_tensor(out=at, in0=bank[n][0:rr, :], scalar=gate[0:rr, t, bass.ds(e, 1)], in1=at,
                                               op0=ALU.mult, op1=ALU.add).then_inc(S["x_added"], 1)

                def step(cb, g0, s, extra=0):
                    hidden_of(g0, s, extra)
                    lo(cb, 3 * s + 2, extra)
                    turned_of(g0, s, extra)
                    lo(cb, 3 * s + 3, extra)
                    lo(cb, 3 * s + 4, extra)

                def expert(e, j, last):
                    q, cb, g0 = regs(e)
                    if not last:
                        select(e + 1)
                    with V.Fori(0, STEPS // 2 - 2) as p:
                        step(cb, g0, 2, p)
                        step(cb, g0, 3, p)
                    s = STEPS - 2
                    hidden_of(g0, s)
                    lo(cb, 3 * s + 2)
                    if last:
                        turned_of(g0, s)
                        lo(cb, 3 * s + 3)
                        hidden_of(g0, s + 1)
                        turned_of(g0, s + 1)
                        y_lo_of(q)
                        add(q, e, 0, 1, 2, 3, 4, 5)
                        return
                    gathered_lo(q + 1, 1 - j, 0)
                    turned_of(g0, s)
                    gathered_lo(q + 1, 1 - j, 1)
                    lo(cb, 3 * s + 3)
                    lo(cb, 3 * s + 4)
                    s = STEPS - 1
                    hidden_of(g0, s)
                    lo(cb, 3 * s + 2)
                    turned_of(g0, s)
                    lo(cb, 3 * s + 3)
                    keep_selT(q + 1, 1 - j)
                    lo(cb, 3 * s + 4)
                    s = STEPS
                    hidden_of(g0, s)
                    y_lo_of(q)
                    lo(cb, 3 * s + 2)
                    turned_of(g0, s)
                    lo(cb, 3 * s + 3)
                    add(q, e, 0, 1)
                    lo(cb, 3 * s + 4)
                    s = STEPS + 1
                    hidden_of(g0, s)
                    lo(cb, 3 * s + 2)
                    add(q, e, 2, 3)
                    turned_of(g0, s)
                    lo(cb, 3 * s + 3)
                    add(q, e, 4, 5)
                    lo(cb, 3 * s + 4)

                select(0)
                q, cb, g0 = regs(0)
                for off in (-2, -1, 0):
                    lo(cb, off)
                for b in range(2):
                    gathered_lo(q, 0, b)
                keep_selT(q, 0)
                lo(cb, 1)
                step(cb, g0, 0)
                step(cb, g0, 1)
                with V.Fori(0, NE // 2 - 1) as pair:
                    for j in range(2):
                        expert(2 * pair + j, j, False)
                for j in range(2):
                    expert(NE - 2 + j, j, j == 1)
                V.tensor_scalar(posm[:, :, :], posm[:, :, :], -float(P), None, ALU.add).then_inc(S["pos_moved"], 1)
                dve.wait_ge(S["pos_moved"], r + 1)
            dve.wait_ge(gain_in, 32)
            for t in range(3):
                rr = ROWS[t]
                dve.wait_ge(rstd_ok, event(DEPTH, 1 + t))
                V.scalar_tensor_tensor(out=xm[0:rr, t, :], in0=x[0:rr, t, :], scalar=rstd[0:rr, N_MEM, t:t + 1],
                                       in1=g_rows[0:rr, :], op0=ALU.mult, op1=ALU.mult).then_inc(S["fin_out"], 1)

        @block.tensor
        def _(pe):
            T = nc.tensor

            def arrived(c):
                pe.wait_ge(lo_ready, c + 1)

            def turn(l, which, tiles=(0, 1, 2), product=None, rows=None):
                u = use(l, which)
                if u:
                    pe.wait_ge(turned_lo, KD * u)
                for k in range(KD):
                    if rows and k in rows:
                        pe.wait_ge(rows_ok, rows[k])
                    if k >= 2:
                        pe.wait_ge(turned_lo, KD * u + k - 1)
                    for t in tiles:
                        r = ROWS[t]
                        last = T.transpose(bank[k % 2][:, t * P:t * P + r], xn[0:r, t, k * P:(k + 1) * P],
                                           ident[0:r, 0:r])
                    last.then_inc(turned, 1)
                    if product and k:
                        pe.wait_ge(turned_lo, KD * u + k)
                        product(k - 1)
                pe.wait_ge(turned_lo, KD * u + KD)
                if product:
                    product(KD - 1)

            def rows_times(c, b, n_blocks, k, banks, first, last_k):
                out = []
                for t in range(3):
                    r = ROWS[t]
                    out.append(mm3(bank[banks + t][0:r, 0:n_blocks * P], hT_hi[:, k, t * P:t * P + r],
                                   hT_lo[:, k, t * P:t * P + r], blk(whi, c, b, n_blocks), blk(wlo, c, b, n_blocks),
                                   first, last_k))
                return out

            pe.wait_ge(first_in, 16)
            for l in range(DEPTH):
                def keys_values(k):
                    c = KV_CH * l + k // 4
                    if k % 4 == 0:
                        arrived(c)
                    for t in range(2):
                        m = mm3(bank[(2, 6)[l] + t][:, :], hT_hi[:, k, t * P:(t + 1) * P], hT_lo[:, k, t * P:(t + 1) * P],
                                blk(whi, c, 4 * (k % 4), 4), blk(wlo, c, 4 * (k % 4), 4), k == 0, k == KD - 1)
                    if k % 4 == 3:
                        m.then_inc(chunk_used, 1)
                turn(l, G_MEM, (0, 1), keys_values, {0: 1})
            for l in range(DEPTH):
                c0 = C_LAYER[l]
                if l:
                    pe.wait_ge(S["x_dense"], KD + 2)

                def queries(k):
                    if k == 0:
                        arrived(c0 + 2)
                    for f in range(2):
                        m = mm3(bank[4 + f][:, 0:NT], blk(whi, c0 + 2, 2 * k + f), blk(wlo, c0 + 2, 2 * k + f),
                                hT_hi[:, k, :], hT_lo[:, k, :], k == 0, k == KD - 1)
                    if k == KD - 1:
                        m.then_inc(chunk_used, 1)
                turn(l, G_MIX, product=queries, rows={0: ready(l, R_MIX)})
                pe.wait_ge(S["kv_out"], DEPTH)
                for f in range(2):
                    for t in range(2):
                        last = T.transpose(bank[2][:, f * 256 + t * P:f * 256 + (t + 1) * P], kv[:, l, t, f * P:(f + 1) * P],
                                           ident)
                last.then_inc(S["kT_done"], 1)
                pe.wait_ge(S["q_out"], l + 1)
                pe.wait_ge(S["kT_out"], l + 1)
                for t in (1, 0):
                    if t == 0:
                        pe.wait_ge(S["qs_out"], l + 1)
                    for f in range(2):
                        for p in range(2):
                            m = T.matmul(bank[4 + 2 * t + p][:, f * NMEM:(f + 1) * NMEM],
                                         qT[HD * p:HD * p + HD, f, t * P:(t + 1) * P], kT[HD * p:HD * p + HD, f, :],
                                         start=True, stop=True)
                            if f == 1:
                                m.then_inc(S["sc_done"], 1)
                for c in (0, 1):
                    arrived(c0 + 3 + c)
                    for b in range(4):
                        for f in range(2):
                            r = 4 * c + b
                            m = mm3(bank[3][:, 0:NMEM], only(qs[0], f, r), only(qs[1], f, r),
                                    blk(whi, c0 + 3 + c, 4 * b + 2 * f, 2), blk(wlo, c0 + 3 + c, 4 * b + 2 * f, 2),
                                    r == 0 and f == 0, r == NREQ - 1 and f == 1)
                    m.then_inc(chunk_used, 1)
                arrived(c0 + 5)
                for k in range(5):
                    m = rows_times(c0 + 5, 3 * k, 3, k, 0, k == 0, False)[-1]
                m.then_inc(chunk_used, 1)
                arrived(c0 + 6)
                for k in (5, 6, 7):
                    ms_ = rows_times(c0 + 6, 3 * (k - 5), 3, k, 0, False, k == 7)
                for m in ms_:
                    m.then_inc(S["v_done"], 1)
                pe.wait_ge(S["exp_done"], 4 * l + 4)
                for k in (0, 1):
                    m = rows_times(c0 + 6, 9 + 3 * k, 3, k, 4, k == 0, False)[-1]
                m.then_inc(chunk_used, 1)
                arrived(c0 + 7)
                for k in range(2, 7):
                    m = rows_times(c0 + 7, 3 * (k - 2), 3, k, 4, False, False)[-1]
                m.then_inc(chunk_used, 1)
                arrived(c0 + 8)
                for m in rows_times(c0 + 8, 0, 3, 7, 4, False, True):
                    m.then_inc(S["xb_done"], 1)
                pe.wait_ge(S["vg_out"], l + 1)
                for k in range(4):
                    m = rows_times(c0 + 8, 3 + 3 * k, 3, k, 0, k == 0, False)[-1]
                m.then_inc(chunk_used, 1)
                arrived(c0 + 9)
                for k in range(4, 8):
                    m = rows_times(c0 + 9, 3 * (k - 4), 3, k, 0, False, k == 7)[-1]
                m.then_inc(chunk_used, 1)

                def turn_probs(i):
                    if i == 1:
                        pe.wait_ge(S["sexp_done"], l + 1)
                    if i >= 2:
                        pe.wait_ge(S["PT_out"], 4 * l + i - 1)
                    for f in range(2):
                        for mt in range(2):
                            last = T.transpose(bank[(7, 3)[i % 2]][:, (2 * f + mt) * P:(2 * f + mt + 1) * P],
                                               prob[:, 2 * i + f, mt * P:(mt + 1) * P], ident)
                    last.then_inc(S["PT_done"], 1)

                def attend(i):
                    t, p = i // 2, i % 2
                    pe.wait_ge(S["PT_out"], 4 * l + i + 1)
                    for f in range(2):
                        h = 2 * f + p
                        for mt in range(2):
                            last = T.matmul(bank[4][:, t * DX + h * HD:t * DX + (h + 1) * HD], PT[:, i % 2, 2 * f + mt, :],
                                            kv[:, l, mt, DX + h * HD:DX + (h + 1) * HD], start=mt == 0, stop=mt == 1)
                    last.then_inc(S["o_done"], 1)

                turn_probs(0)
                turn_probs(1)
                pe.wait_ge(S["xb_out"], l + 1)
                attend(0)
                turn_probs(2)
                attend(1)
                turn_probs(3)
                pe.wait_ge(S["sexp_done"], l + 1)
                for mt in range(2):
                    last = T.transpose(bank[5][:, mt * P:(mt + 1) * P], sP[:, mt * P:(mt + 1) * P], ident)
                last.then_inc(S["sPT_done"], 1)
                attend(2)
                attend(3)
                pe.wait_ge(const_in, 16)
                pe.wait_ge(S["ug_out"], l + 1)
                pe.wait_ge(state_in, 16 * (l + 1))
                for g in range(4):
                    ch = slice(g * GD, (g + 1) * GD)
                    T.matmul(bank[g][0:GD, 0:SEQ], xb[:, 0, ch], pool0[:, g, :], start=True, stop=False)
                    T.matmul(bank[g][0:GD, P:SEQ], xb[:, 1, ch], pool1[:, g, :], start=False, stop=True)
                    T.matmul(bank[g][0:GD, SEQ:NT], xb[0:NS, 2, ch], pool_s[:, g, :], start=True, stop=False)
                    T.matmul(bank[g][0:GD, SEQ:NT], state[:, ch], pool_st[:, g, :], start=False, stop=True)\
                        .then_inc(S["dT_done"], 1)

                def sample_values(c):
                    arrived(c0 + 10 + c)
                    for b in range(4):
                        for mt in range(2):
                            r = 4 * c + b
                            m = mm3(bank[6][:, 0:DX], only(sPT[0], mt, r), only(sPT[1], mt, r),
                                    blk(whi, c0 + 10 + c, 4 * b + 2 * mt, 2), blk(wlo, c0 + 10 + c, 4 * b + 2 * mt, 2),
                                    r == 0 and mt == 0, r == NREQ - 1 and mt == 1)
                    m.then_inc(chunk_used, 1)
                pe.wait_ge(masked, l + 1)
                pe.wait_ge(S["v_out"], l + 1)
                pe.wait_ge(S["dT_out"], l + 1)
                for t in range(3):
                    r = ROWS[t]
                    w = w_sp if t < 2 else w_sps
                    for h in range(AH):
                        last = T.matmul(bank[t][0:r, h * AHD:(h + 1) * AHD], w[:, h, :],
                                        vg[0:r, t, h * AHD:(h + 1) * AHD], start=True, stop=True)
                    last.then_inc(S["mix_done"], 1)
                pe.wait_ge(S["sPT_out"], l + 1)
                sample_values(0)
                pe.wait_ge(S["op_out"], l + 1)
                for t in range(3):
                    r = ROWS[t]
                    for g in range(4):
                        last = T.matmul(bank[3 + t][0:r, g * GD:(g + 1) * GD], dT[0:GD, g, t * P:t * P + r], w_pool[:, g, :],
                                        start=True, stop=True)
                    last.then_inc(S["y_done"], 1)
                sample_values(1)
                pe.wait_ge(S["os_rows_out"], l + 1)
                for h in range(HEADS):
                    last = T.matmul(bank[7][0:NS, h * HD:(h + 1) * HD], fold[:, h, :], os_rows[:, h * HD:(h + 1) * HD],
                                    start=True, stop=True)
                last.then_inc(S["os_done"], 1)

                def project(n, k, tiles=(0, 1, 2)):
                    c = c0 + 12 + 2 * n + k // 4
                    for t in tiles:
                        r = ROWS[t]
                        m = mm3(bank[2 + 3 * n + t][0:r, :], hT_hi[:, k, t * P:t * P + r], hT_lo[:, k, t * P:t * P + r],
                                blk(whi, c, 4 * (k % 4), 4), blk(wlo, c, 4 * (k % 4), 4), k == 0, k == KD - 1)
                    return m

                def project_left(k):
                    if k == 0:
                        pe.wait_ge(S["b_out"], l + 1)
                    if k % 4 == 0:
                        arrived(c0 + 12 + k // 4)
                    m = project(0, k)
                    if k % 4 == 3:
                        m.then_inc(chunk_used, 1)
                turn(l, G_GROUP, product=project_left, rows={0: ready(l, R_A), 3: ready(l, R_B), 6: ready(l, R_O)})
                arrived(c0 + 14)
                for k in range(4):
                    m = project(1, k)
                m.then_inc(chunk_used, 1)
                arrived(c0 + 15)
                for t in range(3):
                    for k in range(4, KD):
                        m = project(1, k, (t,))
                    m.then_inc(S["tile_done"] if t < 2 else chunk_used, 1)

                def first_up(k):
                    if k == 0:
                        arrived(C_UP)
                    for w in range(2):
                        m = mm3(bank[2 + w][:, 0:NT], blk(whi, C_UP, 2 * k + w), blk(wlo, C_UP, 2 * k + w), hT_hi[:, k, :],
                                hT_lo[:, k, :], k == 0, k == KD - 1)
                    if k == KD - 1:
                        m.then_inc(chunk_used, 1)

                def route(k):
                    if k == 0:
                        pe.wait_ge(S["rt_out"], 1)
                    mm3(bank[2][0:NE, 0:NT], rt_hi[:, k, :], rt_lo[:, k, :], hT_hi[:, k, :], hT_lo[:, k, :], k == 0, False)
                    m = T.matmul(bank[2][0:NE, 0:NT], rt_lo[:, k, :], hT_lo[:, k, :], start=False, stop=k == KD - 1)
                    if k == KD - 1:
                        m.then_inc(S["logit_done"], 1)
                turn(l, G_FFN, product=route if l else first_up, rows={0: ready(l, R_FFN)})

                if l == 0:
                    def up(f, j):
                        arrived(C_UP + f)
                        pe.wait_ge(S["H_out"], f + 1)
                        for k in range(KD):
                            for w in range(2):
                                m = mm3(bank[2 + 2 * (j % 2) + w][:, 0:NT], blk(whi, C_UP + j, 2 * k + w),
                                        blk(wlo, C_UP + j, 2 * k + w), hT_hi[:, k, :], hT_lo[:, k, :], k == 0, k == KD - 1)
                        m.then_inc(chunk_used, 1)
                    with T.Fori(0, NF // RAWS) as i:
                        for j in range(RAWS):
                            up(RAWS * i + 1 + j, 1 + j)
                    for f in range(NF // RAWS * RAWS + 1, NF):
                        up(f, f)
                    pe.wait_ge(S["H_out"], NF)

                    def down(i, j):
                        pe.wait_ge(S["yT_out"], 4 * i + j + 1)
                        for f in range(NF):
                            b = DOWN_BLOCKS * j + f
                            if j == 0 and f == NF - 2:
                                pe.wait_ge(S["H_out"], NF + 2)
                            if b % 16 == 0 or f == 0:
                                arrived(C_DOWN + RAWS * i + b // 16)
                            m = mm3(bank[6 + j % 2][:, 0:NT], blk(whi, C_DOWN + b // 16, b % 16),
                                    blk(wlo, C_DOWN + b // 16, b % 16), HT_hi[:, f, :], HT_lo[:, f, :], f == 0, f == NF - 1)
                            if b % 16 == 15 or (f == NF - 1 and j % 2):
                                m.then_inc(chunk_used, 1)
                        if j % 2 == 0:
                            m.then_inc(S["yT_done"], 1)

                    def turn_back(i, j):
                        pe.wait_ge(S["yT_out"], 4 * i + j + 3)
                        pe.wait_ge(S["x_dense"], 4 * i + j + 1)
                        for t in range(3):
                            r = ROWS[t]
                            last = T.transpose(bank[j % 2][0:r, t * P:(t + 1) * P], yT[:, j % 2, t * P:t * P + r], ident)
                        last.then_inc(S["y_turned"], 1)
                    with T.Fori(0, DOWN_CH // RAWS) as i:
                        down(i, 0)
                        down(i, 1)
                        turn_back(i, 0)
                        down(i, 2)
                        turn_back(i, 1)
                        down(i, 3)
                        turn_back(i, 2)
                        turn_back(i, 3)

            pe.wait_ge(S["logitT_out"], 1)
            for t in range(3):
                last = T.transpose(bank[4][0:ROWS[t], t * NE:(t + 1) * NE], logitsT[:, t * P:t * P + ROWS[t]],
                                   ident[0:NE, 0:NE])
            last.then_inc(S["logit_turned"], 1)
            pe.wait_ge(S["pos_in"], 1)
            for t in range(3):
                r = ROWS[t]
                for s_ in range(t):
                    T.matmul(bank[3][0:r, t * NE:(t + 1) * NE], ones[:, 0:r], mask[:, s_, :], start=s_ == 0, stop=False)
                T.matmul(bank[3][0:r, t * NE:(t + 1) * NE], before[0:r, 0:r], mask[0:r, t, :], start=t == 0, stop=True)
            for t in range(3):
                r = ROWS[t]
                last = T.matmul(bank[3][0:1, 3 * NE:4 * NE], ones[0:r, 0:1], mask[0:r, t, :], start=t == 0, stop=t == 2)
            last.then_inc(S["pos_done"], 1)

            pe.wait_ge(S["rounds_ok"], 1)
            pe.wait_ge(S["xm_out"], 2)
            pe.wait_ge(S["xm_tile1_out"], 1)
            n_rounds = T.value_load(rounds[0:1, 0:1], min_val=1, max_val=MAX_ROUNDS)
            with T.Fori(0, n_rounds) as r:
                def regs(e):
                    q = T.snap(r * NE + e)
                    return q, T.snap(q * EXP_CH + (C_MOE + 2)), T.snap(q * STEPS)

                def gather(b):
                    for k in range(4 * b, 4 * b + 4):
                        for t in range(3):
                            rr = ROWS[t]
                            last = T.matmul(bank[b][:, (k % 4) * P:(k % 4 + 1) * P], xm[0:rr, t, k * P:(k + 1) * P],
                                            sel[0:rr, t, :], start=t == 0, stop=t == 2)
                    last.then_inc(S["gat_done"], 1)

                def turn_sel(q):
                    pe.wait_ge(S["gat_lo"], 2 * q + 2)
                    for t in range(3):
                        rr = ROWS[t]
                        last = T.transpose(bank[0][:, t * P:t * P + rr], sel[0:rr, t, :], ident[0:rr, 0:rr])
                    last.then_inc(S["selT_done"], 1)

                def gate_up(cb, off, s, half_, j, extra=0):
                    pe.wait_ge(lo_ready, cb + off + 1 + RAWS * extra)
                    for k in range(4):
                        kk = 4 * half_ + k
                        m = mm3(bank[2 + s % 2][:, :], gT_hi[:, j, kk, :], gT_lo[:, j, kk, :], blk(whi, off + 2, 4 * k, 4),
                                blk(wlo, off + 2, 4 * k, 4), kk == 0, kk == KD - 1)
                    m.then_inc(chunk_used, 1)

                def turn_hidden(g0, s, extra=0):
                    pe.wait_ge(S["eh_out"], g0 + s + 1 + 2 * extra)
                    for b in range(2):
                        last = T.transpose(bank[4 + s % 2][:, b * P:(b + 1) * P], eh[:, s % 2, b * P:(b + 1) * P], ident)
                    last.then_inc(S["eT_done"], 1)

                def down(cb, g0, off, s, extra=0):
                    pe.wait_ge(lo_ready, cb + off + 1 + RAWS * extra)
                    pe.wait_ge(S["eT_out"], g0 + s + 1 + 2 * extra)
                    for b in range(2):
                        for n in range(2):
                            m = mm3(bank[6 + n][:, :], eT_hi[:, s % 2, b, :], eT_lo[:, s % 2, b, :],
                                    blk(whi, off + 2, 8 * b + 4 * n, 4), blk(wlo, off + 2, 8 * b + 4 * n, 4),
                                    s % STEPS == 0 and b == 0, s == STEPS - 1 and b == 1, skip_group_check=True)
                    m.then_inc(chunk_used, 1)

                def scatter(q, j, *ms_):
                    for m_ in ms_:
                        t, n = m_ // 2, m_ % 2
                        rr = ROWS[t]
                        pe.wait_ge(S["x_added"], 6 * q + m_ + 1)
                        T.matmul(bank[n][0:rr, :], selT[:, j, t * P:t * P + rr], y_hi[:, n * 512:(n + 1) * 512],
                                 start=True, stop=False)
                        T.matmul(bank[n][0:rr, :], selT[:, j, t * P:t * P + rr], y_lo[:, n * 512:(n + 1) * 512],
                                 start=False, stop=True).then_inc(S["scat_done"], 1)

                def step(cb, g0, s, j, extra=0):
                    gate_up(cb, 3 * s, s + 1, 0, j, extra)
                    turn_hidden(g0, s, extra)
                    gate_up(cb, 3 * s + 1, s + 1, 1, j, extra)
                    down(cb, g0, 3 * s + 2, s, extra)

                def expert(e, j, last):
                    q, cb, g0 = regs(e)
                    with T.Fori(0, STEPS // 2 - 2) as p:
                        step(cb, g0, 2, j, p)
                        step(cb, g0, 3, j, p)
                    s = STEPS - 2
                    if last:
                        step(cb, g0, s, j)
                        turn_hidden(g0, s + 1)
                        down(cb, g0, 3 * s + 3, s + 1)
                        pe.wait_ge(S["y_out"], q + 1)
                        pe.wait_ge(S["selT_out"], q + 1)
                        scatter(q, j, 0, 1, 2, 3, 4, 5)
                        return
                    pe.wait_ge(S["sel_out"], q + 2)
                    pe.wait_ge(S["selT_out"], q + 1)
                    pe.wait_ge(S["x_added"], 6 * q + 2)
                    gather(0)
                    gate_up(cb, 3 * s, s + 1, 0, j)
                    turn_hidden(g0, s)
                    gather(1)
                    gate_up(cb, 3 * s + 1, s + 1, 1, j)
                    down(cb, g0, 3 * s + 2, s)
                    s = STEPS - 1
                    pe.wait_ge(S["gat_lo"], 2 * q + 4)
                    gate_up(cb, 3 * s, s + 1, 0, 1 - j)
                    turn_hidden(g0, s)
                    turn_sel(q + 1)
                    gate_up(cb, 3 * s + 1, s + 1, 1, 1 - j)
                    down(cb, g0, 3 * s + 2, s)
                    s = STEPS
                    gate_up(cb, 3 * s, s + 1, 0, 1 - j)
                    turn_hidden(g0, s)
                    gate_up(cb, 3 * s + 1, s + 1, 1, 1 - j)
                    pe.wait_ge(S["y_out"], q + 1)
                    pe.wait_ge(S["selT_out"], q + 2)
                    scatter(q, j, 0, 1)
                    down(cb, g0, 3 * s + 2, s)
                    s = STEPS + 1
                    gate_up(cb, 3 * s, s + 1, 0, 1 - j)
                    scatter(q, j, 2, 3)
                    turn_hidden(g0, s)
                    gate_up(cb, 3 * s + 1, s + 1, 1, 1 - j)
                    scatter(q, j, 4, 5)
                    down(cb, g0, 3 * s + 2, s)

                q, cb, g0 = regs(0)
                pe.wait_ge(S["sel_out"], q + 1)
                pe.wait_ge(S["x_added"], 6 * q + 2)
                gather(0)
                gather(1)
                turn_sel(q)
                gate_up(cb, -2, 0, 0, 0)
                gate_up(cb, -1, 0, 1, 0)
                step(cb, g0, 0, 0)
                step(cb, g0, 1, 0)
                with T.Fori(0, NE // 2 - 1) as pair:
                    for j in range(2):
                        expert(2 * pair + j, j, False)
                for j in range(2):
                    expert(NE - 2 + j, j, j == 1)


def _pool_tables():
    full = np.zeros((4, SEQ, SEQ), np.float32)
    req = np.zeros((4, PBUF + REQT, REQT), np.float32)
    for g, w in enumerate(WINDOWS):
        for t in range(SEQ):
            first = max(0, t - w + 1)
            full[g, first:t + 1, t] = 1.0 / (t + 1 - first)
            full[g, t, t] -= 1.0
        for t in range(REQT):
            req[g, PBUF + t - w + 1:PBUF + t + 1, t] = 1.0 / w
            req[g, PBUF + t, t] -= 1.0
    own = np.zeros((4, NS, NS), np.float32)
    old = np.zeros((4, NREQ * PBUF, NS), np.float32)
    for b in range(NREQ):
        own[:, b * REQT:(b + 1) * REQT, b * REQT:(b + 1) * REQT] = req[:, PBUF:]
        old[:, b * PBUF:(b + 1) * PBUF, b * REQT:(b + 1) * REQT] = req[:, :PBUF]
    return full, own, old


def _constants(v):
    table = np.zeros((P, N_CONST), np.float32)

    def put(name, a):
        a = np.asarray(a).reshape(a.shape[0], -1)
        lo, hi = COL[name]
        assert a.shape[1] == hi - lo, name
        table[:a.shape[0], lo:hi] = a

    put("ident", np.eye(P, dtype=np.float32))
    g = np.stack([v["g_mem"], v["g_mix_norm"], v["g_group"], v["g_ffn_norm"]], 1)
    put("gains", g.reshape(DEPTH, 4, KD, P).transpose(3, 0, 1, 2))
    full, own, old = _pool_tables()
    put("pool0", full[:, 0:P].transpose(1, 0, 2))
    put("pool1", full[:, P:, P:].transpose(1, 0, 2))
    put("pool_s", own.transpose(1, 0, 2))
    put("pool_st", old.transpose(1, 0, 2))
    bias = np.zeros((P, DEPTH, 2, AH), np.float32)
    bias[:, :, 0] = v["b_spatial"].transpose(2, 0, 1)
    bias[:NS, :, 1] = np.tile(v["b_spatial"][:, :, :REQT].transpose(2, 0, 1), (NREQ, 1, 1))
    put("bias", bias)
    fold = np.zeros((NREQ, HEADS, REQT, HEADS, NREQ, REQT), np.float32)
    for b in range(NREQ):
        for h in range(HEADS):
            fold[b, h, :, h, b, :] = np.eye(REQT)
    put("fold", fold.reshape(P, -1))
    put("before", np.triu(np.ones((P, P), np.float32), 1))
    put("ones", np.ones((P, P), np.float32))
    put("slots", np.tile(np.arange(P, dtype=np.float32), (P, 1)))
    put("router", v["w_router"][0].reshape(KD, P, NE).transpose(1, 0, 2))
    return table


def _layer_tables(v):
    small = np.zeros((NS, DEPTH, AH, NS), np.float32)
    for b in range(NREQ):
        at = slice(b * REQT, (b + 1) * REQT)
        small[at, :, :, at] = v["w_spatial"][:, :, :REQT, :REQT].transpose(3, 0, 1, 2)
    out = np.zeros((DEPTH, P, N_LAYER), np.float32)
    at = 0
    for a in (v["w_pool"].transpose(0, 2, 1, 3), v["w_spatial"].transpose(0, 3, 1, 2), small.transpose(1, 0, 2, 3),
              np.broadcast_to(v["g_v"].reshape(DEPTH, 1, DA), (DEPTH, P, DA)),
              np.broadcast_to(v["s_pool"].reshape(DEPTH, 1, DB), (DEPTH, P, DB))):
        a = a.reshape(DEPTH, a.shape[1], -1)
        out[:, :a.shape[1], at:at + a.shape[2]] = a
        at += a.shape[2]
    assert at == N_LAYER
    return out


def _stream(v):
    out = np.zeros((N_CH, P, CW), np.float32)
    n = 0

    def put(a):
        nonlocal n
        out[n:n + len(a), :, :a.shape[2]] = a
        n += len(a)

    def columns4(w):
        m = w.shape[1] // 512
        return w.reshape(2, 4, P, m, 512).transpose(3, 0, 2, 1, 4).reshape(2 * m, P, CW)

    for l in range(DEPTH):
        put(columns4(v["w_mem_kv"][l]))
    for l in range(DEPTH):
        w = v["w_in"][l].reshape(KD, P, -1)
        put(w[:, :, 2 * DA + DB:].transpose(1, 0, 2).reshape(1, P, CW))
        put(v["cache_mem_k"][l].reshape(2, 4, NMEM, 2, P).transpose(0, 4, 1, 3, 2).reshape(2, P, CW))
        rows = np.concatenate([w[:, :, DA:2 * DA], w[:, :, 2 * DA:2 * DA + DB], w[:, :, 0:DA]])
        for a, b in ((0, 5), (5, 10), (10, 15), (15, 20), (20, 24)):
            put(rows[a:b].transpose(1, 0, 2).reshape(1, P, -1))
        put(v["cache_mem_v"][l].reshape(2, 4, 2, P, DX).transpose(0, 3, 1, 2, 4).reshape(2, P, CW))
        put(columns4(v["w_out"][l]))
        if l == 0:
            gu = np.stack([v["w_dense_gate"][0], v["w_dense_up"][0]]).reshape(2, KD, P, NF, P)
            put(gu.transpose(3, 2, 1, 0, 4).reshape(NF, P, CW))
            d = np.zeros((KD, DOWN_BLOCKS, P, P), np.float32)
            d[:, :NF] = v["w_dense_down"][0].reshape(NF, P, KD, P).transpose(2, 0, 1, 3)
            put(d.reshape(DOWN_CH, 16, P, P).transpose(0, 2, 1, 3).reshape(DOWN_CH, P, CW))
    assert n == C_MOE
    gate_up, down = [], []
    for e in range(NE):
        gu = np.stack([v["w_moe_gate"][0, e], v["w_moe_up"][0, e]])
        gate_up.append(gu.reshape(2, 2, 4, P, STEPS, 256).transpose(4, 1, 3, 2, 0, 5).reshape(STEPS, 2, P, CW))
        down.append(v["w_moe_down"][0, e].reshape(STEPS, 2, P, D).transpose(0, 2, 1, 3).reshape(STEPS, 1, P, CW))
    gate_up, down = np.concatenate(gate_up), np.concatenate(down)
    put(gate_up[0])
    for s in range(NE * STEPS):
        if s + 1 < NE * STEPS:
            put(gate_up[s + 1])
        put(down[s])
    assert n == N_CH
    return out.reshape(N_CH * P, CW)


def kernel(**inputs):
    import concourse.bacc as bacc
    from concourse.bass_utils import run_bass_kernel_spmd

    v = {k: np.asarray(a) for k, a in inputs.items()}
    arrays = {
        "stream": _stream(v),
        "const": _constants(v),
        "table": _layer_tables(v),
        "mem": v["mem_prompt"].reshape(NMEM, D),
        "x_prompt": v["x_prompt"].reshape(SEQ, D),
        "x_sample": v["x_sample"].reshape(NS, D),
        "state": v["state_pool"].reshape(DEPTH, NREQ * PBUF, DB),
        "g_moe": np.tile(v["g_ffn_norm"][DEPTH - 1].reshape(1, D), (P, 1)),
        "g_final": np.tile(v["g_final"].reshape(1, D), (P, 1)),
    }
    outs = {
        "y_prompt": (SEQ, D), "y_sample": (NS, D), "pool_prompt": (DEPTH, PBUF, DB), "mem_k": (DEPTH, NMEM, DX),
        "mem_v": (DEPTH, NMEM, DX), "pool_sample": (DEPTH, NREQ, PBUF, DB), "v_rows": (DEPTH, NS, DA),
    }
    nc = bacc.Bacc("TRN2", target_bir_lowering=False, num_devices=1)
    io = {}
    for name, a in arrays.items():
        arrays[name] = np.ascontiguousarray(a)
        io[name] = nc.dram_tensor(f"in_{name}", a.shape, mybir.dt.float32, kind="ExternalInput").ap()
    for name, shape in outs.items():
        io[name] = nc.dram_tensor(f"out_{name}", shape, mybir.dt.float32, kind="ExternalOutput").ap()
    build(nc, io)
    r = run_bass_kernel_spmd(nc, [{f"in_{name}": a for name, a in arrays.items()}], core_ids=[0]).results[0]
    return (
        r["out_y_prompt"].reshape(1, SEQ, D), r["out_y_sample"].reshape(NREQ, REQT, D), r["out_pool_prompt"].reshape(DEPTH, 1, PBUF, DB),
        r["out_mem_k"].reshape(DEPTH, 1, NMEM, HEADS, HD), r["out_mem_v"].reshape(DEPTH, 1, NMEM, HEADS, HD), r["out_pool_sample"],
        r["out_v_rows"].reshape(DEPTH, NREQ, REQT, DA),
    )
```
